# Optimizing a Trainium2 kernel written in Bass

```python
import math
import jax, jax.numpy as jnp
from jax import lax
import numpy as np

D_MODEL = 1024
BATCH = 1
SEQ = 256
DEPTH = 2
DEC_BATCH = 8
DEC_SEQ = 1
PAST_LEN = 256
PAGE_SIZE = 128

MIX_WIDTH = D_MODEL
ATT_HEADS = 4
ATT_V_DIM = MIX_WIDTH // 2 // ATT_HEADS
ATT_QK_DIM = ATT_V_DIM // 2
SSM_INNER = MIX_WIDTH // 2
SSM_HEAD_DIM = 64
SSM_HEADS = SSM_INNER // SSM_HEAD_DIM
SSM_GROUPS = 2
SSM_STATE = 128
CONV_WIDTH = 4
CONV_DIM = SSM_INNER + 2 * SSM_GROUPS * SSM_STATE
SSD_CHUNK = 128
Q_COLS = ATT_HEADS * 2 * ATT_QK_DIM
K_COLS = ATT_HEADS * 2 * ATT_QK_DIM
V_COLS = ATT_HEADS * ATT_V_DIM
Z_COLS = SSM_INNER
IN_COLS = Q_COLS + K_COLS + V_COLS + Z_COLS + CONV_DIM + SSM_HEADS
IN_SPLITS = (Q_COLS, Q_COLS + K_COLS, Q_COLS + K_COLS + V_COLS,
             Q_COLS + K_COLS + V_COLS + Z_COLS, Q_COLS + K_COLS + V_COLS + Z_COLS + CONV_DIM)
N_MEM = 256
MEM_HEADS = 4
MEM_HEAD_DIM = D_MODEL // MEM_HEADS
D_FF = 2816
N_EXPERTS = 8
TOP_K = 2
D_FF_EXPERT = 2816
N_DENSE = (DEPTH + 1) // 2
N_MOE = DEPTH // 2
ROPE_THETA = 10000.0
Q_BLOCK = 128
LN_EPS = 1e-5
NORM_EPS = 1e-5
DEEPNORM_ALPHA = (2 * DEPTH) ** 0.25
DEEPNORM_BETA = (8 * DEPTH) ** -0.25

kernel_name = "hymba_diffattn_ssd_deepnorm_moe_step"

def _layer_norm(x, g, b):
    xf = x.astype(jnp.float32)
    mu = jnp.mean(xf, -1, keepdims=True)
    xc = xf - mu
    var = jnp.mean(xc * xc, -1, keepdims=True)
    return (xc * lax.rsqrt(var + LN_EPS)).astype(x.dtype) * g + b

def _rms_norm(x, w):
    xf = x.astype(jnp.float32)
    return (xf * lax.rsqrt(jnp.mean(xf * xf, -1, keepdims=True) + NORM_EPS)).astype(x.dtype) * w

def _rope(x, pos):
    d = x.shape[-1]
    inv = ROPE_THETA ** (-jnp.arange(0, d, 2, dtype=jnp.float32) / d)
    ang = pos.astype(jnp.float32)[:, None] * inv[None, :]
    cos, sin = jnp.cos(ang)[:, None, :], jnp.sin(ang)[:, None, :]
    xf = x.astype(jnp.float32)
    x1, x2 = xf[..., : d // 2], xf[..., d // 2:]
    return jnp.concatenate([x1 * cos - x2 * sin, x2 * cos + x1 * sin], -1).astype(x.dtype)

def _diff_attention(q, k, v, q_pos, k_pos, lam):
    b, sq = q.shape[:2]
    bq = min(Q_BLOCK, sq)
    n_blk = -(-sq // bq)
    pad = n_blk * bq - sq
    q = jnp.pad(q, ((0, 0), (0, pad), (0, 0), (0, 0), (0, 0)))
    q_pos = jnp.pad(q_pos, (0, pad), mode='edge')
    qb = q.reshape(b, n_blk, bq, *q.shape[2:]).swapaxes(0, 1)
    pb = q_pos.reshape(n_blk, bq)
    scale = ATT_QK_DIM ** -0.5

    def block(args):
        qi, pi = args
        s = jnp.einsum('bqhmd,bkhmd->bhmqk', qi, k, preferred_element_type=jnp.float32) * scale
        s = jnp.where((k_pos[None, :] <= pi[:, None])[None, None, None], s, -jnp.inf)
        p = jax.nn.softmax(s, axis=-1)
        a = p[:, :, 0] - lam * p[:, :, 1]
        return jnp.einsum('bhqk,bkhd->bqhd', a.astype(v.dtype), v)

    out = lax.map(block, (qb, pb))
    return out.swapaxes(0, 1).reshape(b, n_blk * bq, *out.shape[3:])[:, :sq]

def _ssd(xh, dt, a_head, bmat, cmat, h0):
    b, L = xh.shape[:2]
    G, R, P, N = SSM_GROUPS, SSM_HEADS // SSM_GROUPS, SSM_HEAD_DIM, SSM_STATE
    q = min(SSD_CHUNK, L)
    nc = -(-L // q)
    pad = nc * q - L
    f32 = jnp.float32
    padl = lambda t: jnp.pad(t, ((0, 0), (0, pad)) + ((0, 0),) * (t.ndim - 2))
    x = padl(xh.astype(f32)).reshape(b, nc, q, G, R, P)
    dtc = padl(dt).reshape(b, nc, q, G, R)
    B = padl(bmat.astype(f32)).reshape(b, nc, q, G, N)
    C = padl(cmat.astype(f32)).reshape(b, nc, q, G, N)
    acs = jnp.cumsum(dtc * a_head.reshape(G, R), axis=2)
    xdt = x * dtc[..., None]
    seg = acs[:, :, :, None] - acs[:, :, None, :]
    causal = jnp.tril(jnp.ones((q, q), bool))[:, :, None, None]
    decay = jnp.exp(jnp.where(causal, seg, -jnp.inf))
    cb = jnp.einsum('bclgn,bcsgn->bclsg', C, B)
    y_diag = jnp.einsum('bclsgr,bcsgrp->bclgrp', cb[..., None] * decay, xdt)
    xw = xdt * jnp.exp(acs[:, :, -1:] - acs)[..., None]
    states = jnp.einsum('bclgn,bclgrp->bcgrpn', B, xw)
    chunk_decay = jnp.exp(acs[:, :, -1])

    def step(h, inp):
        st, dec = inp
        return h * dec[..., None, None] + st, h

    h_last, h_in = lax.scan(step, h0.astype(f32).reshape(b, G, R, P, N),
                            (states.swapaxes(0, 1), chunk_decay.swapaxes(0, 1)))
    h_in = h_in.swapaxes(0, 1)
    y_off = jnp.einsum('bclgn,bcgrpn->bclgrp', C, h_in) * jnp.exp(acs)[..., None]
    y = (y_diag + y_off).reshape(b, nc * q, SSM_HEADS, P)[:, :L]
    return y, h_last.reshape(b, SSM_HEADS, P, N)

def _mixer(x, pos, k_pos, past_k, past_v, conv_prev, h0, layer,
           w_in, conv_w, conv_b, dt_bias, a_log, d_skip, ssm_norm_w,
           lambda_params, attn_norm_w, w_out):
    b, L, _ = x.shape
    q, k, v, z, xbc, dt = jnp.split(x @ w_in, IN_SPLITS, axis=-1)
    q = _rope(q.reshape(b, L, 2 * ATT_HEADS, ATT_QK_DIM), pos)
    k = _rope(k.reshape(b, L, 2 * ATT_HEADS, ATT_QK_DIM), pos)
    v = v.reshape(b, L, ATT_HEADS, ATT_V_DIM)
    k_all = k if past_k is None else jnp.concatenate([past_k.astype(k.dtype), k], axis=1)
    v_all = v if past_v is None else jnp.concatenate([past_v.astype(v.dtype), v], axis=1)
    lam_init = 0.8 - 0.6 * math.exp(-0.3 * layer)
    lp = lambda_params.astype(jnp.float32)
    lam = jnp.exp(jnp.dot(lp[0], lp[1])) - jnp.exp(jnp.dot(lp[2], lp[3])) + lam_init
    att = _diff_attention(q.reshape(b, L, ATT_HEADS, 2, ATT_QK_DIM),
                          k_all.reshape(b, -1, ATT_HEADS, 2, ATT_QK_DIM), v_all, pos, k_pos, lam)
    att = (_rms_norm(att, attn_norm_w) * (1.0 - lam_init)).reshape(b, L, V_COLS)
    xbc_pad = jnp.concatenate([conv_prev.astype(xbc.dtype), xbc], axis=1)
    conv = conv_b + sum(xbc_pad[:, i:i + L] * conv_w[i] for i in range(CONV_WIDTH))
    new_conv = xbc_pad[:, -(CONV_WIDTH - 1):]
    conv = jax.nn.silu(conv)
    xs, bm, cm = jnp.split(conv, (SSM_INNER, SSM_INNER + SSM_GROUPS * SSM_STATE), axis=-1)
    dt = jax.nn.softplus(dt.astype(jnp.float32) + dt_bias.astype(jnp.float32))
    a_head = -jnp.exp(a_log.astype(jnp.float32))
    xh = xs.reshape(b, L, SSM_HEADS, SSM_HEAD_DIM)
    y, h_last = _ssd(xh, dt, a_head, bm.reshape(b, L, SSM_GROUPS, SSM_STATE),
                     cm.reshape(b, L, SSM_GROUPS, SSM_STATE), h0)
    y = y + d_skip.astype(jnp.float32)[:, None] * xh.astype(jnp.float32)
    y = y.astype(x.dtype).reshape(b, L, SSM_INNER) * jax.nn.silu(z)
    y = _rms_norm(y.reshape(b, L, SSM_GROUPS, SSM_INNER // SSM_GROUPS),
                  ssm_norm_w.reshape(SSM_GROUPS, -1)).reshape(b, L, SSM_INNER)
    out = jnp.concatenate([att, y], axis=-1) @ w_out
    return out, k, v, new_conv, h_last

def _mem_kv(mem, w_ckv):
    b = mem.shape[0]
    mk, mv = jnp.split(mem @ w_ckv, 2, axis=-1)
    return (mk.reshape(b, N_MEM, MEM_HEADS, MEM_HEAD_DIM), mv.reshape(b, N_MEM, MEM_HEADS, MEM_HEAD_DIM))

def _cross_attn(x, mem_k, mem_v, w_cq, w_co):
    b, L, _ = x.shape
    q = (x @ w_cq).reshape(b, L, MEM_HEADS, MEM_HEAD_DIM)
    s = jnp.einsum('bqhd,bkhd->bhqk', q, mem_k.astype(q.dtype),
                   preferred_element_type=jnp.float32) * (MEM_HEAD_DIM ** -0.5)
    p = jax.nn.softmax(s, axis=-1)
    o = jnp.einsum('bhqk,bkhd->bqhd', p.astype(x.dtype), mem_v.astype(x.dtype))
    return o.reshape(b, L, D_MODEL) @ w_co

def _swiglu(x, w_gu, w_down):
    g, u = jnp.split(x @ w_gu, 2, axis=-1)
    return (jax.nn.silu(g) * u) @ w_down

def _moe(x, w_router, w_exp_gu, w_exp_down):
    logits = (x @ w_router).astype(jnp.float32)
    top_v, top_i = lax.top_k(logits, TOP_K)
    gates = jax.nn.softmax(top_v, axis=-1)
    gate = jnp.sum(jax.nn.one_hot(top_i, N_EXPERTS, dtype=jnp.float32) * gates[..., None], axis=-2)
    out = jnp.zeros_like(x)
    for e in range(N_EXPERTS):
        out = out + _swiglu(x, w_exp_gu[e], w_exp_down[e]) * gate[..., e:e + 1].astype(x.dtype)
    return out

def _channel(x, layer, w_ffn_gu, w_ffn_down, w_router, w_exp_gu, w_exp_down):
    if layer % 2 == 0:
        return _swiglu(x, w_ffn_gu[layer // 2], w_ffn_down[layer // 2])
    return _moe(x, w_router[layer // 2], w_exp_gu[layer // 2], w_exp_down[layer // 2])

def setup_inputs(seed: int = 0) -> dict:
    key = jax.random.key(seed)
    ks = iter(jax.random.split(key, 48))
    f32 = jnp.float32
    n_pages = PAST_LEN // PAGE_SIZE
    n_used = DEC_BATCH * n_pages
    n_phys = n_used + n_used // 4

    def nrm(shape, scale=1.0):
        return jax.random.normal(next(ks), shape, f32) * scale

    def gain(shape):
        return 1.0 + nrm(shape, 0.02)

    page_table = jax.random.permutation(next(ks), n_phys)[:n_used].reshape(DEC_BATCH, n_pages).astype(jnp.int32)
    dt0 = jnp.exp(jax.random.uniform(next(ks), (DEPTH, SSM_HEADS), f32, math.log(1e-3), math.log(1e-1)))
    dt_bias = dt0 + jnp.log(-jnp.expm1(-dt0))
    a_log = jnp.log(jax.random.uniform(next(ks), (DEPTH, SSM_HEADS), f32, 1.0, 16.0))
    beta = DEEPNORM_BETA
    return {
        "x_prompt": nrm((BATCH, SEQ, D_MODEL)),
        "x_sample": nrm((DEC_BATCH, DEC_SEQ, D_MODEL)),
        "cache_attn_k": nrm((DEPTH, n_phys, PAGE_SIZE, 2 * ATT_HEADS, ATT_QK_DIM)),
        "cache_attn_v": nrm((DEPTH, n_phys, PAGE_SIZE, ATT_HEADS, ATT_V_DIM)),
        "cache_mem_k": nrm((DEPTH, DEC_BATCH, N_MEM, MEM_HEADS, MEM_HEAD_DIM)),
        "cache_mem_v": nrm((DEPTH, DEC_BATCH, N_MEM, MEM_HEADS, MEM_HEAD_DIM)),
        "state_conv": nrm((DEPTH, DEC_BATCH, CONV_WIDTH - 1, CONV_DIM)),
        "state_ssm": nrm((DEPTH, DEC_BATCH, SSM_HEADS, SSM_HEAD_DIM, SSM_STATE), 0.5),
        "page_table": page_table,
        "mem_prompt": nrm((BATCH, N_MEM, D_MODEL)),
        "ln_g": gain((DEPTH, 3, D_MODEL)),
        "ln_b": nrm((DEPTH, 3, D_MODEL), 0.02),
        "w_in": nrm((DEPTH, D_MODEL, IN_COLS), D_MODEL ** -0.5),
        "conv_w": nrm((DEPTH, CONV_WIDTH, CONV_DIM), CONV_WIDTH ** -0.5),
        "conv_b": nrm((DEPTH, CONV_DIM), 0.02),
        "dt_bias": dt_bias,
        "a_log": a_log,
        "d_skip": gain((DEPTH, SSM_HEADS)),
        "ssm_norm_w": gain((DEPTH, SSM_INNER)),
        "lambda_params": nrm((DEPTH, 4, ATT_QK_DIM), 0.1),
        "attn_norm_w": gain((DEPTH, ATT_V_DIM)),
        "w_out": nrm((DEPTH, MIX_WIDTH, D_MODEL), beta * MIX_WIDTH ** -0.5),
        "w_cq": nrm((DEPTH, D_MODEL, D_MODEL), D_MODEL ** -0.5),
        "w_ckv": nrm((DEPTH, D_MODEL, 2 * D_MODEL), D_MODEL ** -0.5),
        "w_co": nrm((DEPTH, D_MODEL, D_MODEL), beta * D_MODEL ** -0.5),
        "w_ffn_gu": nrm((N_DENSE, D_MODEL, 2 * D_FF), D_MODEL ** -0.5),
        "w_ffn_down": nrm((N_DENSE, D_FF, D_MODEL), beta * D_FF ** -0.5),
        "w_router": nrm((N_MOE, D_MODEL, N_EXPERTS), D_MODEL ** -0.5),
        "w_exp_gu": nrm((N_MOE, N_EXPERTS, D_MODEL, 2 * D_FF_EXPERT), D_MODEL ** -0.5),
        "w_exp_down": nrm((N_MOE, N_EXPERTS, D_FF_EXPERT, D_MODEL), beta * D_FF_EXPERT ** -0.5),
    }

def reference(x_prompt, x_sample, cache_attn_k, cache_attn_v, cache_mem_k, cache_mem_v,
              state_conv, state_ssm, page_table, mem_prompt, ln_g, ln_b, w_in, conv_w, conv_b,
              dt_bias, a_log, d_skip, ssm_norm_w, lambda_params, attn_norm_w, w_out,
              w_cq, w_ckv, w_co, w_ffn_gu, w_ffn_down, w_router, w_exp_gu, w_exp_down):
    bp, seq = x_prompt.shape[:2]
    bs, dec_seq = x_sample.shape[:2]
    past_len = page_table.shape[1] * cache_attn_k.shape[2]
    pos_p = jnp.arange(seq, dtype=jnp.int32)
    pos_s = past_len + jnp.arange(dec_seq, dtype=jnp.int32)
    kpos_s = jnp.arange(past_len + dec_seq, dtype=jnp.int32)
    hp, hs = x_prompt, x_sample
    kp_l, vp_l, mkp_l, mvp_l, cp_l, sp_l = [], [], [], [], [], []
    ks_l, vs_l, cs_l, ss_l = [], [], [], []
    for l in range(DEPTH):
        mix_w = (w_in[l], conv_w[l], conv_b[l], dt_bias[l], a_log[l], d_skip[l], ssm_norm_w[l],
                 lambda_params[l], attn_norm_w[l], w_out[l])
        conv0 = jnp.zeros((bp, CONV_WIDTH - 1, CONV_DIM), hp.dtype)
        h0 = jnp.zeros((bp, SSM_HEADS, SSM_HEAD_DIM, SSM_STATE), jnp.float32)
        m, k_new, v_new, c_new, s_new = _mixer(hp, pos_p, pos_p, None, None, conv0, h0, l, *mix_w)
        hp = _layer_norm(DEEPNORM_ALPHA * hp + m, ln_g[l, 0], ln_b[l, 0])
        mk, mv = _mem_kv(mem_prompt, w_ckv[l])
        hp = _layer_norm(DEEPNORM_ALPHA * hp + _cross_attn(hp, mk, mv, w_cq[l], w_co[l]), ln_g[l, 1], ln_b[l, 1])
        hp = _layer_norm(DEEPNORM_ALPHA * hp + _channel(hp, l, w_ffn_gu, w_ffn_down, w_router, w_exp_gu, w_exp_down),
                         ln_g[l, 2], ln_b[l, 2])
        kp_l.append(k_new); vp_l.append(v_new); mkp_l.append(mk); mvp_l.append(mv)
        cp_l.append(c_new); sp_l.append(s_new.astype(x_prompt.dtype))
        past_k = cache_attn_k[l, page_table].reshape(bs, past_len, 2 * ATT_HEADS, ATT_QK_DIM)
        past_v = cache_attn_v[l, page_table].reshape(bs, past_len, ATT_HEADS, ATT_V_DIM)
        m, k_new, v_new, c_new, s_new = _mixer(hs, pos_s, kpos_s, past_k, past_v,
                                               state_conv[l], state_ssm[l], l, *mix_w)
        hs = _layer_norm(DEEPNORM_ALPHA * hs + m, ln_g[l, 0], ln_b[l, 0])
        hs = _layer_norm(DEEPNORM_ALPHA * hs + _cross_attn(hs, cache_mem_k[l], cache_mem_v[l], w_cq[l], w_co[l]),
                         ln_g[l, 1], ln_b[l, 1])
        hs = _layer_norm(DEEPNORM_ALPHA * hs + _channel(hs, l, w_ffn_gu, w_ffn_down, w_router, w_exp_gu, w_exp_down),
                         ln_g[l, 2], ln_b[l, 2])
        ks_l.append(k_new); vs_l.append(v_new); cs_l.append(c_new); ss_l.append(s_new.astype(state_ssm.dtype))
    return (hp, hs,
            jnp.stack(kp_l), jnp.stack(vp_l), jnp.stack(mkp_l), jnp.stack(mvp_l),
            jnp.stack(cp_l), jnp.stack(sp_l),
            jnp.stack(ks_l), jnp.stack(vs_l), jnp.stack(cs_l), jnp.stack(ss_l))


_drawn_inputs = setup_inputs


def setup_inputs(seed=0):
    import zlib

    import numpy as np

    out = dict(_drawn_inputs(seed))
    spreads = {}
    factors = {'d_skip': 17.059, 'ssm_norm_w': 19.114, 'lambda_params': 3.098, 'attn_norm_w': 13.372}
    for name, (base, spread) in spreads.items():
        noise = np.random.default_rng([zlib.crc32(name.encode()), seed]).standard_normal(out[name].shape)
        drawn = base * np.exp(spread * noise) if base else spread * noise
        out[name] = __import__('jax').numpy.asarray(drawn.astype(out[name].dtype))
    for name, factor in factors.items():
        out[name] = (out[name] * factor).astype(out[name].dtype)
    return out
```

```python
import math
from contextlib import ExitStack

import numpy as np
import concourse.bass as bass
from concourse import mybir

F32 = mybir.dt.float32
I32 = mybir.dt.int32
ALU = mybir.AluOpType
ACT = mybir.ActivationFunctionType
AX = mybir.AxisListType

P = 128
D = 1024
KT = D // P
L = 2
NP_TOK = 256
NS_TOK = 8
T = NP_TOK + NS_TOK
DECODE_FIRST = (2, 0, 1)
NORM_ORDER = (0, 2, 1)
TILES = [(0, P), (P, P), (2 * P, NS_TOK)]
AH, DQ, DV = 4, 64, 128
SH, SP_, SN, SG = 8, 64, 128, 2
CW = 4
MH, MD = 4, 256
PAGES = 2
N_PHYS = 20
FF = 2816
FT = FF // P
GU = 256
NGU = FF // GU
NDN = 6
EXPERTS = 8
SLOTS = 128
ALPHA = (2 * L) ** 0.25
EPS = 1e-5
NEG = -1e30
RING = 6
SLOT = 4096
EPOS = NGU + NDN + 1
assert EPOS % RING == 0
LAM_INIT = [0.8 - 0.6 * math.exp(-0.3 * l) for l in range(L)]

C_ID, C_U, C_US, C_NEG, C_CM, C_IOTA = (P * i for i in range(6))
C_COS = 6 * P
C_SIN = C_COS + 3 * 32
C_REQ = C_SIN + 3 * 32
C_HEAD = C_REQ + 8
C_REQT = C_HEAD + 8
C_TRI = C_REQT + 64
NCONST = C_TRI + 64


def constants():
    c = np.zeros((P, NCONST), np.float32)
    i = np.arange(P)
    c[:, C_ID:C_ID + P] = np.eye(P)
    c[:, C_U:C_U + P] = i[:, None] <= i[None, :]
    c[:, C_US:C_US + P] = i[:, None] < i[None, :]
    c[:, C_NEG:C_NEG + P] = np.where(i[None, :] >= i[:, None], 0, NEG)
    c[:, C_CM:C_CM + P] = np.where(i[None, :] <= i[:, None], 0, NEG)
    c[:, C_IOTA:C_IOTA + P] = i[None, :]
    inv = np.float32(10000.0) ** (-np.arange(0, DQ, 2, dtype=np.float32) / np.float32(DQ))
    for t in range(3):
        pos = (t * P + i if t < 2 else np.full(P, NP_TOK)).astype(np.float32)
        ang = (pos[:, None] * inv[None, :]).astype(np.float32)
        c[:, C_COS + 32 * t:C_COS + 32 * t + 32] = np.cos(ang)
        c[:, C_SIN + 32 * t:C_SIN + 32 * t + 32] = np.sin(ang)
    r = np.arange(64)
    c[:64, C_REQ:C_REQ + 8] = (r[:, None] // 8) == np.arange(8)[None, :]
    c[:64, C_HEAD:C_HEAD + 8] = (r[:, None] % 8) == np.arange(8)[None, :]
    c[:8, C_REQT:C_REQT + 64] = c[:64, C_REQ:C_REQ + 8].T
    e = np.arange(8)
    c[:, C_TRI:C_TRI + 64] = (e[None, :] < e[:, None]).astype(np.float32).reshape(1, 64)
    return c


class Signal:

    def __init__(self, sem, per_layer):
        self.sem, self.per = sem, per_layer

    def value(self, l, i=0):
        assert i < self.per
        return l * self.per + i + 1

    def wait(self, eng, l, i=0):
        eng.wait_ge(self.sem, self.value(l, i))


class Steps:

    def __init__(self, eng, sem):
        self.eng, self.sem, self.n = eng, sem, 0

    def inc(self, ins):
        ins.then_inc(self.sem, 1)
        self.n += 1

    def done(self, ins):
        self.inc(ins)
        self.eng.wait_ge(self.sem, self.n)


class PsumTurns:

    def __init__(self, groups, banks, full, emptied):
        self.groups, self.banks, self.full, self.emptied = groups, banks, full, emptied
        self.index = {g: n for n, (g, _) in enumerate(groups)}
        seen = {k: 0 for k in emptied}
        self.rank = []
        for _, by in groups:
            seen[by] += 1
            self.rank.append(seen[by])
        self.opened = 0
        self.closed = {k: 0 for k in emptied}

    def open(self, pe, name):
        n = self.index[name]
        assert n == self.opened, (name, self.groups[self.opened])
        self.opened += 1
        if n >= len(self.banks):
            by = self.groups[n - len(self.banks)][1]
            pe.wait_ge(self.emptied[by], self.rank[n - len(self.banks)])
        return self.banks[n % len(self.banks)]

    def take(self, eng, name):
        n = self.index[name]
        eng.wait_ge(self.full, n + 1)
        return self.banks[n % len(self.banks)]

    def passed(self, eng, name):
        eng.wait_ge(self.full, self.index[name] + 1)

    def copied(self, eng, name):
        n = self.index[name]
        eng.wait_ge(self.emptied[self.groups[n][1]], self.rank[n])

    def emptied_after(self, name, ins):
        n = self.index[name]
        by = self.groups[n][1]
        self.closed[by] += 1
        assert self.closed[by] == self.rank[n], name
        ins.then_inc(self.emptied[by], 1)


def psum_groups():
    g = [(("vec",), "V")]
    g += [(("xin", n), "V") for n in range(5)] + [(("mem", n), "A") for n in range(4)]
    for l in range(L):
        def add(by, *name):
            g.append(((l,) + name, by))

        add("V", "dt")
        for c in ("q", "k"):
            for t in DECODE_FIRST:
                add("A", "tok", c, t)
        add("V", "acs")
        add("V", "scT")
        for m in range(8):
            add("V", "xbc", m)
            add("V", "qb", m)
            if m == 0:
                add("V", "dtb")
        for t in range(3):
            add("A", "tok", "v", t)
            if t == 0:
                add("V", "sST")
        for t in range(3):
            add("A", "xt", t)
            add("A", "Bt", t)
        add("A", "cp", 0)
        add("A", "cp", 1)
        for i in range(4):
            add("V", "BC", 2 * i)
            add("V", "BC", 2 * i + 1)
            if i < 3:
                add("A", "tok", "z", i)
            if i == 0:
                add("V", "pT")
                add("V", "pself")
        add("A", "mkv", 0)
        add("V", "st", 0)
        add("V", "st", 1)
        for c in range(2):
            add("V", "ab", c, 0)
            add("V", "ab", c, 1)
            add("V", "cb", c)
            add("A", "mkv", 1 + c)
            add("V", "y", c)
        add("V", "yo")
        add("A", "stT")
        add("V", "ysT")
        for i in range(4):
            add("A", "qkT", i)
        for qt in range(2):
            for hp in range(2):
                for m in range(2):
                    add("V", "S", qt, hp, m)
            add("A", "mkv", 3 + qt)
        add("A", "aT", 0, 0)
        add("V", "O", 0)
        add("A", "mkv", 5)
        add("V", "oS")
        add("A", "mkv", 6)
        add("V", "oSt")
        add("A", "aT", 1, 0)
        add("A", "aT", 1, 1)
        add("V", "O", 1)
        add("A", "mkv", 7)
        for n in range(5):
            add("V", "mixT", n)
        for m in range(8):
            add("V", "m", m)
        for i in range(4):
            add("A", "mkT", i)
        add("V", "mu", 0)
        add("V", "var", 0)
        for m in range(8):
            add("A", "cq", m)
        for t in range(2):
            for hp in range(2):
                add("A", "cS", t, hp)
        add("V", "qsT", 0)
        add("V", "qsT", 1)
        for t in range(2):
            for kt in range(2):
                add("A", "cPT", t, kt)
        for i in range(4):
            add("A", "cO", i)
        for b in range(8):
            add("V", "qsb", b, 0)
            add("V", "qsb", b, 1)
        for n in ("sCT", "sPT", "soT"):
            add("V", n)
        for m in range(8):
            add("V", "co", m)
        add("V", "mu", 1)
        add("V", "var", 1)
        if l == 0:
            for f in range(NGU):
                for s in range(2):
                    add("A", "g", f, s)
                    add("V", "u", f, s)
            for m in range(8):
                add("V", "d", m)
        else:
            for n in range(6):
                add("A", "xtok", n)
            add("V", "lg")
            add("V", "pos")
        add("V", "mu", 2)
        add("V", "var", 2)
    for n in range(6):
        g.append((("out", n), "A"))
    return g


def ring_chunks():
    c = [(("x",), 2, "pe", ("xin", 4)), (("mem",), 1, "pe", ("mem", 3))]
    for l in range(L):
        c += [((l, n), 1, "pe", (l, "tok", n, DECODE_FIRST[-1])) for n in ("q", "k")]
        c += [((l, "xbc0"), 1, "pe", (l, "xbc", 3)), ((l, "xbc1"), 1, "pe", (l, "xbc", 7))]
        c += [((l, "K", i), 8, "v", (l, "qb", 4 * i + 3)) for i in range(2)]
        c += [((l, n), 1, "pe", (l, "tok", n, 2)) for n in ("v", "z")]
        c += [((l, "state"), 1, "st", l)]
        c += [((l, "ckv", i), 1, "pe", (l, "mkv", 2 * i + 1)) for i in range(3)]
        c += [((l, "V", i), 8, "pe", (l, "oS")) for i in range(2)]
        c += [((l, "ckv", 3), 1, "pe", (l, "mkv", 7))]
        c += [((l, "out", i), 1, "pe", (l, "m", 4 * i + 3)) for i in range(2)]
        c += [((l, "cq", i), 1, "pe", (l, "cq", 4 * i + 3)) for i in range(2)]
        c += [((l, "mkv"), 2, "pe", (l, "cO", 3))]
        c += [((l, "mK", i), 2, "v", (l, "qsb", 2 * i + 1, 1)) for i in range(4)]
        c += [((l, "mV", i), 2, "pe", (l, "soT")) for i in range(4)]
        c += [((l, "co", i), 1, "pe", (l, "co", 4 * i + 3)) for i in range(2)]
        if l == 0:
            c += [((l, "gu", f), 2, "pe", (l, "u", f, 1)) for f in range(NGU)]
            c += [((l, "dn", i), 1, "pe", (l, "d", 4 * (i // 3) + 3)) for i in range(NDN)]
    return c


class Ring:
    def __init__(self, chunks, landed, turns, state_stored):
        self.chunks, self.landed, self.turns, self.state_stored = chunks, landed, turns, state_stored
        self.pos = {c[0]: n for n, c in enumerate(chunks)}
        per = [0] * RING
        self.value = []
        for n, (_, dmas, _, _) in enumerate(chunks):
            per[n % RING] += 16 * dmas
            self.value.append(per[n % RING])
        self.slot_total = per
        self.next = 0

    def freed(self, sp, n):
        if n < RING:
            return
        _, _, by, what = self.chunks[n - RING]
        if by == "pe":
            self.turns.passed(sp, what)
        elif by == "v":
            self.turns.copied(sp, what)
        else:
            sp.wait_ge(self.state_stored, 16 * (what + 1))

    def claim(self, sp, key):
        n = self.pos[key]
        assert n == self.next, key
        self.next += 1
        self.freed(sp, n)
        return n % RING

    def arrived(self, eng, key):
        n = self.pos[key]
        eng.wait_ge(self.landed[n % RING], self.value[n])
        return n % RING


def expert_positions(start):
    per, out = [0] * RING, []
    for p in range(EPOS - 1):
        s = (start + p) % RING
        kind, i = ("gu", p) if p < NGU else ("dn", p - NGU)
        per[s] += 16 * (2 if kind == "gu" else 1)
        out.append((kind, i, s, per[s]))
    return out, per


ARENA = 16256
STORES_LAYER = 10
NSTORES = STORES_LAYER * L + 2


def build(nc, a, outs, lots=SLOTS, always=False):
    (y_p, y_s, o_kp, o_vp, o_mk, o_mv, o_cp, o_sp, o_ks, o_vs, o_cs, o_ss) = outs
    passes = -(-T // lots)
    with ExitStack() as ctx:
        def sb(name, shape, dt=F32):
            return ctx.enter_context(nc.sbuf_tensor(name, shape, dt))

        def sem(name):
            return ctx.enter_context(nc.semaphore(name))

        ring = sb("ring", [P, RING, SLOT])
        xT = sb("xT", [P, KT, T])
        R = sb("R", [P, KT, T])
        SQ = sb("SQ", [P, KT, T])
        memT = sb("memT", [P, KT, NP_TOK])
        const = sb("const", [P, NCONST])
        one_col = sb("one_col", [P, 1])
        mean_col = sb("mean_col", [P, 1])
        ones, mean_of = one_col[:].to_broadcast([P, P]), mean_col[:].to_broadcast([P, P])
        vecT = sb("vecT", [P, 2, P])
        dtb = sb("dtb", [P, L, 32])
        An = sb("An", [P, L, 32])
        raw8 = sb("raw8", [P, 3, L, SH])
        col8 = sb("col8", [SH, 2, L])
        nlam = sb("nlam", [P, L])
        lamt = sb("lamt", [P, L, 2])
        wdt = sb("wdt", [P, L, KT, SH])
        wr = sb("wr", [P, KT, EXPERTS])
        ptab = sb("ptab", [1, NS_TOK * PAGES], I32)
        NST = 848
        st = sb("st", [P, NST])
        pself_r = sb("pself_r", [64, 8])
        stat = sb("stat", [P, 2, T])
        gates = sb("gates", [P, 3, 9])
        posp = sb("posp", [P, 3, 9])
        sel = sb("sel", [P, 3, 8])
        lgb = sb("lgb", [P, 3, 8])
        lsm = sb("lsm", [P, 3, 8])
        l3 = sb("l3", [P, 3])
        cnt = sb("cnt", [1, 1])
        cnti = sb("cnti", [1, 1], I32)
        mem_rows = sb("mem_rows", [P, 512])
        arena = sb("arena", [P, ARENA])
        banks = [ctx.enter_context(nc.psum_tensor(f"bank{i}", [P, 512], F32)) for i in range(8)]

        used = [0]

        def carve(n, at=None):
            if at is not None:
                used[0] = at
            o = used[0]
            used[0] += n
            assert used[0] <= ARENA, used[0]
            return arena[:, o:o + n]

        vraw = carve(2 * P, 0).rearrange("p (a n) -> p a n", a=2)
        lraw = carve(L * 4 * DQ).rearrange("p (l a d) -> p l a d", l=L, a=4)
        lprod = carve(L * 2 * DQ).rearrange("p (l a d) -> p l a d", l=L, a=2)
        qk_raw = carve(3 * 1024, 0).rearrange("p (t n) -> p t n", t=3)
        mix = qk_raw
        vz = carve(3 * 1024).rearrange("p (t n) -> p t n", t=3)
        qkr = carve(3 * 1024).rearrange("p (t n) -> p t n", t=3)
        conv_at = used[0]
        xpad = carve(8 * 259).rearrange("p (m n) -> p m n", m=8)
        win = carve(8 * 32).rearrange("p (m i b) -> p m i b", m=8, i=CW)
        ct11 = carve(88).rearrange("p (m n) -> p m n", m=8)
        tmp = carve(1024)
        wtmp = tmp[:, 512:768]
        share = used[0]
        rope_t = carve(512, share)
        Mdec = carve(2 * 512, conv_at).rearrange("p (g r n) -> p g r n", g=2, r=4)
        xdt = carve(2 * 512).rearrange("p (c n) -> p c n", c=2)
        probs = carve(2048, conv_at).rearrange("p (h m k) -> p h m k", h=AH, m=2)
        xtok = carve(3 * 512, share).rearrange("p (t n) -> p t n", t=3)
        Btok = carve(512).rearrange("p (c n) -> p c n", c=2)
        xw = carve(2 * 512).rearrange("p (c n) -> p c n", c=2)
        STf = xw[:, 0, :]
        ST0 = carve(512)
        kqT = carve(8 * 256, share).rearrange("p (m n) -> p m n", m=8)
        aT = carve(3 * 512).rearrange("p (k h n) -> p k h n", k=3, h=AH)
        convT = R
        mixT = SQ
        sqf = SQ[:, :, :].rearrange("p k t -> p (k t)")
        sc_in = sqf[0:24, 0:1024]
        conv_rows = sqf[0:11, 0:1024]
        ssm_rows = sqf[:, 1024:1536].rearrange("p (j n) -> p j n", j=4)
        BCs = sqf[0:8, 1536:2048]
        pSx = sqf[0:64, 1024:1281]
        sbt = sqf[0:64, 2048:2112]
        mkT = carve(8 * 256, 0).rearrange("p (m n) -> p m n", m=8)
        qcT = carve(8 * T).rearrange("p (m n) -> p m n", m=8)
        cP = carve(2 * 1024).rearrange("p (t h k) -> p t h k", t=2, h=MH)
        cPT = carve(2 * 1024).rearrange("p (k h q) -> p k h q", k=2, h=MH)
        qs = carve(1024)
        ctmp = carve(1024)
        sP = carve(256)
        oT = SQ
        hT = carve(FT * T, 0).rearrange("p (f n) -> p f n", f=FT)
        sgd = carve(2 * T).rearrange("p (s n) -> p s n", s=2)
        x_tok = carve(3 * 1024, 0).rearrange("p (t n) -> p t n", t=3)
        Sel = carve(3 * P).rearrange("p (t n) -> p t n", t=3)
        GSel = carve(3 * P).rearrange("p (t n) -> p t n", t=3)
        xgT = carve(KT * P).rearrange("p (k n) -> p k n", k=KT)
        sg = carve(2 * GU).rearrange("p (s n) -> p s n", s=2)
        hh = carve(2 * GU).rearrange("p (s n) -> p s n", s=2)
        heT = carve(FT * P).rearrange("p (f n) -> p f n", f=FT)
        ye = carve(1024)
        GSelT = carve(T)
        acc = carve(KT * T).rearrange("p (k n) -> p k n", k=KT)
        cmp_gt = carve(192).rearrange("p (t e j) -> p t e j", t=3, e=8)
        cmp_eq = carve(192).rearrange("p (t e j) -> p t e j", t=3, e=8)
        y_tok = carve(3 * 1024, 0).rearrange("p (t n) -> p t n", t=3)

        so = [0]

        def small(n):
            o = so[0]
            so[0] += n
            assert so[0] <= NST
            return st[:, o:o + n]

        dtr, dte, dtv, da = small(32), small(32), small(32), small(32)
        sc = small(56)
        ex = small(56)
        xwsc = small(16)
        dcol = small(64).rearrange("p (j c) -> p j c", j=4)
        dtx = small(32).rearrange("p (j b) -> p j b", j=4)
        ysT = small(32).rearrange("p (j b) -> p j b", j=4)
        mx, nb, rs, rr = small(8), small(8), small(8), small(8)
        sS = small(128).rearrange("p (g b h) -> p g b h", g=2, b=8)
        ms, rstd6 = small(6), small(6)
        ss, as4 = small(8), small(4)
        mx1, nb1, rs1, rr1 = small(1), small(1), small(1), small(1)
        aTs = small(64).rearrange("p (g b h) -> p g b h", g=2, b=8)
        attS = small(32)
        sC = small(64).rearrange("p (t b h) -> p t b h", t=2, b=8)
        sPTs = small(64).rearrange("p (t c) -> p t c", t=2)

        ident = const[:, C_ID:C_ID + P]
        upper = const[:, C_U:C_U + P]
        before = const[:, C_US:C_US + P]
        negm = const[:, C_NEG:C_NEG + P]
        cmask = const[:, C_CM:C_CM + P]
        iota = const[:, C_IOTA:C_IOTA + P]

        def col_g(l, i, k):
            o = (l * 3 + i) * 8 + k
            return vecT[:, 0, o:o + 1]

        def col_b(l, i, k):
            o = 48 + (l * 3 + i) * 8 + k
            return vecT[:, 0, o:o + 1]

        def cols_ssm(l):
            return vecT[:, 0, 96 + 4 * l:100 + 4 * l]

        def col_attn(l):
            return vecT[:, 0, 104 + l:105 + l]

        def cols_cb(l, m, n=1):
            return vecT[:, 0, 106 + 8 * l + m:106 + 8 * l + m + n]

        def col_cw(l, i, m):
            o = l * 32 + i * 8 + m
            return vecT[:, 1, o:o + 1]

        landed = [sem(f"landed{s}") for s in range(RING)]
        psum_full, emptied_by_act, emptied_by_dve = sem("psum_full"), sem("emptied_by_act"), sem("emptied_by_dve")
        const_landed, vecs_landed, small_landed, ptab_landed = (
            sem("const_landed"), sem("vecs_landed"), sem("small_landed"), sem("ptab_landed"))
        conv_state_landed, stored, state_stored = sem("conv_state_landed"), sem("stored"), sem("state_stored")
        mem_stored = sem("mem_stored")
        dve_steps, act_steps, pool_steps = sem("dve_steps"), sem("act_steps"), sem("pool_steps")
        buffers_set = sem("buffers_set")
        lam_dots, setup_exps, vectors_ready = sem("lam_dots"), sem("setup_exps"), sem("vectors_ready")

        def signal(name, per=1):
            return Signal(sem(name), per)

        dt_abs, dt_exp, dt_exp1, dt_ln, da_ready = (
            signal(n) for n in ("dt_abs", "dt_exp", "dt_exp1", "dt_ln", "da_ready"))
        tap0_done, taps_done, conv_ready = signal("tap0_done", 8), signal("taps_done", 9), signal("conv_ready", 9)
        rope_ready = signal("rope_ready", 3)
        decays_in, decays_out, xwsc_ready = signal("decays_in"), signal("decays_out"), signal("xwsc_ready")
        xdt_ready, xskip_ready = signal("xdt_ready", 2), signal("xskip_ready", 3)
        seg_ready, decay_ready = signal("seg_ready", 4), signal("decay_ready", 4)
        state_decayed, ysT_ready = signal("state_decayed", 8), signal("ysT_ready")
        max_ready, probs_ready, a_ready = signal("max_ready", 8), signal("probs_ready", 8), signal("a_ready", 2)
        dec_scores, dec_rows, dec_exp, dec_probs = (
            signal(n) for n in ("dec_scores", "dec_rows", "dec_exp", "dec_probs"))
        ms_ready, rstd_ready, mix_ready = signal("ms_ready", 3), signal("rstd_ready", 3), signal("mix_ready", 3)
        centred, squared, ln_rstd, scaled = (
            signal("centred", 3), signal("squared", 6), signal("ln_rstd", 3), signal("scaled", 6))
        xT_act, xT_dve = signal("xT_act", 3), signal("xT_dve", 3)
        cmax_ready, cP_ready = signal("cmax_ready", 4), signal("cP_ready", 2)
        cs_scores, cs_rows, cs_exp, cs_probs = (
            signal(n) for n in ("cs_scores", "cs_rows", "cs_exp", "cs_probs"))
        lsm_ready, lexp_ready, sel_known, pos_known = (
            sem("lsm_ready"), sem("lexp_ready"), sem("sel_known"), sem("pos_known"))
        sel_ready, gu_full, sg_ready, h_ready, T_full, T_done = (
            sem("sel_ready"), sem("gu_full"), sem("sg_ready"), sem("h_ready"), sem("T_full"), sem("T_done"))
        X_full, xg_taken, part_added, dn_done, y_by_act, y_by_dve = (
            sem("X_full"), sem("xg_taken"), sem("part_added"), sem("dn_done"), sem("y_by_act"), sem("y_by_dve"))
        moe_done, pass_shift = sem("moe_done"), sem("pass_shift")

        turns = PsumTurns(psum_groups(), banks, psum_full, {"A": emptied_by_act, "V": emptied_by_dve})
        rg = Ring(ring_chunks(), landed, turns, state_stored)
        e_start = len(rg.chunks)
        epos, eper = expert_positions(e_start % RING)
        take, passed, copied, emptied_after = turns.take, turns.passed, turns.copied, turns.emptied_after

        def expert_no(e, c):
            return e + EXPERTS * c

        def transposes_before(e, c):
            return expert_no(e, c) * (NGU + 1) + (c + 1)

        def parts_added(e, c):
            return expert_no(e, c) * KT + KT

        def x_groups_before(e, c):
            return expert_no(e, c) * (2 + KT) + 2 * (c + 1)

        block = ctx.enter_context(nc.Block())

        @block.sync
        def _(sp):
            sp.dma_start(const[:], a["consts"]).then_inc(const_landed, 16)
            for j, (src, r0) in enumerate((
                    (a["ln_g"].rearrange("l i (k n) -> (l i k) n", n=P), 0),
                    (a["ln_b"].rearrange("l i (k n) -> (l i k) n", n=P), 48),
                    (a["ssm_norm_w"].rearrange("l (k n) -> (l k) n", n=P), 96),
                    (a["attn_norm_w"], 104),
                    (a["conv_b"].rearrange("l (k n) -> (l k) n", n=P), 106))):
                sp.dma_start(vraw[r0:r0 + src.shape[0], 0, :], src).then_inc(vecs_landed, 16)
            sp.dma_start(vraw[0:64, 1, :], a["conv_w"].rearrange("l i (k n) -> (l i k) n", n=P)
                         ).then_inc(vecs_landed, 16)
            s = rg.claim(sp, ("x",))
            sp.dma_start(ring[:, s, 0:2048].rearrange("p (t n) -> p t n", t=2),
                         a["x_prompt"].rearrange("o (t p) n -> p (o t) n", p=P)).then_inc(landed[s], 16)
            sp.dma_start(ring[0:NS_TOK, s, 2048:3072], a["x_sample"].rearrange("b o n -> (b o) n")
                         ).then_inc(landed[s], 16)
            s = rg.claim(sp, ("mem",))
            sp.dma_start(ring[:, s, 0:2048].rearrange("p (t n) -> p t n", t=2),
                         a["mem_prompt"].rearrange("o (t p) n -> p (o t) n", p=P)).then_inc(landed[s], 16)
            sp.dma_start(ptab[:], a["page_table"].rearrange("b g -> (b g)").unsqueeze(0)).then_inc(ptab_landed, 16)
            for i, n in enumerate(("dt_bias", "a_log", "d_skip")):
                sp.dma_start(raw8[:, i], a[n].partition_broadcast(P)).then_inc(small_landed, 16)
            with nc.allow_non_contiguous_dma(reason="sixteen words"):
                for i, n in enumerate(("dt_bias", "a_log")):
                    sp.dma_start(col8[:, i, :], a[n].rearrange("l h -> h l")).then_inc(small_landed, 16)
            sp.dma_start(lraw, a["lambda_params"].partition_broadcast(P)).then_inc(small_landed, 16)
            for l in range(L):
                sp.dma_start(wdt[:, l], a["w_in"][l, :, 3072:3080].rearrange("(k p) n -> p k n", p=P)
                             ).then_inc(small_landed, 16)
            sp.dma_start(wr[:], a["w_router"][0].rearrange("(k p) n -> p k n", p=P)).then_inc(small_landed, 16)
            sp.wait_ge(ptab_landed, 16)

            def columns(key, w, c0):
                s = rg.claim(sp, key)
                sp.dma_start(ring[:, s, :].rearrange("p (k n) -> p k n", k=KT),
                             w[:, c0:c0 + 512].rearrange("(k p) n -> p k n", p=P)).then_inc(landed[s], 16)

            def pages(key, cache, b0):
                s = rg.claim(sp, key)
                for i in range(8):
                    n = b0 * PAGES + i
                    page = sp.value_load(ptab[0:1, n:n + 1], min_val=0, max_val=N_PHYS - 1)
                    sp.dma_start(ring[:, s, i * 512:(i + 1) * 512],
                                 cache[bass.ds(page, 1)].rearrange("o t h d -> (o t) (h d)")
                                 ).then_inc(landed[s], 16)

            for l in range(L):
                w_in = a["w_in"][l]
                for key, c0 in (("q", 0), ("k", 512), ("xbc0", 2048), ("xbc1", 2560)):
                    columns((l, key), w_in, c0)
                for i in range(2):
                    pages((l, "K", i), a["cache_attn_k"][l], 4 * i)
                for key, c0 in (("v", 1024), ("z", 1536)):
                    columns((l, key), w_in, c0)
                s = rg.claim(sp, (l, "state"))
                sp.dma_start(ring[:, s, :].rearrange("p (j n) -> p j n", j=32),
                             a["state_ssm"][l].rearrange("b h p n -> (b h p) n").rearrange("(j p) n -> p j n", p=P)
                             ).then_inc(landed[s], 16)
                for i in range(3):
                    columns((l, "ckv", i), a["w_ckv"][l], 512 * i)
                for i in range(2):
                    pages((l, "V", i), a["cache_attn_v"][l], 4 * i)
                columns((l, "ckv", 3), a["w_ckv"][l], 512 * 3)
                for i in range(2):
                    columns((l, "out", i), a["w_out"][l], 512 * i)
                for i in range(2):
                    columns((l, "cq", i), a["w_cq"][l], 512 * i)
                s = rg.claim(sp, (l, "mkv"))
                sp.wait_ge(mem_stored, 16 * 8 * (l + 1))
                for i, src in enumerate((o_mk, o_mv)):
                    sp.dma_start(ring[:, s, :].rearrange("p (t n) -> p t n", t=2)[:, :, 1024 * i:1024 * (i + 1)],
                                 src[l, 0].rearrange("(t p) h d -> p t (h d)", p=P)).then_inc(landed[s], 16)
                for kind, name in (("mK", "cache_mem_k"), ("mV", "cache_mem_v")):
                    for i in range(4):
                        s = rg.claim(sp, (l, kind, i))
                        for j in range(2):
                            sp.dma_start(ring[:, s, 2048 * j:2048 * (j + 1)].rearrange("p (t n) -> p t n", t=2),
                                         a[name][l, 2 * i + j].rearrange("(t p) h d -> p t (h d)", p=P)
                                         ).then_inc(landed[s], 16)
                for i in range(2):
                    columns((l, "co", i), a["w_co"][l], 512 * i)
                if l == 0:
                    gu = a["w_ffn_gu"][0].rearrange("(k p) (u n) -> p k u n", p=P, u=2)
                    for f in range(NGU):
                        s = rg.claim(sp, (l, "gu", f))
                        d = ring[:, s, :].rearrange("p (k u n) -> p k u n", k=KT, u=2)
                        for u in range(2):
                            sp.dma_start(d[:, :, u, :], gu[:, :, u, f * GU:(f + 1) * GU]).then_inc(landed[s], 16)
                    dn = a["w_ffn_down"][0].rearrange("(f p) n -> p f n", p=P)
                    for i in range(NDN):
                        half, f0 = i // 3, 8 * (i % 3)
                        nf = min(8, FT - f0)
                        s = rg.claim(sp, (l, "dn", i))
                        sp.dma_start(ring[:, s, 0:nf * 512].rearrange("p (f n) -> p f n", f=nf),
                                     dn[:, f0:f0 + nf, half * 512:(half + 1) * 512]).then_inc(landed[s], 16)
            assert rg.next == e_start

            def load(e, p):
                kind, i, s, _ = epos[p]
                if kind == "gu":
                    gu = a["w_exp_gu"][0][bass.ds(e, 1)].rearrange("o (k p) (u n) -> p (o k) u n", p=P, u=2)
                    d = ring[:, s, :].rearrange("p (k u n) -> p k u n", k=KT, u=2)
                    for u in range(2):
                        sp.dma_start(d[:, :, u, :], gu[:, :, u, i * GU:(i + 1) * GU]).then_inc(landed[s], 16)
                else:
                    dn = a["w_exp_down"][0][bass.ds(e, 1)].rearrange("o (f p) n -> p (o f) n", p=P)
                    nf = min(4, FT - 4 * i)
                    sp.dma_start(ring[:, s, 0:nf * 1024].rearrange("p (f n) -> p f n", f=nf),
                                 dn[:, 4 * i:4 * i + nf, :]).then_inc(landed[s], 16)

            def expert_chunk_used(e, c, p):
                kind, i, _, _ = epos[p]
                if kind == "gu":
                    sp.wait_ge(gu_full, expert_no(e, c) * NGU + (i + 1))
                else:
                    sp.wait_ge(dn_done, expert_no(e, c) * NDN + (i + 1))

            def rest_of_expert(e, c):
                for p in range(RING, EPOS - 1):
                    expert_chunk_used(e, c, p - RING)
                    load(e, p)

            def start_of_expert(e, c):
                for p in range(RING):
                    expert_chunk_used(e - 1, c, p + 12 if p + 12 < EPOS - 1 else p + 6)
                    load(e, p)

            def stream_experts(c):
                with sp.Fori(0, EXPERTS - 1) as e:
                    rest_of_expert(e, c)
                    start_of_expert(e + 1, c)
                rest_of_expert(EXPERTS - 1, c)

            for p in range(RING):
                rg.freed(sp, e_start + p)
                load(0, p)
            stream_experts(0)
            sp.wait_ge(pos_known, 1)
            most = sp.value_load(cnti[0:1, 0:1], min_val=0, max_val=T)
            for c in range(1, passes):
                with sp.If(most > (0 if always else lots * c)):
                    for p in range(RING):
                        expert_chunk_used(EXPERTS - 1, c - 1, p + 12 if p + 12 < EPOS - 1 else p + 6)
                        load(0, p)
                    stream_experts(c)

        @block.gpsimd
        def _(pool):
            G = nc.gpsimd
            step = Steps(pool, pool_steps)
            nstore = [0]

            def store(dst, src):
                pool.dma_start(dst, src).then_inc(stored, 16)
                nstore[0] += 1

            G.memset(one_col[:], 1.0).then_inc(buffers_set, 1)
            G.memset(mean_col[:], 1.0 / D).then_inc(buffers_set, 1)
            G.memset(st[:], 0.0).then_inc(buffers_set, 1)
            G.memset(lgb[:], 0.0).then_inc(buffers_set, 1)
            G.memset(xpad[:, :, 0:3], 0.0).then_inc(buffers_set, 1)
            pool.wait_ge(const_landed, 16)
            for l in range(L):
                if l:
                    passed(pool, (l - 1, "var", 2))
                pool.dma_start(sc_in, a["state_conv"][l].rearrange("b i n -> (b i) n")
                               ).then_inc(conv_state_landed, 16)
                store(o_cs[l, :, 0:2, :], a["state_conv"][l][:, 1:3, :])
                for i, t in enumerate(DECODE_FIRST):
                    n = TILES[t][1]
                    copied(pool, (l, "tok", "q", t))
                    copied(pool, (l, "tok", "k", t))
                    x = qk_raw[0:n, t, :].rearrange("p (h s d) -> p h s d", h=16, s=2)
                    o = qkr[0:n, t, :].rearrange("p (h s d) -> p h s d", h=16, s=2)
                    w = rope_t[0:n, :].rearrange("p (h d) -> p h d", h=16)
                    cos = const[0:n, C_COS + 32 * t:C_COS + 32 * t + 32].unsqueeze(1).to_broadcast([n, 16, 32])
                    sin = const[0:n, C_SIN + 32 * t:C_SIN + 32 * t + 32].unsqueeze(1).to_broadcast([n, 16, 32])
                    step.inc(G.tensor_tensor(o[:, :, 0, :], x[:, :, 0, :], cos, ALU.mult))
                    step.done(G.tensor_tensor(w, x[:, :, 1, :], sin, ALU.mult))
                    step.inc(G.tensor_tensor(o[:, :, 0, :], o[:, :, 0, :], w, ALU.subtract))
                    step.done(G.tensor_tensor(o[:, :, 1, :], x[:, :, 1, :], cos, ALU.mult))
                    step.done(G.tensor_tensor(w, x[:, :, 0, :], sin, ALU.mult))
                    G.tensor_tensor(o[:, :, 1, :], o[:, :, 1, :], w, ALU.add).then_inc(rope_ready.sem, 1)
                    rope_ready.wait(pool, l, i)
                for t in range(2):
                    store(o_kp[l, 0, t * P:(t + 1) * P].rearrange("t h d -> t (h d)"), qkr[:, t, 512:1024])
                store(o_ks[l, :, 0].rearrange("b h d -> b (h d)"), qkr[0:8, 2, 512:1024])
                copied(pool, (l, "dtb"))
                s = rg.arrived(pool, (l, "state"))
                S = ring[:, s, :].rearrange("p (b j n) -> p b j n", b=8, j=4)
                for b in range(8):
                    G.tensor_tensor(S[:, b], S[:, b], dcol[:, :, 8 + b].unsqueeze(2).to_broadcast([P, 4, SN]),
                                    ALU.mult).then_inc(state_decayed.sem, 1)
                xwsc_ready.wait(pool, l)
                for c in range(2):
                    copied(pool, (l, "xt", c))
                    xv = xtok[:, c, :].rearrange("p (h d) -> p h d", h=SH)
                    step.inc(G.tensor_tensor(
                        xdt[:, c, :].rearrange("p (h d) -> p h d", h=SH), xv,
                        dtv[:, 8 * c:8 * c + 8].unsqueeze(2).to_broadcast([P, SH, SP_]), ALU.mult))
                    G.tensor_tensor(
                        xw[:, c, :].rearrange("p (h d) -> p h d", h=SH), xv,
                        xwsc[:, 8 * c:8 * c + 8].unsqueeze(2).to_broadcast([P, SH, SP_]), ALU.mult
                    ).then_inc(xdt_ready.sem, 1)
                for t, (_, n) in enumerate(TILES):
                    copied(pool, (l, "xt", t))
                    G.tensor_tensor(
                        mix[0:n, t, 512:1024].rearrange("p (h d) -> p h d", h=SH),
                        xtok[0:n, t, :].rearrange("p (h d) -> p h d", h=SH),
                        raw8[0:n, 2, l, :].unsqueeze(2).to_broadcast([n, SH, SP_]), ALU.mult
                    ).then_inc(xskip_ready.sem, 1)
                copied(pool, (l, "cp", 1))
                store(o_cp[l, 0], conv_rows[0:3])
                store(o_cs[l, :, 2, :], conv_rows[3:11])
                copied(pool, (l, "tok", "v", 2))
                for t in range(2):
                    store(o_vp[l, 0, t * P:(t + 1) * P].rearrange("t h d -> t (h d)"), vz[:, t, 0:512])
                store(o_vs[l, :, 0].rearrange("b h d -> b (h d)"), vz[0:8, 2, 0:512])
                ysT_ready.wait(pool, l)
                pool.dma_start(o_ss[l].rearrange("b h p n -> (b h p) n").rearrange("(j p) n -> p j n", p=P),
                               ring[:, s, :].rearrange("p (j n) -> p j n", j=32)).then_inc(state_stored, 16)
                copied(pool, (l, "stT"))
                store(o_sp[l, 0].rearrange("h p n -> (h p) n").rearrange("(j p) n -> p j n", p=P), ssm_rows)
                assert nstore[0] == STORES_LAYER * (l + 1)
                if l == 0:
                    passed(pool, (l, "d", 7))
                    G.memset(xpad[:, :, 0:3], 0.0).then_inc(buffers_set, 1)
                else:
                    passed(pool, (l, "co", 7))
                    pool.wait_ge(stored, 16 * STORES_LAYER * (l + 1))
                    for k in range(KT):
                        G.memset(acc[:, k, :], 0.0).then_inc(part_added, 1)
                    G.memset(gates[:], 0.0).then_inc(buffers_set, 1)
                    G.memset(posp[:], -1.0).then_inc(buffers_set, 1)
            copied(pool, ("out", 5))
            store(y_p[0].rearrange("(t p) n -> p t n", p=P), y_tok[:, 0:2, :])
            store(y_s[:, 0, :], y_tok[0:8, 2, :])
            assert nstore[0] == NSTORES
            pool.wait_ge(stored, 16 * NSTORES)
            pool.wait_ge(state_stored, 16 * L)
            pool.wait_ge(mem_stored, 16 * 8 * L)

        GU_BANKS, T_BANKS, Y_BANKS, X_BANKS = banks[0:2], banks[2:4], banks[4:6], banks[6:8]

        def expert_products(pe, mm, tr):
            def gather(e, c):
                pe.wait_ge(sel_ready, expert_no(e, c) + (c + 1))
                pe.wait_ge(part_added, parts_added(e, c) if isinstance(e, int) else parts_added(e - 1, c))
                for n in range(2):
                    for k in range(4):
                        for t, (_, rows) in enumerate(TILES):
                            last = mm(X_BANKS[n][:, k * lots:(k + 1) * lots],
                                      x_tok[0:rows, t, (4 * n + k) * P:(4 * n + k + 1) * P],
                                      Sel[0:rows, t, 0:lots], t == 0, t == 2)
                    last.then_inc(X_full, 1)

            def scatter_matrix(taken):
                if taken is not None:
                    pe.wait_ge(T_done, taken)
                for t, (t0, rows) in enumerate(TILES):
                    last = tr(T_BANKS[1][0:lots, t0:t0 + rows], GSel[0:rows, t, 0:lots], rows)
                last.then_inc(T_full, 1)

            def expert(e, c):
                i = expert_no(e, c)
                tb = transposes_before(e, c)

                def weights(p):
                    _, _, s, v = epos[p]
                    pe.wait_ge(landed[s], i * eper[s] + (rg.slot_total[s] + v))
                    return ring[:, s, :]

                def gate_up(f):
                    w = weights(f).rearrange("p (k n) -> p k n", k=KT)
                    if f >= 2:
                        pe.wait_ge(h_ready, i * NGU + (f - 1))
                    for k in range(KT):
                        last = mm(GU_BANKS[f % 2][0:lots, :], xgT[:, k, 0:lots], w[:, k, :], k == 0, k == KT - 1)
                    last.then_inc(gu_full, 1)

                def transpose_h(f):
                    pe.wait_ge(h_ready, i * NGU + (f + 1))
                    pe.wait_ge(T_done, tb + max(f - 1, 0))
                    for s in range(2):
                        last = tr(T_BANKS[f % 2][:, s * lots:(s + 1) * lots],
                                  hh[0:lots, f % 2, s * P:(s + 1) * P], lots)
                    last.then_inc(T_full, 1)

                def down(d):
                    w = weights(NGU + d).rearrange("p (f n) -> p f n", n=1024)
                    nf = min(4, FT - 4 * d)
                    pe.wait_ge(T_done, tb + ((4 * d + nf - 1) // 2 + 1))
                    for f in range(nf):
                        for n in range(2):
                            ff = 4 * d + f
                            last = mm(Y_BANKS[n][0:lots, :], heT[:, ff, 0:lots], w[:, f, n * 512:(n + 1) * 512],
                                      ff == 0, ff == FT - 1)
                    last.then_inc(dn_done, 1)

                pe.wait_ge(xg_taken, i * 2 + 2 * (c + 1))
                for f in range(NGU):
                    gate_up(f)
                    if f:
                        transpose_h(f - 1)
                down(0)
                transpose_h(NGU - 1)
                for d in range(1, NDN):
                    down(d)
                gather(e + 1, c)
                pe.wait_ge(y_by_act, i + 1)
                pe.wait_ge(y_by_dve, i + 1)
                for k in range(KT):
                    if k < 2:
                        pe.wait_ge(xg_taken, i * 2 + (2 * (c + 1) + k + 1))
                    else:
                        pe.wait_ge(part_added, parts_added(e, c) + (k - 1))
                    last = mm(X_BANKS[k % 2][:, 0:T], ye[0:lots, k * P:(k + 1) * P], GSelT[0:lots, :], True, True)
                    last.then_inc(X_full, 1)
                scatter_matrix(tb + (NGU - 1))

            def one_pass(c):
                gather(0, c)
                scatter_matrix(transposes_before(0, c) - 1 if c else None)
                with pe.Fori(0, EXPERTS) as e:
                    expert(e, c)

            one_pass(0)
            pe.wait_ge(pos_known, 1)
            most = pe.value_load(cnti[0:1, 0:1], min_val=0, max_val=T)
            for c in range(1, passes):
                with pe.If(most > (0 if always else lots * c)):
                    one_pass(c)

        @block.tensor
        def _(pe):
            M = nc.tensor

            def mm(out, lhsT, rhs, start, stop):
                return M.matmul(out, lhsT, rhs, start=start, stop=stop)

            def tr(out, in_, n):
                return M.transpose(out, in_, ident[0:n, 0:n])

            def full(ins):
                ins.then_inc(psum_full, 1)

            def slot(key):
                return ring[:, rg.arrived(pe, key), :]

            def blocks8(name, src, wait=None):
                for n in range(5):
                    t = n // 2
                    rows = TILES[t][1]
                    if wait is not None:
                        wait(t)
                    bk = turns.open(pe, name + (n,))
                    ks = range(8) if t == 2 else range(4 * (n % 2), 4 * (n % 2) + 4)
                    for j, k in enumerate(ks):
                        last = tr(bk[:, j * rows:(j + 1) * rows], src[0:rows, t, k * P:(k + 1) * P], rows)
                    full(last)

            def to_tokens(name):
                for n in range(6):
                    t, h = n // 2, n % 2
                    t0, rows = TILES[t]
                    bk = turns.open(pe, name + (n,))
                    for j in range(4):
                        last = tr(bk[0:rows, j * P:(j + 1) * P], xT[:, 4 * h + j, t0:t0 + rows], P)
                    full(last)

            def block_of(w, name, m, rhs):
                bk = turns.open(pe, name + (m,))
                for k in range(KT):
                    last = mm(bk[:, 0:T], w[:, k, (m % 4) * P:(m % 4 + 1) * P], rhs[:, k, :], k == 0, k == KT - 1)
                full(last)

            def columns_of(key, name, m0, rhs):
                w = slot(key).rearrange("p (k n) -> p k n", k=KT)
                for m in range(4):
                    block_of(w, name, m0 + m, rhs)

            def norm_sums(l, i, part):
                bk = turns.open(pe, (l, "mu", i))
                for k in range(KT):
                    if part:
                        copied(pe, (l, part, k))
                    last = mm(bk[:, 0:T], mean_of, R[:, k, :], k == 0, k == KT - 1)
                full(last)
                bk = turns.open(pe, (l, "var", i))
                for k in range(KT):
                    if k % 4 == 0:
                        squared.wait(pe, l, 2 * i + k // 4)
                    last = mm(bk[:, 0:T], mean_of, SQ[:, k, :], k == 0, k == KT - 1)
                full(last)

            def x_ready(l, i):
                if l < 0:
                    copied(pe, ("xin", 4))
                else:
                    xT_act.wait(pe, l, i)
                    xT_dve.wait(pe, l, i)

            pe.wait_ge(const_landed, 16)
            pe.wait_ge(vecs_landed, 16 * 6)
            bk = turns.open(pe, ("vec",))
            tr(bk[:, 0:122], vraw[0:122, 0, :], 122)
            full(tr(bk[:, 128:192], vraw[0:64, 1, :], 64))
            blocks8(("xin",), slot(("x",))[:, 0:3072].rearrange("p (t n) -> p t n", t=3))
            mem_in = slot(("mem",))[:, 0:2048].rearrange("p (t n) -> p t n", t=2)
            for n in range(4):
                bk = turns.open(pe, ("mem", n))
                for j in range(4):
                    k = 4 * (n % 2) + j
                    last = tr(bk[:, j * P:(j + 1) * P], mem_in[:, n // 2, k * P:(k + 1) * P], P)
                full(last)
            pe.wait_ge(buffers_set, 5)
            pe.wait_ge(small_landed, 16 * 9)

            for l in range(L):
                x_ready(l - 1, 2)
                bk = turns.open(pe, (l, "dt"))
                for t, (t0, n) in enumerate(TILES):
                    for k in range(KT):
                        mm(bk[0:n, 8 * t:8 * t + 8], xT[:, k, t0:t0 + n], wdt[:, l, k, :], k == 0, k == KT - 1)
                for k in range(KT):
                    last = mm(bk[0:8, 24:32], wdt[:, l, k, :], xT[:, k, NP_TOK:T], k == 0, k == KT - 1)
                full(last)

                def token_major(c, t):
                    w = slot((l, c)).rearrange("p (k n) -> p k n", k=KT)
                    t0, n = TILES[t]
                    bk = turns.open(pe, (l, "tok", c, t))
                    for k in range(KT):
                        last = mm(bk[0:n, :], xT[:, k, t0:t0 + n], w[:, k, :], k == 0, k == KT - 1)
                    full(last)

                def memory_part(i):
                    c, t = divmod(i, 2)
                    w = slot((l, "ckv", c)).rearrange("p (k n) -> p k n", k=KT)
                    bk = turns.open(pe, (l, "mkv", i))
                    if l == 0 and i == 0:
                        copied(pe, ("mem", 3))
                    for k in range(KT):
                        last = mm(bk[:], memT[:, k, t * P:(t + 1) * P], w[:, k, :], k == 0, k == KT - 1)
                    full(last)

                for c in ("q", "k"):
                    for t in DECODE_FIRST:
                        token_major(c, t)
                bk = turns.open(pe, (l, "acs"))
                da_ready.wait(pe, l)
                for c in range(2):
                    mm(bk[:, 8 * c:8 * c + 8], upper, da[:, 8 * c:8 * c + 8], True, True)
                for c in range(2):
                    last = mm(bk[:, 16 + 8 * c:24 + 8 * c], ones, da[:, 8 * c:8 * c + 8], True, True)
                full(last)
                bk = turns.open(pe, (l, "scT"))
                pe.wait_ge(conv_state_landed, 16 * (l + 1))
                for m in range(8):
                    last = tr(bk[:, 24 * m:24 * m + 24], sc_in[:, m * P:(m + 1) * P], 24)
                full(last)
                rope_ready.wait(pe, l, 0)
                for b in range(8):
                    w = slot((l, f"xbc{b // 4}")).rearrange("p (k n) -> p k n", k=KT)
                    block_of(w, (l, "xbc"), b, xT)
                    bk = turns.open(pe, (l, "qb", b))
                    full(mm(bk[:], ident[0:8, b:b + 1].to_broadcast([8, P]), qkr[0:8, 2, 0:512], True, True))
                    if b == 0:
                        bk = turns.open(pe, (l, "dtb"))
                        decays_out.wait(pe, l)
                        for h in range(SH):
                            r0, j = 64 * (h % 2), h // 2
                            this_head = ident[0:8, h:h + 1].to_broadcast([8, 64])
                            mm(bk[r0:r0 + 64, 16 * j:16 * j + 8], this_head, dtv[0:8, 24:32], True, True)
                            last = mm(bk[r0:r0 + 64, 16 * j + 8:16 * j + 16], this_head, ex[0:8, 48:56], True, True)
                        full(last)
                token_major("v", 0)
                bk = turns.open(pe, (l, "sST"))
                dec_scores.wait(pe, l)
                for g in range(2):
                    tr(bk[0:64, g * P:(g + 1) * P], sS[:, g].rearrange("p b h -> p (b h)"), P)
                full(mm(bk[0:64, 256:257], sbt[0:8, :], one_col[0:8, :], True, True))
                token_major("v", 1)
                token_major("v", 2)
                conv_ready.wait(pe, l, 8)
                for t, (t0, n) in enumerate(TILES):
                    bk = turns.open(pe, (l, "xt", t))
                    for j in range(4):
                        last = tr(bk[0:n, j * P:(j + 1) * P], convT[:, j, t0:t0 + n], P)
                    full(last)
                    bk = turns.open(pe, (l, "Bt", t))
                    for j in range(4 if t == 2 else 2):
                        last = tr(bk[0:n, j * P:(j + 1) * P], convT[:, 4 + j, t0:t0 + n], P)
                    full(last)
                for h in range(2):
                    bk = turns.open(pe, (l, "cp", h))
                    for j in range(4):
                        last = tr(bk[0:11, j * P:(j + 1) * P], ct11[:, 4 * h + j, :], P)
                    full(last)
                copied(pe, (l, "Bt", 2))
                for i in range(4):
                    for b in (2 * i, 2 * i + 1):
                        bk = turns.open(pe, (l, "BC", b))
                        full(mm(bk[:], ident[0:8, b:b + 1].to_broadcast([8, P]), BCs, True, True))
                    if i < 3:
                        token_major("z", i)
                    if i == 0:
                        bk = turns.open(pe, (l, "pT"))
                        dec_probs.wait(pe, l)
                        for g in range(2):
                            last = tr(bk[:, g * 64:(g + 1) * 64], pSx[:, g * P:(g + 1) * P], 64)
                        full(last)
                        bk = turns.open(pe, (l, "pself"))
                        full(mm(bk[0:8, 0:8], const[0:64, C_REQ:C_REQ + 8], pself_r[:], True, True))
                memory_part(0)
                for c in range(2):
                    bk = turns.open(pe, (l, "st", c))
                    xdt_ready.wait(pe, l, c)
                    copied(pe, (l, "Bt", c))
                    for g in range(SG):
                        last = mm(bk[:, g * 256:(g + 1) * 256], Btok[:, c, g * P:(g + 1) * P],
                                  xw[:, c, g * 256:(g + 1) * 256], True, True)
                    full(last)
                for c in range(2):
                    for g in range(SG):
                        bk = turns.open(pe, (l, "ab", c, g))
                        for r in range(4):
                            h = 8 * c + 4 * g + r
                            last = mm(bk[:, r * P:(r + 1) * P], da[:, h:h + 1].to_broadcast([P, P]), upper,
                                      True, True)
                        full(last)
                    bk = turns.open(pe, (l, "cb", c))
                    for g in range(SG):
                        last = mm(bk[:, g * P:(g + 1) * P], convT[:, 4 + g, c * P:(c + 1) * P],
                                  convT[:, 6 + g, c * P:(c + 1) * P], True, True)
                    full(last)
                    memory_part(1 + c)
                    bk = turns.open(pe, (l, "y", c))
                    copied(pe, (l, "cb", c))
                    for h in range(SH):
                        last = mm(bk[:, h * SP_:(h + 1) * SP_], Mdec[:, h // 4, h % 4, :],
                                  xdt[:, c, h * SP_:(h + 1) * SP_], True, True)
                    full(last)
                bk = turns.open(pe, (l, "yo"))
                copied(pe, (l, "st", 0))
                for g in range(SG):
                    last = mm(bk[:, g * 256:(g + 1) * 256], convT[:, 6 + g, P:2 * P],
                              ST0[:, g * 256:(g + 1) * 256], True, True)
                full(last)
                bk = turns.open(pe, (l, "stT"))
                copied(pe, (l, "st", 1))
                for j in range(4):
                    last = tr(bk[:, j * P:(j + 1) * P], STf[:, j * P:(j + 1) * P], P)
                full(last)
                bk = turns.open(pe, (l, "ysT"))
                ysT_ready.wait(pe, l)
                for j in range(4):
                    last = tr(bk[0:8, j * P:(j + 1) * P], ysT[:, j, :], P)
                full(last)
                rope_ready.wait(pe, l, 2)
                for i in range(4):
                    bk = turns.open(pe, (l, "qkT", i))
                    for j in range(2):
                        for t in range(2):
                            last = tr(bk[:, j * 256 + t * P:j * 256 + (t + 1) * P],
                                      qkr[:, t, (2 * i + j) * P:(2 * i + j + 1) * P], P)
                    full(last)
                copied(pe, (l, "qkT", 3))
                for qt in range(2):
                    nk = (qt + 1) * P
                    for hp in range(2):
                        for m in range(2):
                            bk = turns.open(pe, (l, "S", qt, hp, m))
                            for j in range(2):
                                h = 2 * hp + j
                                last = mm(bk[:, j * nk:(j + 1) * nk],
                                          kqT[64 * m:64 * m + 64, h, qt * P:(qt + 1) * P],
                                          kqT[64 * m:64 * m + 64, 4 + h, 0:nk], True, True)
                            full(last)
                    memory_part(3 + qt)

                def attend(qt):
                    for kt in range(qt + 1):
                        bk = turns.open(pe, (l, "aT", qt, kt))
                        a_ready.wait(pe, l, qt)
                        for h in range(AH):
                            last = tr(bk[:, h * P:(h + 1) * P], probs[:, h, 0, kt * P:(kt + 1) * P], P)
                        full(last)
                    bk = turns.open(pe, (l, "O", qt))
                    copied(pe, (l, "aT", qt, qt))
                    for h in range(AH):
                        for kt in range(qt + 1):
                            last = mm(bk[:, h * P:(h + 1) * P], aT[:, qt + kt, h, :],
                                      vz[:, kt, h * DV:(h + 1) * DV], kt == 0, kt == qt)
                    full(last)

                attend(0)
                memory_part(5)
                bk = turns.open(pe, (l, "oS"))
                copied(pe, (l, "pT"))
                for i in range(2):
                    V4 = slot((l, "V", i)).rearrange("p (b g n) -> p b g n", b=4, g=2)
                    for j in range(4):
                        b = 4 * i + j
                        for h in range(AH):
                            for g in range(2):
                                last = mm(bk[:, h * 8 + b:h * 8 + b + 1], V4[:, j, g, h * DV:(h + 1) * DV],
                                          aTs[:, g, b, h:h + 1], g == 0, g == 1)
                full(last)
                memory_part(6)
                bk = turns.open(pe, (l, "oSt"))
                copied(pe, (l, "oS"))
                for h in range(AH):
                    last = tr(bk[0:8, h * P:(h + 1) * P], attS[:, h * 8:(h + 1) * 8], P)
                full(last)
                attend(1)
                memory_part(7)
                blocks8((l, "mixT"), mix, lambda t: mix_ready.wait(pe, l, NORM_ORDER.index(t)))
                copied(pe, (l, "mixT", 4))
                columns_of((l, "out", 0), (l, "m"), 0, mixT)
                columns_of((l, "out", 1), (l, "m"), 4, mixT)
                mkv = slot((l, "mkv")).rearrange("p (t n) -> p t n", t=2)
                for i in range(4):
                    bk = turns.open(pe, (l, "mkT", i))
                    for j in range(2):
                        for t in range(2):
                            last = tr(bk[:, j * 256 + t * P:j * 256 + (t + 1) * P],
                                      mkv[:, t, (2 * i + j) * P:(2 * i + j + 1) * P], P)
                    full(last)
                norm_sums(l, 0, "m")
                x_ready(l, 0)
                columns_of((l, "cq", 0), (l, "cq"), 0, xT)
                columns_of((l, "cq", 1), (l, "cq"), 4, xT)
                copied(pe, (l, "cq", 7))
                for t in range(2):
                    for hp in range(2):
                        bk = turns.open(pe, (l, "cS", t, hp))
                        for j in range(2):
                            h = 2 * hp + j
                            for d in range(2):
                                last = mm(bk[:, j * 256:(j + 1) * 256], qcT[:, 2 * h + d, t * P:(t + 1) * P],
                                          mkT[:, 2 * h + d, :], d == 0, d == 1)
                        full(last)
                for i in range(2):
                    bk = turns.open(pe, (l, "qsT", i))
                    for j in range(4):
                        last = tr(bk[0:8, j * P:(j + 1) * P], qcT[:, 4 * i + j, NP_TOK:T], P)
                    full(last)
                for t in range(2):
                    for kt in range(2):
                        bk = turns.open(pe, (l, "cPT", t, kt))
                        cP_ready.wait(pe, l, t)
                        for h in range(MH):
                            last = tr(bk[:, h * P:(h + 1) * P], cP[:, t, h, kt * P:(kt + 1) * P], P)
                        full(last)
                copied(pe, (l, "cPT", 1, 1))
                for i in range(4):
                    bk = turns.open(pe, (l, "cO", i))
                    for d in range(2):
                        for kt in range(2):
                            last = mm(bk[:, d * 256:(d + 1) * 256],
                                      mkv[:, kt, 1024 + i * MD + d * P:1024 + i * MD + (d + 1) * P],
                                      cPT[:, kt, i, :], kt == 0, kt == 1)
                    full(last)
                copied(pe, (l, "qsT", 1))
                for b in range(8):
                    for i in range(2):
                        bk = turns.open(pe, (l, "qsb", b, i))
                        full(mm(bk[:], ident[0:8, b:b + 1].to_broadcast([8, P]), qs[0:8, i * 512:(i + 1) * 512],
                                True, True))
                bk = turns.open(pe, (l, "sCT"))
                cs_scores.wait(pe, l)
                for t in range(2):
                    last = tr(bk[0:32, t * P:(t + 1) * P], sC[:, t].rearrange("p b h -> p (b h)"), P)
                full(last)
                bk = turns.open(pe, (l, "sPT"))
                cs_probs.wait(pe, l)
                for t in range(2):
                    last = tr(bk[:, t * 32:(t + 1) * 32], sP[0:32, t * P:(t + 1) * P], 32)
                full(last)
                bk = turns.open(pe, (l, "soT"))
                copied(pe, (l, "sPT"))
                for i in range(4):
                    V2 = slot((l, "mV", i)).rearrange("p (b t n) -> p b t n", b=2, t=2)
                    for j in range(2):
                        b = 2 * i + j
                        for m in range(8):
                            for t in range(2):
                                last = mm(bk[:, m * 8 + b:m * 8 + b + 1], V2[:, j, t, m * P:(m + 1) * P],
                                          sPTs[:, t, b * 4 + m // 2:b * 4 + m // 2 + 1], t == 0, t == 1)
                full(last)
                copied(pe, (l, "cO", 3))
                copied(pe, (l, "soT"))
                columns_of((l, "co", 0), (l, "co"), 0, oT)
                columns_of((l, "co", 1), (l, "co"), 4, oT)
                norm_sums(l, 1, "co")
                x_ready(l, 1)
                if l == 0:
                    for f in range(NGU):
                        w = slot((l, "gu", f)).rearrange("p (k u n) -> p k u n", k=KT, u=2)
                        for s in range(2):
                            for u in range(2):
                                bk = turns.open(pe, (l, "gu"[u], f, s))
                                for k in range(KT):
                                    last = mm(bk[:, 0:T], w[:, k, u, s * P:(s + 1) * P], xT[:, k, :],
                                              k == 0, k == KT - 1)
                                full(last)
                    for half in range(2):
                        bks = [turns.open(pe, (l, "d", 4 * half + m)) for m in range(4)]
                        for i in range(3):
                            w = slot((l, "dn", 3 * half + i)).rearrange("p (f n) -> p f n", n=512)
                            nf = min(8, FT - 8 * i)
                            f_last = 8 * i + nf - 1
                            copied(pe, (l, "u", f_last // 2, f_last % 2))
                            for m in range(4):
                                for f in range(nf):
                                    ff = 8 * i + f
                                    last = mm(bks[m][:, 0:T], w[:, f, m * P:(m + 1) * P], hT[:, ff, :],
                                              ff == 0, ff == FT - 1)
                                if i == 2:
                                    full(last)
                    norm_sums(l, 2, "d")
                else:
                    to_tokens((l, "xtok"))
                    bk = turns.open(pe, (l, "lg"))
                    for t, (t0, n) in enumerate(TILES):
                        for k in range(KT):
                            last = mm(bk[0:n, 8 * t:8 * t + 8], xT[:, k, t0:t0 + n], wr[:, k, :],
                                      k == 0, k == KT - 1)
                    full(last)
                    bk = turns.open(pe, (l, "pos"))
                    pe.wait_ge(sel_known, 1)
                    for t, (_, n) in enumerate(TILES):
                        for u in range(t):
                            mm(bk[0:n, 8 * t:8 * t + 8], one_col[:].to_broadcast([P, n]), sel[:, u, :], u == 0, False)
                        mm(bk[0:n, 8 * t:8 * t + 8], before[0:n, 0:n], sel[0:n, t, :], t == 0, True)
                    for t, (_, n) in enumerate(TILES):
                        last = mm(bk[:, 24:32], one_col[0:n, :].to_broadcast([n, P]), sel[0:n, t, :], t == 0, t == 2)
                    full(last)
                    copied(pe, (l, "xtok", 5))
                    copied(pe, (l, "pos"))
                    expert_products(pe, mm, tr)
                    pe.wait_ge(moe_done, 1)
                    norm_sums(l, 2, None)
            x_ready(L - 1, 2)
            to_tokens(("out",))

        def expert_activations(act):
            S = nc.scalar

            def take_gathered(e, c):
                for n in range(2):
                    act.wait_ge(X_full, x_groups_before(e, c) + (n + 1 - 2))
                    S.activation(xgT[:, 4 * n:4 * n + 4, 0:lots],
                                 X_BANKS[n][:, 0:4 * lots].rearrange("p (k n) -> p k n", k=4), ACT.Copy
                                 ).then_inc(xg_taken, 1)

            def take_scatter(count):
                act.wait_ge(T_full, count)
                S.activation(GSelT[0:lots, :], T_BANKS[1][0:lots, 0:T], ACT.Copy).then_inc(T_done, 1)

            def expert(e, c):
                i = expert_no(e, c)
                tb = transposes_before(e, c)
                for f in range(NGU + 1):
                    if f < NGU:
                        act.wait_ge(gu_full, i * NGU + (f + 1))
                        if f >= 2:
                            act.wait_ge(h_ready, i * NGU + (f - 1))
                        S.activation(sg[0:lots, f % 2, :], GU_BANKS[f % 2][0:lots, 0:GU], ACT.Silu
                                     ).then_inc(sg_ready, 1)
                    if f:
                        act.wait_ge(T_full, tb + f)
                        S.activation(heT[:, 2 * f - 2:2 * f, 0:lots],
                                     T_BANKS[(f - 1) % 2][:, 0:2 * lots].rearrange("p (s n) -> p s n", s=2),
                                     ACT.Copy).then_inc(T_done, 1)
                act.wait_ge(dn_done, i * NDN + NDN)
                S.activation(ye[0:lots, 0:512], Y_BANKS[0][0:lots, :], ACT.Copy).then_inc(y_by_act, 1)
                for n in range(2):
                    act.wait_ge(X_full, x_groups_before(e, c) + (n + 1))
                    S.activation(xgT[:, 4 * n:4 * n + 4, 0:lots],
                                 X_BANKS[n][:, 0:4 * lots].rearrange("p (k n) -> p k n", k=4), ACT.Copy
                                 ).then_inc(xg_taken, 1)
                take_scatter(tb + (NGU + 1))

            def one_pass(c):
                take_gathered(0, c)
                take_scatter(transposes_before(0, c))
                with act.Fori(0, EXPERTS) as e:
                    expert(e, c)

            one_pass(0)
            act.wait_ge(pos_known, 1)
            most = act.value_load(cnti[0:1, 0:1], min_val=0, max_val=T)
            for c in range(1, passes):
                with act.If(most > (0 if always else lots * c)):
                    one_pass(c)

        @block.scalar
        def _(act):
            S = nc.scalar
            step = Steps(act, act_steps)

            def copy_out(name, dst, src, func=ACT.Copy):
                bk = take(act, name)
                emptied_after(name, S.activation(dst, src(bk), func))

            def norm(l, i):
                for h in range(2):
                    if h == 0:
                        centred.wait(act, l, i)
                    else:
                        copied(act, (l, "mu", i))
                    S.activation(SQ[:, 4 * h:4 * h + 4, :], R[:, 4 * h:4 * h + 4, :], ACT.Square
                                 ).then_inc(squared.sem, 1)
                copied(act, (l, "var", i))
                step.done(S.activation(stat[:, 1, :], stat[:, 0, :], ACT.Ln))
                S.activation(stat[:, 1, :], stat[:, 1, :], ACT.Exp, scale=-0.5).then_inc(ln_rstd.sem, 1)
                scaled.wait(act, l, 2 * i)
                for k in range(4):
                    ins = S.activation(xT[:, k, :], R[:, k, :], ACT.Identity, bias=col_b(l, i, k),
                                       scale=col_g(l, i, k))
                ins.then_inc(xT_act.sem, 1)

            act.wait_ge(small_landed, 16 * 9)
            step.inc(S.activation(raw8[:, 1], raw8[:, 1], ACT.Exp))
            S.activation(col8[:, 1, :], col8[:, 1, :], ACT.Exp).then_inc(setup_exps, 1)
            act.wait_ge(lam_dots, 1)
            S.activation(lamt[:], lamt[:], ACT.Exp).then_inc(setup_exps, 1)
            for n in range(4):
                copy_out(("mem", n), memT[:, 4 * (n % 2):4 * (n % 2) + 4, (n // 2) * P:(n // 2 + 1) * P],
                         lambda bk: bk[:].rearrange("p (k n) -> p k n", k=4))
            act.wait_ge(vectors_ready, 1)
            act.wait_ge(buffers_set, 5)

            for l in range(L):
                dt_abs.wait(act, l)
                S.activation(dte, dte, ACT.Exp, scale=-1.0).then_inc(dt_exp.sem, 1)
                dt_exp1.wait(act, l)
                S.activation(dte, dte, ACT.Ln).then_inc(dt_ln.sem, 1)
                if l:
                    act.wait_ge(buffers_set, 6)
                for c, name in enumerate(("q", "k")):
                    for t in DECODE_FIRST:
                        n = TILES[t][1]
                        copy_out((l, "tok", name, t), qk_raw[0:n, t, 512 * c:512 * (c + 1)], lambda bk: bk[0:n, :])
                decays_in.wait(act, l)
                S.activation(ex, sc, ACT.Exp).then_inc(decays_out.sem, 1)
                for m in range(10):
                    if m < 8:
                        copied(act, (l, "xbc", m))
                        S.activation(convT[:, m, 0:NP_TOK], xpad[:, m, 0:NP_TOK], ACT.Identity,
                                     bias=cols_cb(l, m), scale=col_cw(l, 0, m)).then_inc(tap0_done.sem, 1)
                    if m >= 2:
                        taps_done.wait(act, l, m - 2)
                        S.activation(convT[:, m - 2, 0:NP_TOK], convT[:, m - 2, 0:NP_TOK], ACT.Silu
                                     ).then_inc(conv_ready.sem, 1)
                taps_done.wait(act, l, 8)
                S.activation(convT[:, :, NP_TOK:T], convT[:, :, NP_TOK:T], ACT.Silu).then_inc(conv_ready.sem, 1)
                for t, (_, n) in enumerate(TILES):
                    copy_out((l, "tok", "v", t), vz[0:n, t, 0:512], lambda bk: bk[0:n, :])
                dec_rows.wait(act, l)
                S.activation(pSx, pSx, ACT.Exp, bias=nb1[0:64], scale=DQ ** -0.5, accum_out=rs1[0:64]
                             ).then_inc(dec_exp.sem, 1)
                rope_ready.wait(act, l, 2)
                for t, (_, n) in enumerate(TILES):
                    copy_out((l, "xt", t), xtok[0:n, t, :], lambda bk: bk[0:n, :])
                    if t < 2:
                        copy_out((l, "Bt", t), Btok[:, t, :], lambda bk: bk[:, 0:256])
                    else:
                        copy_out((l, "Bt", t), BCs, lambda bk: bk[0:8, :])
                for h in range(2):
                    copy_out((l, "cp", h), conv_rows[:, 512 * h:512 * (h + 1)], lambda bk: bk[0:11, :])
                for t, (_, n) in enumerate(TILES):
                    copy_out((l, "tok", "z", t), vz[0:n, t, 512:1024], lambda bk: bk[0:n, :], ACT.Silu)

                def memory_part(i):
                    c, t = divmod(i, 2)
                    n = 8 * l + i
                    if n >= 1:
                        act.wait_ge(mem_stored, 16 * n)
                    copy_out((l, "mkv", i), mem_rows[:], lambda bk: bk[:])
                    copied(act, (l, "mkv", i))
                    out = (o_mk if c < 2 else o_mv)[l, 0, t * P:(t + 1) * P].rearrange("t h d -> t (h d)")
                    act.dma_start(out[:, 512 * (c % 2):512 * (c % 2 + 1)], mem_rows[:]
                                  ).then_inc(mem_stored, 16)

                memory_part(0)
                for n in range(4):
                    seg_ready.wait(act, l, n)
                    S.activation(Mdec[:, n % 2], Mdec[:, n % 2], ACT.Exp).then_inc(decay_ready.sem, 1)
                    if n % 2:
                        memory_part(1 + n // 2)
                copy_out((l, "stT"), ssm_rows, lambda bk: bk[:].rearrange("p (j n) -> p j n", j=4))
                xskip_ready.wait(act, l, 2)
                for i in range(4):
                    copy_out((l, "qkT", i), kqT[:, 2 * i:2 * i + 2, :],
                             lambda bk: bk[:].rearrange("p (j n) -> p j n", j=2))

                def exps(qt):
                    nk = (qt + 1) * P
                    for n in range(4):
                        hp, m = n // 2, n % 2
                        max_ready.wait(act, l, 4 * qt + n)
                        for j in range(2):
                            h = 2 * hp + j
                            ins = S.activation(probs[:, h, m, 0:nk], probs[:, h, m, 0:nk], ACT.Exp,
                                               bias=nb[:, 2 * h + m:2 * h + m + 1], scale=DQ ** -0.5,
                                               accum_out=rs[:, 2 * h + m:2 * h + m + 1])
                            if j == 0:
                                step.inc(ins)
                        ins.then_inc(probs_ready.sem, 1)

                def rms(n):
                    rows = TILES[NORM_ORDER[n]][1]
                    ms_ready.wait(act, l, n)
                    step.done(S.activation(rstd6[0:rows], ms[0:rows], ACT.Ln))
                    S.activation(rstd6[0:rows], rstd6[0:rows], ACT.Exp, scale=-0.5).then_inc(rstd_ready.sem, 1)

                def take_aT(qt, kt):
                    copy_out((l, "aT", qt, kt), aT[:, qt + kt], lambda bk: bk[:].rearrange("p (h n) -> p h n", h=AH))

                exps(0)
                memory_part(3)
                memory_part(4)
                take_aT(0, 0)
                exps(1)
                rms(0)
                memory_part(5)
                memory_part(6)
                take_aT(1, 0)
                take_aT(1, 1)
                rms(1)
                memory_part(7)
                rms(2)
                act.wait_ge(stored, 16 * STORES_LAYER * (l + 1))
                for i in range(4):
                    copy_out((l, "mkT", i), mkT[:, 2 * i:2 * i + 2, :],
                             lambda bk: bk[:].rearrange("p (j n) -> p j n", j=2))
                norm(l, 0)
                for m in range(8):
                    copy_out((l, "cq", m), qcT[:, m, :], lambda bk: bk[:, 0:T])
                for t in range(2):
                    for hp in range(2):
                        q = 2 * t + hp
                        bk = take(act, (l, "cS", t, hp))
                        cmax_ready.wait(act, l, q)
                        for j in range(2):
                            ins = S.activation(cP[:, t, 2 * hp + j, :], bk[:, 256 * j:256 * (j + 1)], ACT.Exp,
                                               bias=nb[:, 2 * q + j:2 * q + j + 1], scale=MD ** -0.5,
                                               accum_out=rs[:, 2 * q + j:2 * q + j + 1])
                            if j == 0:
                                step.inc(ins)
                        emptied_after((l, "cS", t, hp), ins)
                for t in range(2):
                    for kt in range(2):
                        copy_out((l, "cPT", t, kt), cPT[:, kt, :, t * P:(t + 1) * P],
                                 lambda bk: bk[:].rearrange("p (h n) -> p h n", h=MH))
                for i in range(4):
                    copy_out((l, "cO", i), oT[:, 2 * i:2 * i + 2, 0:NP_TOK],
                             lambda bk: bk[:].rearrange("p (j n) -> p j n", j=2))
                cs_rows.wait(act, l)
                S.activation(sP[0:32], sP[0:32], ACT.Exp, bias=nb1[0:32], scale=MD ** -0.5, accum_out=rs1[0:32]
                             ).then_inc(cs_exp.sem, 1)
                norm(l, 1)
                if l == 0:
                    for f in range(NGU):
                        for s in range(2):
                            if f:
                                copied(act, (l, "u", f - 1, s))
                            copy_out((l, "g", f, s), sgd[:, s, :], lambda bk: bk[:, 0:T], ACT.Silu)
                else:
                    for n in range(6):
                        rows = TILES[n // 2][1]
                        copy_out((l, "xtok", n), x_tok[0:rows, n // 2, 512 * (n % 2):512 * (n % 2 + 1)],
                                 lambda bk: bk[0:rows, :])
                    act.wait_ge(lsm_ready, 1)
                    S.activation(lsm[:], lsm[:], ACT.Exp).then_inc(lexp_ready, 1)
                    expert_activations(act)
                norm(l, 2)
            for n in range(6):
                rows = TILES[n // 2][1]
                copy_out(("out", n), y_tok[0:rows, n // 2, 512 * (n % 2):512 * (n % 2 + 1)], lambda bk: bk[0:rows, :])

        def route(l, dve, step):
            V = nc.vector

            def bc(ap, shape, axis):
                return ap.unsqueeze(axis).to_broadcast(shape)

            dve.wait_ge(buffers_set, 8)
            bk = take(dve, (l, "lg"))
            step.inc(V.tensor_copy(lgb[:, 0:2, :], bk[:, 0:16].rearrange("p (t e) -> p t e", t=2)))
            emptied_after((l, "lg"), V.tensor_copy(lgb[0:8, 2, :], bk[0:8, 16:24]))
            copied(dve, (l, "lg"))
            other, this = bc(lgb[:], [P, 3, 8, 8], 2), bc(lgb[:], [P, 3, 8, 8], 3)
            step.inc(V.tensor_tensor(cmp_gt, other, this, ALU.is_gt))
            step.inc(V.tensor_tensor(cmp_eq, other, this, ALU.is_equal))
            step.done(V.reduce_max(l3[:], lgb[:], AX.X))
            tri = const[:, C_TRI:C_TRI + 64].rearrange("p (e j) -> p e j", e=8)
            step.inc(V.tensor_tensor(cmp_eq, cmp_eq, bc(tri, [P, 3, 8, 8], 1), ALU.mult))
            V.tensor_tensor(lsm[:], lgb[:], bc(l3[:], [P, 3, 8], 2), ALU.subtract).then_inc(lsm_ready, 1)
            dve.wait_ge(dve_steps, step.n)
            step.done(V.tensor_tensor(cmp_gt, cmp_gt, cmp_eq, ALU.add))
            step.done(V.reduce_sum(sel[:], cmp_gt, AX.X))
            V.tensor_scalar(sel[:], sel[:], 1.5, None, ALU.is_lt).then_inc(sel_known, 1)
            dve.wait_ge(sel_known, 1)
            dve.wait_ge(lexp_ready, 1)
            step.done(V.tensor_tensor(lsm[:], lsm[:], sel[:], ALU.mult))
            step.done(V.reduce_sum(l3[:], lsm[:], AX.X))
            step.done(V.reciprocal(l3[:], l3[:]))
            step.inc(V.tensor_tensor(gates[:, :, 0:8], lsm[:], bc(l3[:], [P, 3, 8], 2), ALU.mult))
            bk = take(dve, (l, "pos"))
            step.inc(V.tensor_scalar(posp[:, 0:2, 0:8], bk[:, 0:16].rearrange("p (t e) -> p t e", t=2), 1.0, None,
                                     ALU.add))
            step.inc(V.tensor_scalar(posp[0:8, 2, 0:8], bk[0:8, 16:24], 1.0, None, ALU.add))
            emptied_after((l, "pos"), V.reduce_max(cnt[:], bk[0:1, 24:32], AX.X))
            copied(dve, (l, "pos"))
            V.tensor_copy(cnti[:], cnt[:]).then_inc(pos_known, 1)
            dve.wait_ge(dve_steps, step.n)
            step.done(V.tensor_tensor(posp[:, :, 0:8], posp[:, :, 0:8], sel[:], ALU.mult))
            step.done(V.tensor_scalar(posp[:, :, 0:8], posp[:, :, 0:8], -1.0, None, ALU.add))

        def expert_elementwise(dve):
            V = nc.vector

            def selection(col):
                for t, (_, rows) in enumerate(TILES):
                    where = posp[0:rows, t, col]
                    V.tensor_scalar(Sel[0:rows, t, 0:lots], iota[0:rows, 0:lots], where, None, ALU.is_equal)
                    ins = V.tensor_scalar(GSel[0:rows, t, 0:lots], iota[0:rows, 0:lots], where,
                                          gates[0:rows, t, col], ALU.is_equal, ALU.mult)
                ins.then_inc(sel_ready, 1)

            def expert(e, c):
                i = expert_no(e, c)
                tb = transposes_before(e, c)
                dve.wait_ge(T_full, tb)
                selection(bass.ds(e + 1, 1))
                for f in range(NGU):
                    dve.wait_ge(sg_ready, i * NGU + (f + 1))
                    dve.wait_ge(T_full, tb + max(f - 1, 0))
                    V.tensor_tensor(hh[0:lots, f % 2, :], sg[0:lots, f % 2, :], GU_BANKS[f % 2][0:lots, GU:2 * GU],
                                    ALU.mult).then_inc(h_ready, 1)
                dve.wait_ge(dn_done, i * NDN + NDN)
                V.tensor_copy(ye[0:lots, 512:1024], Y_BANKS[1][0:lots, :]).then_inc(y_by_dve, 1)
                dve.wait_ge(part_added, parts_added(e, c))
                for k in range(KT):
                    dve.wait_ge(X_full, x_groups_before(e, c) + (2 + k + 1))
                    V.tensor_tensor(acc[:, k, :], acc[:, k, :], X_BANKS[k % 2][:, 0:T], ALU.add
                                    ).then_inc(part_added, 1)

            def one_pass(c):
                if c:
                    dve.wait_ge(T_full, transposes_before(0, c) - 1)
                    V.tensor_scalar(posp[:], posp[:], -float(lots), None, ALU.add).then_inc(pass_shift, 1)
                    dve.wait_ge(pass_shift, c)
                selection(slice(0, 1))
                with dve.Fori(0, EXPERTS) as e:
                    expert(e, c)

            one_pass(0)
            dve.wait_ge(pos_known, 1)
            most = dve.value_load(cnti[0:1, 0:1], min_val=0, max_val=T)
            for c in range(1, passes):
                with dve.If(most > (0 if always else lots * c)):
                    one_pass(c)
                    dve.wait_ge(part_added, parts_added(EXPERTS, c))

        @block.vector
        def _(dve):
            V = nc.vector
            step = Steps(dve, dve_steps)

            def bc(ap, shape, axis):
                return ap.unsqueeze(axis).to_broadcast(shape)

            def residual(l, name, m):
                bk = take(dve, (l, name, m))
                emptied_after((l, name, m), V.scalar_tensor_tensor(
                    R[:, m, :], xT[:, m, :], ALPHA, bk[:, 0:T], ALU.mult, ALU.add))

            def norm(l, i, part):
                bk = take(dve, (l, "mu", i))
                if part:
                    copied(dve, (l, part, 7))
                for h in range(2):
                    ins = V.tensor_tensor(R[:, 4 * h:4 * h + 4, :], R[:, 4 * h:4 * h + 4, :],
                                          bc(bk[:, 0:T], [P, 4, T], 1), ALU.subtract)
                    if h == 0:
                        ins.then_inc(centred.sem, 1)
                emptied_after((l, "mu", i), ins)
                bk = take(dve, (l, "var", i))
                emptied_after((l, "var", i), V.tensor_scalar(stat[:, 0, :], bk[:, 0:T], EPS, None, ALU.add))
                ln_rstd.wait(dve, l, i)
                copied(dve, (l, "mu", i))
                for h in range(2):
                    V.tensor_tensor(R[:, 4 * h:4 * h + 4, :], R[:, 4 * h:4 * h + 4, :],
                                    bc(stat[:, 1, :], [P, 4, T], 1), ALU.mult).then_inc(scaled.sem, 1)
                scaled.wait(dve, l, 2 * i + 1)
                for k in range(4, 8):
                    ins = V.tensor_scalar(xT[:, k, :], R[:, k, :], col_g(l, i, k), col_b(l, i, k),
                                          ALU.mult, ALU.add)
                ins.then_inc(xT_dve.sem, 1)
                xT_act.wait(dve, l, i)
                xT_dve.wait(dve, l, i)

            bk = take(dve, ("vec",))
            step.inc(V.tensor_copy(vecT[:, 0, 0:122], bk[:, 0:122]))
            emptied_after(("vec",), V.tensor_copy(vecT[:, 1, 0:64], bk[:, 128:192]))
            for n in range(5):
                t, bk = n // 2, take(dve, ("xin", n))
                t0, rows = TILES[t]
                nk = 8 if t == 2 else 4
                k0 = 0 if t == 2 else 4 * (n % 2)
                emptied_after(("xin", n), V.tensor_copy(
                    xT[:, k0:k0 + nk, t0:t0 + rows], bk[:, 0:nk * rows].rearrange("p (k n) -> p k n", k=nk)))
            dve.wait_ge(small_landed, 16 * 9)
            step.inc(V.tensor_tensor(lprod[:, :, 0, :], lraw[:, :, 0, :], lraw[:, :, 1, :], ALU.mult))
            step.done(V.tensor_tensor(lprod[:, :, 1, :], lraw[:, :, 2, :], lraw[:, :, 3, :], ALU.mult))
            V.reduce_sum(lamt[:], lprod, AX.X).then_inc(lam_dots, 1)
            step.inc(V.memset(dtb[:], 0.0))
            step.done(V.memset(An[:], 0.0))
            dve.wait_ge(setup_exps, 2)
            for l in range(L):
                for q in range(3):
                    step.inc(V.tensor_copy(dtb[:, l, 8 * q:8 * q + 8], raw8[:, 0, l, :]))
                    step.inc(V.tensor_scalar(An[:, l, 8 * q:8 * q + 8], raw8[:, 1, l, :], -1.0, None, ALU.mult))
                step.inc(V.tensor_copy(dtb[0:8, l, 24:32], col8[:, 0, l:l + 1].to_broadcast([8, 8])))
                step.inc(V.tensor_scalar(An[0:8, l, 24:32], col8[:, 1, l:l + 1].to_broadcast([8, 8]), -1.0, None,
                                         ALU.mult))
                step.done(V.tensor_tensor(nlam[:, l:l + 1], lamt[:, l, 1:2], lamt[:, l, 0:1], ALU.subtract))
                step.inc(V.tensor_scalar(nlam[:, l:l + 1], nlam[:, l:l + 1], -LAM_INIT[l], None, ALU.add))
                ins = V.tensor_scalar(col_attn(l), col_attn(l), 1.0 - LAM_INIT[l], None, ALU.mult)
                if l == 0:
                    step.inc(ins)
            ins.then_inc(vectors_ready, 1)
            dve.wait_ge(vectors_ready, 1)
            dve.wait_ge(buffers_set, 5)

            for l in range(L):
                bk = take(dve, (l, "dt"))
                step.inc(V.tensor_tensor(dtr[:, 0:16], bk[:, 0:16], dtb[:, l, 0:16], ALU.add))
                emptied_after((l, "dt"), V.tensor_tensor(dtr[0:8, 16:32], bk[0:8, 16:32], dtb[0:8, l, 16:32],
                                                         ALU.add))
                copied(dve, (l, "dt"))
                V.scalar_tensor_tensor(dte, dtr, -1.0, dtr, ALU.mult, ALU.max).then_inc(dt_abs.sem, 1)

                dt_exp.wait(dve, l)
                V.tensor_scalar(dte, dte, 1.0, None, ALU.add).then_inc(dt_exp1.sem, 1)
                dt_ln.wait(dve, l)
                step.done(V.scalar_tensor_tensor(dtv, dtr, 0.0, dte, ALU.max, ALU.add))
                V.tensor_tensor(da, dtv, An[:, l, :], ALU.mult).then_inc(da_ready.sem, 1)
                bk = take(dve, (l, "acs"))
                step.inc(V.tensor_copy(sc[:, 0:16], bk[:, 0:16]))
                step.done(V.tensor_copy(sc[:, 32:48], bk[:, 16:32]))
                emptied_after((l, "acs"), V.tensor_tensor(sc[:, 16:32], bk[:, 16:32], sc[:, 0:16], ALU.subtract))
                da_ready.wait(dve, l)
                V.tensor_copy(sc[0:8, 48:56], da[0:8, 24:32]).then_inc(decays_in.sem, 1)
                bk = take(dve, (l, "scT"))
                emptied_after((l, "scT"), V.tensor_copy(
                    win[:, :, 0:3, :], bk[:, 0:192].rearrange("p (m b i) -> p m i b", m=8, b=8)))
                decays_out.wait(dve, l)
                V.tensor_tensor(xwsc, dtv[:, 0:16], ex[:, 16:32], ALU.mult).then_inc(xwsc_ready.sem, 1)

                def conv_input(m):
                    bk = take(dve, (l, "xbc", m))
                    step.inc(V.tensor_copy(xpad[:, m, 3:259], bk[:, 0:NP_TOK]))
                    step.inc(V.tensor_copy(win[:, m, 3, :], bk[:, NP_TOK:T]))
                    emptied_after((l, "xbc", m), V.tensor_copy(ct11[:, m, :], bk[:, NP_TOK - 3:T]))

                def later_taps(m):
                    tap0_done.wait(dve, l, m)
                    for i in range(1, CW):
                        ins = V.scalar_tensor_tensor(convT[:, m, 0:NP_TOK], xpad[:, m, i:i + NP_TOK],
                                                     col_cw(l, i, m), convT[:, m, 0:NP_TOK], ALU.mult, ALU.add)
                        if i < CW - 1:
                            step.done(ins)
                    ins.then_inc(taps_done.sem, 1)

                def cached_scores(b):
                    bk = take(dve, (l, "qb", b))
                    s = rg.arrived(dve, (l, "K", b // 4))
                    Kb = ring[:, s, :].rearrange("p (b g n) -> p b g n", b=4, g=2)[:, b % 4]
                    tb = tmp.rearrange("p (g n) -> p g n", g=2)
                    emptied_after((l, "qb", b), V.tensor_tensor(tb, Kb, bc(bk[:], [P, 2, 512], 1), ALU.mult))
                    copied(dve, (l, "qb", b))
                    step.inc(V.reduce_sum(sS[:, :, b, :], tmp.rearrange("p (g h d) -> p g h d", g=2, h=8), AX.X))

                for m in range(8):
                    conv_input(m)
                    dve.wait_ge(dve_steps, step.n)
                    cached_scores(m)
                    if m == 0:
                        bk = take(dve, (l, "dtb"))
                        emptied_after((l, "dtb"), V.tensor_copy(dcol.rearrange("p j c -> p (j c)"), bk[:, 0:64]))
                    else:
                        later_taps(m - 1)
                later_taps(7)
                dve.wait_ge(dve_steps, step.n)
                taps = vecT[:, 1, 32 * l:32 * l + 32].rearrange("p (i m) -> p m i", i=CW)
                w4 = wtmp.rearrange("p (m i b) -> p m i b", m=8, i=CW)
                copied(dve, (l, "scT"))
                step.done(V.tensor_tensor(w4, win, bc(taps, [P, 8, CW, 8], 3), ALU.mult))
                step.done(V.reduce_sum(convT[:, :, NP_TOK:T], w4.rearrange("p m i b -> p m b i"), AX.X))
                V.tensor_tensor(convT[:, :, NP_TOK:T], convT[:, :, NP_TOK:T],
                                bc(cols_cb(l, 0, 8), [P, 8, 8], 2), ALU.add).then_inc(taps_done.sem, 1)
                step.done(V.tensor_tensor(tmp[0:8, 0:512], qkr[0:8, 2, 0:512], qkr[0:8, 2, 512:1024], ALU.mult))
                step.done(V.reduce_sum(ss[0:8], tmp[0:8, 0:512].rearrange("p (h d) -> p h d", h=8), AX.X))
                V.tensor_tensor(sbt[0:8, :].rearrange("p (b h) -> p b h", b=8),
                                const[0:8, C_REQT:C_REQT + 64].rearrange("p (b h) -> p b h", b=8),
                                bc(ss[0:8], [8, 8, 8], 1), ALU.mult).then_inc(dec_scores.sem, 1)
                bk = take(dve, (l, "sST"))
                emptied_after((l, "sST"), V.tensor_copy(pSx, bk[0:64, 0:257]))
                copied(dve, (l, "sST"))
                step.done(V.reduce_max(mx1[0:64], pSx, AX.X))
                V.tensor_scalar(nb1[0:64], mx1[0:64], -DQ ** -0.5, None, ALU.mult).then_inc(dec_rows.sem, 1)

                def decode_probabilities():
                    dec_exp.wait(dve, l)
                    step.done(V.reciprocal(rr1[0:64], rs1[0:64]))
                    step.done(V.tensor_scalar(pSx, pSx, rr1[0:64], None, ALU.mult))
                    V.tensor_scalar(pself_r[:], const[0:64, C_HEAD:C_HEAD + 8], pSx[:, 256:257], None, ALU.mult
                                    ).then_inc(dec_probs.sem, 1)
                    bk = take(dve, (l, "pT"))
                    pv = bk[:, 0:128].rearrange("p (g b h m) -> p g b h m", g=2, b=8, h=AH)
                    dst = aTs.rearrange("p g b h -> p (g b h)")
                    pf = bk[:, 0:128].rearrange("p (c m) -> p c m", m=2)
                    step.done(V.tensor_scalar(dst, pf[:, :, 1], nlam[:, l:l + 1], None, ALU.mult))
                    emptied_after((l, "pT"), V.tensor_tensor(dst, dst, pf[:, :, 0], ALU.add))
                    bk = take(dve, (l, "pself"))
                    pf = bk[0:8, 0:8].rearrange("p (c m) -> p c m", m=2)
                    step.done(V.tensor_scalar(as4[0:8], pf[:, :, 1], nlam[0:8, l:l + 1], None, ALU.mult))
                    emptied_after((l, "pself"), V.tensor_tensor(as4[0:8], as4[0:8], pf[:, :, 0], ALU.add))

                conv_ready.wait(dve, l, 8)
                step.done(V.tensor_tensor(dtx, dcol[:, :, 0:8], convT[:, 0:4, NP_TOK:T], ALU.mult))
                s = rg.arrived(dve, (l, "state"))
                for b in range(8):
                    if b == 2:
                        decode_probabilities()
                    state_decayed.wait(dve, l, b)
                    bk = take(dve, (l, "BC", b))
                    Sb = ring[:, s, 512 * b:512 * (b + 1)].rearrange("p (g r n) -> p g r n", g=2, r=2)
                    tb = tmp[:, 0:512].rearrange("p (g r n) -> p g r n", g=2, r=2)

                    def on_heads(q):
                        return bc(bk[:, 256 * q:256 * (q + 1)].rearrange("p (g n) -> p g n", g=2), [P, 2, 2, SN], 2)

                    xb = bc(dtx[:, :, b].rearrange("p (g r) -> p g r", g=2), [P, 2, 2, SN], 3)
                    step.done(V.tensor_tensor(tb, on_heads(0), xb, ALU.mult))
                    step.done(V.tensor_tensor(Sb, Sb, tb, ALU.add))
                    emptied_after((l, "BC", b), V.tensor_tensor(tb, Sb, on_heads(1), ALU.mult))
                    copied(dve, (l, "BC", b))
                    ins = V.reduce_sum(ysT[:, :, b], tmp[:, 0:512].rearrange("p (j n) -> p j n", j=4), AX.X)
                    if b < 7:
                        step.done(ins)
                ins.then_inc(ysT_ready.sem, 1)
                bk = take(dve, (l, "st", 0))
                emptied_after((l, "st", 0), V.tensor_copy(ST0, bk[:]))
                bk = take(dve, (l, "st", 1))
                copied(dve, (l, "st", 0))
                step.done(V.tensor_tensor(STf.rearrange("p (h d) -> p h d", h=SH),
                                          ST0.rearrange("p (h d) -> p h d", h=SH),
                                          bc(ex[:, 40:48], [P, SH, SP_], 2), ALU.mult))
                emptied_after((l, "st", 1), V.tensor_tensor(STf, STf, bk[:], ALU.add))
                for c in range(2):
                    for g in range(SG):
                        bk = take(dve, (l, "ab", c, g))
                        emptied_after((l, "ab", c, g), V.tensor_tensor(
                            Mdec[:, g], bk[:].rearrange("p (r n) -> p r n", r=4),
                            bc(sc[:, 8 * c + 4 * g:8 * c + 4 * g + 4], [P, 4, P], 2), ALU.subtract))
                        copied(dve, (l, "ab", c, g))
                        V.tensor_tensor(Mdec[:, g], Mdec[:, g], bc(negm, [P, 4, P], 1), ALU.add
                                        ).then_inc(seg_ready.sem, 1)
                    bk = take(dve, (l, "cb", c))
                    for g in range(SG):
                        decay_ready.wait(dve, l, 2 * c + g)
                        ins = V.tensor_tensor(Mdec[:, g], Mdec[:, g], bc(bk[:, g * P:(g + 1) * P], [P, 4, P], 1),
                                              ALU.mult)
                        if g == 0:
                            step.inc(ins)
                    emptied_after((l, "cb", c), ins)
                    bk = take(dve, (l, "y", c))
                    xskip_ready.wait(dve, l, c)
                    emptied_after((l, "y", c), V.tensor_tensor(mix[:, c, 512:1024], mix[:, c, 512:1024], bk[:],
                                                               ALU.add))
                bk = take(dve, (l, "yo"))
                emptied_after((l, "yo"), V.tensor_tensor(
                    tmp[:, 0:512].rearrange("p (h d) -> p h d", h=SH), bk[:].rearrange("p (h d) -> p h d", h=SH),
                    bc(ex[:, 8:16], [P, SH, SP_], 2), ALU.mult))
                copied(dve, (l, "yo"))
                step.done(V.tensor_tensor(mix[:, 1, 512:1024], mix[:, 1, 512:1024], tmp[:, 0:512], ALU.add))
                copied(dve, (l, "tok", "z", 2))
                for c in range(2):
                    step.inc(V.tensor_tensor(mix[:, c, 512:1024], mix[:, c, 512:1024], vz[:, c, 512:1024],
                                             ALU.mult))
                bk = take(dve, (l, "ysT"))
                xskip_ready.wait(dve, l, 2)
                emptied_after((l, "ysT"), V.tensor_tensor(mix[0:8, 2, 512:1024], mix[0:8, 2, 512:1024],
                                                          bk[0:8, :], ALU.add))
                copied(dve, (l, "ysT"))
                step.inc(V.tensor_tensor(mix[0:8, 2, 512:1024], mix[0:8, 2, 512:1024], vz[0:8, 2, 512:1024],
                                         ALU.mult))
                for qt in range(2):
                    nk = (qt + 1) * P
                    if qt:
                        passed(dve, (l, "aT", 0, 0))
                    for n in range(4):
                        hp, m = n // 2, n % 2
                        bk = take(dve, (l, "S", qt, hp, m))
                        sv = bk[:, 0:2 * nk].rearrange("p (j k) -> p j k", j=2)
                        pv = probs[:, 2 * hp:2 * hp + 2, m, :]
                        if qt:
                            step.inc(V.tensor_copy(pv[:, :, 0:P], sv[:, :, 0:P]))
                        emptied_after((l, "S", qt, hp, m), V.tensor_tensor(
                            pv[:, :, nk - P:nk], sv[:, :, nk - P:nk], bc(cmask, [P, 2, P], 1), ALU.add))
                        copied(dve, (l, "S", qt, hp, m))
                        mv_ = mx.rearrange("p (h m) -> p h m", m=2)[:, 2 * hp:2 * hp + 2, m]
                        nv = nb.rearrange("p (h m) -> p h m", m=2)[:, 2 * hp:2 * hp + 2, m]
                        step.done(V.reduce_max(mv_, pv[:, :, 0:nk], AX.X))
                        V.tensor_scalar(nv, mv_, -DQ ** -0.5, None, ALU.mult).then_inc(max_ready.sem, 1)
                    probs_ready.wait(dve, l, 4 * qt + 3)
                    step.done(V.reciprocal(rr, rs))
                    r2 = rr.rearrange("p (h m) -> p h m", m=2)[:, :, 1]
                    step.done(V.tensor_scalar(r2, r2, nlam[:, l:l + 1], None, ALU.mult))
                    for h in range(AH):
                        step.inc(V.tensor_scalar(probs[:, h, 0, 0:nk], probs[:, h, 0, 0:nk],
                                                 rr[:, 2 * h:2 * h + 1], None, ALU.mult))
                    first = step.n - AH
                    for h in range(AH):
                        dve.wait_ge(dve_steps, first + h + 1)
                        ins = V.scalar_tensor_tensor(probs[:, h, 0, 0:nk], probs[:, h, 1, 0:nk],
                                                     rr[:, 2 * h + 1:2 * h + 2], probs[:, h, 0, 0:nk],
                                                     ALU.mult, ALU.add)
                        if h < AH - 1:
                            step.inc(ins)
                    ins.then_inc(a_ready.sem, 1)
                def rms(t):
                    n = TILES[t][1]
                    step.done(V.tensor_tensor(tmp[0:n], mix[0:n, t, :], mix[0:n, t, :], ALU.mult))
                    step.inc(V.reduce_sum(ms[0:n, 0:4], tmp[0:n, 0:512].rearrange("p (h d) -> p h d", h=4), AX.X))
                    step.done(V.reduce_sum(ms[0:n, 4:6], tmp[0:n, 512:1024].rearrange("p (h d) -> p h d", h=2),
                                           AX.X))
                    step.inc(V.tensor_scalar(ms[0:n, 0:4], ms[0:n, 0:4], 1.0 / DV, EPS, ALU.mult, ALU.add))
                    V.tensor_scalar(ms[0:n, 4:6], ms[0:n, 4:6], 1.0 / 256, EPS, ALU.mult, ALU.add
                                    ).then_inc(ms_ready.sem, 1)
                    rstd_ready.wait(dve, l, NORM_ORDER.index(t))
                    for o, h in ((0, 4), (512, 2)):
                        v = mix[0:n, t, o:o + 512].rearrange("p (h d) -> p h d", h=h)
                        ins = V.tensor_tensor(v, v, bc(rstd6[0:n, (0 if h == 4 else 4):(4 if h == 4 else 6)],
                                                       [n, h, 512 // h], 2), ALU.mult)
                        if h == 4:
                            step.inc(ins)
                    ins.then_inc(mix_ready.sem, 1)

                bk = take(dve, (l, "O", 0))
                emptied_after((l, "O", 0), V.tensor_copy(mix[:, 0, 0:512], bk[:]))
                copied(dve, (l, "O", 0))
                rms(0)
                bk = take(dve, (l, "oS"))
                emptied_after((l, "oS"), V.tensor_copy(attS, bk[:, 0:32]))
                own = mix[0:8, 2, 0:512]
                copied(dve, (l, "pself"))
                step.done(V.tensor_tensor(own.rearrange("p (h d) -> p h d", h=AH),
                                          vz[0:8, 2, 0:512].rearrange("p (h d) -> p h d", h=AH),
                                          bc(as4[0:8], [8, AH, DV], 2), ALU.mult))
                bk = take(dve, (l, "oSt"))
                emptied_after((l, "oSt"), V.tensor_tensor(own, own, bk[0:8, :], ALU.add))
                copied(dve, (l, "oSt"))
                rms(2)
                bk = take(dve, (l, "O", 1))
                emptied_after((l, "O", 1), V.tensor_copy(mix[:, 1, 0:512], bk[:]))
                copied(dve, (l, "O", 1))
                rms(1)
                dve.wait_ge(stored, 16 * STORES_LAYER * (l + 1))
                for n in range(5):
                    t, bk = n // 2, take(dve, (l, "mixT", n))
                    t0, rows = TILES[t]
                    for half in ((0, 1) if t == 2 else (n % 2,)):
                        src = bk[:, (4 * rows * half if t == 2 else 0):][:, 0:4 * rows]
                        src = src.rearrange("p (k n) -> p k n", k=4)
                        dst = mixT[:, 4 * half:4 * half + 4, t0:t0 + rows]
                        if half:
                            ins = V.tensor_tensor(dst, src, bc(cols_ssm(l), [P, 4, rows], 2), ALU.mult)
                        else:
                            ins = V.tensor_scalar(dst, src, col_attn(l), None, ALU.mult)
                        if t == 2 and half == 0:
                            step.inc(ins)
                    emptied_after((l, "mixT", n), ins)
                for m in range(8):
                    residual(l, "m", m)
                norm(l, 0, "m")
                for t in range(2):
                    for hp in range(2):
                        q = 2 * t + hp
                        bk = take(dve, (l, "cS", t, hp))
                        step.done(V.reduce_max(mx[:, 2 * q:2 * q + 2],
                                               bk[:].rearrange("p (j k) -> p j k", j=2), AX.X))
                        V.tensor_scalar(nb[:, 2 * q:2 * q + 2], mx[:, 2 * q:2 * q + 2], -MD ** -0.5, None, ALU.mult
                                        ).then_inc(cmax_ready.sem, 1)
                for t in range(2):
                    copied(dve, (l, "cS", t, 1))
                    step.done(V.reciprocal(rr[:, 4 * t:4 * t + 4], rs[:, 4 * t:4 * t + 4]))
                    for h in range(MH):
                        ins = V.tensor_scalar(cP[:, t, h, :], cP[:, t, h, :], rr[:, 4 * t + h:4 * t + h + 1], None,
                                              ALU.mult)
                        if h < MH - 1:
                            step.inc(ins)
                    ins.then_inc(cP_ready.sem, 1)
                for i in range(2):
                    bk = take(dve, (l, "qsT", i))
                    emptied_after((l, "qsT", i), V.tensor_copy(qs[0:8, 512 * i:512 * (i + 1)], bk[0:8, :]))
                for b in range(8):
                    s = rg.arrived(dve, (l, "mK", b // 2))
                    Kb = ring[:, s, :].rearrange("p (b t n) -> p b t n", b=2, t=2)[:, b % 2]
                    for i in range(2):
                        bk = take(dve, (l, "qsb", b, i))
                        emptied_after((l, "qsb", b, i), V.tensor_tensor(
                            ctmp.rearrange("p (t n) -> p t n", t=2), Kb[:, :, 512 * i:512 * (i + 1)],
                            bc(bk[:], [P, 2, 512], 1), ALU.mult))
                        copied(dve, (l, "qsb", b, i))
                        ins = V.reduce_sum(sC[:, :, b, 2 * i:2 * i + 2],
                                           ctmp.rearrange("p (t h d) -> p t h d", t=2, h=2), AX.X)
                        if b < 7 or i < 1:
                            step.done(ins)
                ins.then_inc(cs_scores.sem, 1)
                bk = take(dve, (l, "sCT"))
                emptied_after((l, "sCT"), V.tensor_copy(sP[0:32], bk[0:32, 0:256]))
                copied(dve, (l, "sCT"))
                step.done(V.reduce_max(mx1[0:32], sP[0:32], AX.X))
                V.tensor_scalar(nb1[0:32], mx1[0:32], -MD ** -0.5, None, ALU.mult).then_inc(cs_rows.sem, 1)
                cs_exp.wait(dve, l)
                step.done(V.reciprocal(rr1[0:32], rs1[0:32]))
                V.tensor_scalar(sP[0:32], sP[0:32], rr1[0:32], None, ALU.mult).then_inc(cs_probs.sem, 1)
                bk = take(dve, (l, "sPT"))
                emptied_after((l, "sPT"), V.tensor_copy(sPTs.rearrange("p t c -> p (t c)"), bk[:, 0:64]))
                bk = take(dve, (l, "soT"))
                emptied_after((l, "soT"), V.tensor_copy(oT[:, :, NP_TOK:T],
                                                        bk[:, 0:64].rearrange("p (m b) -> p m b", m=8)))
                for m in range(8):
                    residual(l, "co", m)
                norm(l, 1, "co")
                if l == 0:
                    for f in range(NGU):
                        for s in range(2):
                            bk = take(dve, (l, "u", f, s))
                            copied(dve, (l, "g", f, s))
                            emptied_after((l, "u", f, s), V.tensor_tensor(hT[:, 2 * f + s, :], sgd[:, s, :],
                                                                          bk[:, 0:T], ALU.mult))
                    for m in range(8):
                        residual(l, "d", m)
                    norm(l, 2, "d")
                else:
                    route(l, dve, step)
                    expert_elementwise(dve)
                    dve.wait_ge(part_added, parts_added(EXPERTS, 0))
                    V.scalar_tensor_tensor(R[:], xT[:], ALPHA, acc, ALU.mult, ALU.add).then_inc(moe_done, 1)
                    dve.wait_ge(moe_done, 1)
                    norm(l, 2, None)



_INS = ['x_prompt', 'x_sample', 'cache_attn_k', 'cache_attn_v', 'cache_mem_k', 'cache_mem_v', 'state_conv',
        'state_ssm', 'page_table', 'mem_prompt', 'ln_g', 'ln_b', 'w_in', 'conv_w', 'conv_b', 'dt_bias', 'a_log',
        'd_skip', 'ssm_norm_w', 'lambda_params', 'attn_norm_w', 'w_out', 'w_cq', 'w_ckv', 'w_co', 'w_ffn_gu',
        'w_ffn_down', 'w_router', 'w_exp_gu', 'w_exp_down']
_OUTS = [(1, 256, 1024), (8, 1, 1024), (2, 1, 256, 8, 64), (2, 1, 256, 4, 128), (2, 1, 256, 4, 256),
         (2, 1, 256, 4, 256), (2, 1, 3, 1024), (2, 1, 8, 64, 128), (2, 8, 1, 8, 64), (2, 8, 1, 4, 128),
         (2, 8, 3, 1024), (2, 8, 8, 64, 128)]


def kernel(**inputs):
    import concourse.bacc as _bacc
    from concourse.bass_utils import run_bass_kernel_spmd as _run

    nc = _bacc.Bacc("TRN2", target_bir_lowering=False, num_devices=1)
    arrays, args = {}, {}
    for name in _INS + ["consts"]:
        x = constants() if name == "consts" else np.ascontiguousarray(inputs[name])
        arrays[f"in_{name}"] = x
        args[name] = nc.dram_tensor(f"in_{name}", x.shape, mybir.dt.from_np(x.dtype), kind="ExternalInput").ap()
    outs = [nc.dram_tensor(f"out_{i}", shape, F32, kind="ExternalOutput").ap() for i, shape in enumerate(_OUTS)]
    build(nc, args, outs)
    r = _run(nc, [arrays], core_ids=[0])
    return tuple(r.results[0][f"out_{i}"] for i in range(len(_OUTS)))
```

```python
import math
from contextlib import ExitStack

import numpy as np
import concourse.bass as bass
from concourse import mybir

F32 = mybir.dt.float32
F32R = mybir.dt.float32r
I32 = mybir.dt.int32
ALU = mybir.AluOpType
ACT = mybir.ActivationFunctionType
AX = mybir.AxisListType

P = 128
D = 1024
KT = D // P
L = 2
NP_TOK = 256
NS_TOK = 8
T = NP_TOK + NS_TOK
DECODE_FIRST = (2, 0, 1)
NORM_ORDER = (0, 2, 1)
TILES = [(0, P), (P, P), (2 * P, NS_TOK)]
AH, DQ, DV = 4, 64, 128
SH, SP_, SN, SG = 8, 64, 128, 2
CW = 4
MH, MD = 4, 256
PAGES = 2
N_PHYS = 20
FF = 2816
FT = FF // P
GU = 256
NGU = FF // GU
NDN = 6
EXPERTS = 8
SLOTS = 128
ALPHA = (2 * L) ** 0.25
EPS = 1e-5
NEG = -1e30
RING = 6
SLOT = 4096
EPOS = NGU + NDN + 1
HALVES = 2 * (NGU + NDN) - 1
HIGH_BUFS = 3
HALF = SLOT // 2
assert EPOS % RING == 0 and HALVES % HIGH_BUFS == 0
LAM_INIT = [0.8 - 0.6 * math.exp(-0.3 * l) for l in range(L)]

C_ID, C_U, C_US, C_NEG, C_CM, C_IOTA = (P * i for i in range(6))
C_COS = 6 * P
C_SIN = C_COS + 3 * 32
C_REQ = C_SIN + 3 * 32
C_HEAD = C_REQ + 8
C_REQT = C_HEAD + 8
C_TRI = C_REQT + 64
C_R32 = C_TRI + 64
C_H32 = C_R32 + 8
C_EPS = C_H32 + 4
NCONST = C_EPS + 1


def constants():
    c = np.zeros((P, NCONST), np.float32)
    i = np.arange(P)
    c[:, C_ID:C_ID + P] = np.eye(P)
    c[:, C_U:C_U + P] = i[:, None] <= i[None, :]
    c[:, C_US:C_US + P] = i[:, None] < i[None, :]
    c[:, C_NEG:C_NEG + P] = np.where(i[None, :] >= i[:, None], 0, NEG)
    c[:, C_CM:C_CM + P] = np.where(i[None, :] <= i[:, None], 0, NEG)
    c[:, C_IOTA:C_IOTA + P] = i[None, :]
    inv = np.float32(10000.0) ** (-np.arange(0, DQ, 2, dtype=np.float32) / np.float32(DQ))
    for t in range(3):
        pos = (t * P + i if t < 2 else np.full(P, NP_TOK)).astype(np.float32)
        ang = (pos[:, None] * inv[None, :]).astype(np.float32)
        c[:, C_COS + 32 * t:C_COS + 32 * t + 32] = np.cos(ang)
        c[:, C_SIN + 32 * t:C_SIN + 32 * t + 32] = np.sin(ang)
    r = np.arange(64)
    c[:64, C_REQ:C_REQ + 8] = (r[:, None] // 8) == np.arange(8)[None, :]
    c[:64, C_HEAD:C_HEAD + 8] = (r[:, None] % 8) == np.arange(8)[None, :]
    c[:8, C_REQT:C_REQT + 64] = c[:64, C_REQ:C_REQ + 8].T
    c[:32, C_R32:C_R32 + 8] = (r[:32, None] // 4) == np.arange(8)[None, :]
    c[:32, C_H32:C_H32 + 4] = (r[:32, None] % 4) == np.arange(4)[None, :]
    c[:, C_EPS] = EPS
    e = np.arange(8)
    c[:, C_TRI:C_TRI + 64] = (e[None, :] < e[:, None]).astype(np.float32).reshape(1, 64)
    return c


class Signal:

    def __init__(self, sem, per_layer):
        self.sem, self.per = sem, per_layer

    def value(self, l, i=0):
        assert i < self.per
        return l * self.per + i + 1

    def wait(self, eng, l, i=0):
        eng.wait_ge(self.sem, self.value(l, i))


class Steps:

    def __init__(self, eng, sem):
        self.eng, self.sem, self.n = eng, sem, 0

    def inc(self, ins):
        ins.then_inc(self.sem, 1)
        self.n += 1

    def done(self, ins):
        self.inc(ins)
        self.eng.wait_ge(self.sem, self.n)


class PsumTurns:

    def __init__(self, groups, banks, full, emptied):
        self.groups, self.banks, self.full, self.emptied = groups, banks, full, emptied
        self.index = {g: n for n, (g, _) in enumerate(groups)}
        seen = {k: 0 for k in emptied}
        self.rank = []
        for _, by in groups:
            seen[by] += 1
            self.rank.append(seen[by])
        self.opened = 0
        self.closed = {k: 0 for k in emptied}

    def open(self, pe, name):
        n = self.index[name]
        assert n == self.opened, (name, self.groups[self.opened])
        self.opened += 1
        if n >= len(self.banks):
            by = self.groups[n - len(self.banks)][1]
            pe.wait_ge(self.emptied[by], self.rank[n - len(self.banks)])
        return self.banks[n % len(self.banks)]

    def take(self, eng, name):
        n = self.index[name]
        eng.wait_ge(self.full, n + 1)
        return self.banks[n % len(self.banks)]

    def passed(self, eng, name):
        eng.wait_ge(self.full, self.index[name] + 1)

    def copied(self, eng, name):
        n = self.index[name]
        eng.wait_ge(self.emptied[self.groups[n][1]], self.rank[n])

    def emptied_after(self, name, ins):
        n = self.index[name]
        by = self.groups[n][1]
        self.closed[by] += 1
        assert self.closed[by] == self.rank[n], name
        ins.then_inc(self.emptied[by], 1)


def psum_groups():
    g = [(("vec",), "V")]
    g += [(("xin", n), "V") for n in range(5)] + [(("mem", n), "A") for n in range(4)]
    for l in range(L):
        def add(by, *name):
            g.append(((l,) + name, by))

        for c in ("q", "k"):
            for t in DECODE_FIRST:
                add("A", "tok", c, t)
                if c == "q" and t == DECODE_FIRST[0]:
                    add("V", "dt")
        add("V", "acs")
        add("V", "scT")
        for m in range(8):
            add("V", "xbc", m)
            add("V", "qb", m)
            if m == 0:
                add("V", "dtb")
        for t in range(3):
            add("A", "tok", "v", t)
            if t == 0:
                add("V", "sST")
        for t in range(3):
            add("A", "xt", t)
            add("A", "Bt", t)
        add("A", "cp", 0)
        add("A", "cp", 1)
        for i in range(4):
            add("V", "BC", 2 * i)
            add("V", "BC", 2 * i + 1)
            if i < 3:
                add("A", "tok", "z", i)
            if i == 0:
                add("V", "pT")
                add("V", "pself")
        add("A", "mkv", 0)
        add("V", "st", 0)
        add("V", "st", 1)
        for c in range(2):
            add("V", "ab", c, 0)
            add("V", "ab", c, 1)
            add("V", "cb", c)
            add("A", "mkv", 1 + c)
            add("V", "y", c)
        add("V", "yo")
        add("A", "stT")
        add("V", "ysT")
        for i in range(4):
            add("A", "qkT", i)
        for qt in range(2):
            for hp in range(2):
                for m in range(2):
                    add("V", "S", qt, hp, m)
            add("A", "mkv", 3 + qt)
        add("A", "aT", 0, 0)
        add("V", "O", 0)
        add("A", "mkv", 5)
        add("V", "oS")
        add("A", "mkv", 6)
        add("V", "oSt")
        add("A", "aT", 1, 0)
        add("A", "aT", 1, 1)
        add("V", "O", 1)
        add("A", "mkv", 7)
        for n in range(5):
            add("V", "mixT", n)
        for m in range(8):
            add("V", "m", m)
        for i in range(4):
            add("A", "mkT", i)
        add("V", "mu", 0)
        add("A", "var", 0)
        for m in range(4):
            add("A", "cq", m)
        for n in range(4):
            add("A", "cq", 4 + n)
            if n == 0:
                add("V", "qsT", 0)
            add("V", "qsb", 2 * n, 0)
            add("V", "qsb", 2 * n + 1, 0)
        for n in range(4):
            add("A", "cS", n // 2, n % 2)
            if n == 0:
                add("V", "qsT", 1)
            add("V", "qsb", 2 * n, 1)
            add("V", "qsb", 2 * n + 1, 1)
        for t in range(2):
            for kt in range(2):
                add("A", "cPT", t, kt)
        add("V", "sCT")
        for i in range(4):
            add("A", "cO", i)
        for n in (("sPT",), ("oV", 0), ("oV", 1), ("soT",)):
            add("V", *n)
        for m in range(8):
            add("V", "co", m)
        add("V", "mu", 1)
        add("A", "var", 1)
        if l == 0:
            for f in range(NGU):
                for s in range(2):
                    add("A", "g", f, s)
                    add("V", "u", f, s)
            for m in range(8):
                add("V", "d", m)
        else:
            for n in range(6):
                add("A", "xtok", n)
            add("V", "lg")
            add("V", "pos")
        add("V", "mu", 2)
        add("A", "var", 2)
    for n in range(6):
        g.append((("out", n), "A"))
    return g


def ring_chunks():
    c = [(("x",), 2, "pe", ("xin", 4)), (("mem",), 1, "pe", ("mem", 3))]
    for l in range(L):
        c += [((l, n), 1, "pe", (l, "tok", n, DECODE_FIRST[-1])) for n in ("q", "k")]
        c += [((l, "xbc0"), 1, "pe", (l, "xbc", 3)), ((l, "xbc1"), 1, "pe", (l, "xbc", 7))]
        c += [((l, "K", i), 8, "v", (l, "qb", 4 * i + 3)) for i in range(2)]
        c += [((l, n), 1, "pe", (l, "tok", n, 2)) for n in ("v", "z")]
        c += [((l, "state"), 1, "st", l)]
        c += [((l, "ckv", i), 1, "pe", (l, "mkv", 2 * i + 1)) for i in range(3)]
        c += [((l, "V", i), 8, "pe", (l, "oS")) for i in range(2)]
        c += [((l, "ckv", 3), 1, "pe", (l, "mkv", 7))]
        c += [((l, "out", i), 1, "pe", (l, "m", 4 * i + 3)) for i in range(2)]
        c += [((l, "cq", i), 1, "pe", (l, "cq", 4 * i + 3)) for i in range(2)]
        mem = [((l, "mK", i), 2, "v", (l, "qsb", 2 * i + 1, 1)) for i in range(4)]
        c += mem[:1] + [((l, "mkv"), 2, "pe", (l, "cO", 3))] + mem[1:]
        c += [((l, "mV", i), 2, "pe", (l, "oV", 1)) for i in range(4)]
        c += [((l, "co", i), 1, "pe", (l, "co", 4 * i + 3)) for i in range(2)]
        if l == 0:
            c += [((l, "gu", f), 2, "pe", (l, "u", f, 1)) for f in range(NGU)]
            c += [((l, "dn", i), 1, "pe", (l, "d", 4 * (i // 3) + 3)) for i in range(NDN)]
    return c


class Ring:
    def __init__(self, chunks, landed, turns, state_stored):
        self.chunks, self.landed, self.turns, self.state_stored = chunks, landed, turns, state_stored
        self.pos = {c[0]: n for n, c in enumerate(chunks)}
        per = [0] * RING
        self.value = []
        for n, (_, dmas, _, _) in enumerate(chunks):
            per[n % RING] += 16 * dmas
            self.value.append(per[n % RING])
        self.slot_total = per
        self.next = 0

    def freed(self, sp, n):
        if n < RING:
            return
        _, _, by, what = self.chunks[n - RING]
        if by == "pe":
            self.turns.passed(sp, what)
        elif by == "v":
            self.turns.copied(sp, what)
        else:
            sp.wait_ge(self.state_stored, 16 * (what + 1))

    def claim(self, sp, key):
        n = self.pos[key]
        assert n == self.next, key
        self.next += 1
        self.freed(sp, n)
        return n % RING

    def arrived(self, eng, key):
        n = self.pos[key]
        eng.wait_ge(self.landed[n % RING], self.value[n])
        return n % RING


def expert_positions(start):
    per, out = [0] * RING, []
    for p in range(EPOS - 1):
        s = (start + p) % RING
        kind, i = ("gu", p) if p < NGU else ("dn", p - NGU)
        per[s] += 16 * (2 if kind == "gu" else 1)
        out.append((kind, i, s, per[s]))
    return out, per


ARENA = 16248
STORES_LAYER = 10
NSTORES = STORES_LAYER * L + 2


def build(nc, a, outs, lots=SLOTS, always=False):
    (y_p, y_s, o_kp, o_vp, o_mk, o_mv, o_cp, o_sp, o_ks, o_vs, o_cs, o_ss) = outs
    passes = -(-T // lots)
    with ExitStack() as ctx:
        begins = {}

        def sb(name, shape, dt=F32):
            tensor = ctx.enter_context(nc.sbuf_tensor(name, shape, dt))
            begins[name] = nc.sbuf_base - 4 * math.prod(shape[1:])
            return tensor

        def parts_in(name, host, at, shape):
            return nc.alloc_sbuf_tensor_at(name, [P] + shape, F32R, offset=begins[host] + 4 * at)

        def sem(name):
            return ctx.enter_context(nc.semaphore(name))

        ring = sb("ring", [P, RING, SLOT])
        xT = sb("xT", [P, KT, T])
        R = sb("R", [P, KT, T])
        SQ = sb("SQ", [P, KT, T])
        memT = sb("memT", [P, KT, NP_TOK])
        const = sb("const", [P, NCONST])
        one_col = sb("one_col", [P, 1])
        mean_col = sb("mean_col", [P, 1])
        ones, mean_of = one_col[:].to_broadcast([P, P]), mean_col[:].to_broadcast([P, P])
        vecT = sb("vecT", [P, 2, 122])
        dtb = sb("dtb", [P, L, 32])
        An = sb("An", [P, L, 32])
        raw8 = sb("raw8", [P, 3, L, SH])
        col8 = sb("col8", [SH, 2, L])
        nlam = sb("nlam", [P, L])
        lamt = sb("lamt", [P, L, 2])
        wdt = sb("wdt", [P, L, KT, SH])
        wr = sb("wr", [P, KT, EXPERTS])
        ptab = sb("ptab", [1, NS_TOK * PAGES], I32)
        NST = 688
        st = sb("st", [P, NST])
        pself_r = sb("pself_r", [64, 8])
        stat = sb("stat", [P, T])
        own_rows = sb("own_rows", [P, 2, 8 * 36])
        gates = sb("gates", [P, 3, 9])
        posp = sb("posp", [P, 3, 9])
        sel = sb("sel", [P, 3, 8])
        lgb = sb("lgb", [P, 3, 8])
        lsm = sb("lsm", [P, 3, 8])
        l3 = sb("l3", [P, 3])
        cnt = sb("cnt", [1, 1])
        cnti = sb("cnti", [1, 1], I32)
        mem_rows = sb("mem_rows", [P, 512])
        arena = sb("arena", [P, ARENA])
        banks = [ctx.enter_context(nc.psum_tensor(f"bank{i}", [P, 512], F32)) for i in range(8)]

        used = [0]

        def carve(n, at=None):
            if at is not None:
                used[0] = at
            o = used[0]
            used[0] += n
            assert used[0] <= ARENA, used[0]
            return arena[:, o:o + n]

        vraw = carve(2 * P, 0).rearrange("p (a n) -> p a n", a=2)
        lraw = carve(L * 4 * DQ).rearrange("p (l a d) -> p l a d", l=L, a=4)
        lprod = carve(L * 2 * DQ).rearrange("p (l a d) -> p l a d", l=L, a=2)
        qk_raw = carve(3 * 1024, 0).rearrange("p (t n) -> p t n", t=3)
        mix = qk_raw
        vz = carve(3 * 1024).rearrange("p (t n) -> p t n", t=3)
        qkr = carve(3 * 1024).rearrange("p (t n) -> p t n", t=3)
        conv_at = used[0]
        xpad = carve(8 * 259).rearrange("p (m n) -> p m n", m=8)
        win = carve(8 * 32).rearrange("p (m i b) -> p m i b", m=8, i=CW)
        ct11 = carve(88).rearrange("p (m n) -> p m n", m=8)
        tmp = carve(1024)
        wtmp = tmp[:, 512:768]
        share = used[0]
        rope_t = carve(512, share)
        Mdec = carve(2 * 512, conv_at).rearrange("p (g r n) -> p g r n", g=2, r=4)
        xdt = carve(2 * 512).rearrange("p (c n) -> p c n", c=2)
        probs = carve(2048, conv_at).rearrange("p (h m k) -> p h m k", h=AH, m=2)
        xtok = carve(3 * 512, share).rearrange("p (t n) -> p t n", t=3)
        Btok = carve(512).rearrange("p (c n) -> p c n", c=2)
        xw = carve(2 * 512).rearrange("p (c n) -> p c n", c=2)
        STf = xw[:, 0, :]
        ST0 = carve(512)
        kqT = carve(8 * 256, share).rearrange("p (m n) -> p m n", m=8)
        aT = carve(3 * 512).rearrange("p (k h n) -> p k h n", k=3, h=AH)
        convT = R
        mixT = SQ
        sqf = SQ[:, :, :].rearrange("p k t -> p (k t)")
        sc_in = sqf[0:24, 0:1024]
        conv_rows = sqf[0:11, 0:1024]
        ssm_rows = sqf[:, 1024:1536].rearrange("p (j n) -> p j n", j=4)
        BCs = sqf[0:8, 1536:2048]
        pSx = sqf[0:64, 1024:1281]
        sbt = sqf[0:64, 2048:2112]
        mkT = carve(8 * 256, 0).rearrange("p (m n) -> p m n", m=8)
        qcT = carve(8 * T).rearrange("p (m n) -> p m n", m=8)
        cP = carve(2 * 1024).rearrange("p (t h k) -> p t h k", t=2, h=MH)
        cPT = carve(2 * 1024).rearrange("p (k h q) -> p k h q", k=2, h=MH)
        qs = carve(1024)
        ctmp = carve(1024)
        sP = carve(256)
        oT = SQ
        h_high = parts_in("h_high", "arena", 0, [FT, T])
        h_low = parts_in("h_low", "arena", FT * T, [FT, T])
        x_high = parts_in("x_high", "arena", 2 * FT * T, [KT, T])
        x_low = parts_in("x_low", "arena", 2 * FT * T + KT * T, [KT, T])
        h_rows = [mem_rows[:, 0:T], carve(T, 2 * (FT + KT) * T)]
        x_tok = carve(3 * 1024, 0).rearrange("p (t n) -> p t n", t=3)
        Sel = carve(3 * P).rearrange("p (t n) -> p t n", t=3)
        GSel = carve(3 * P).rearrange("p (t n) -> p t n", t=3)
        xg_high = parts_in("xg_high", "arena", used[0], [KT, P])
        xg_low = parts_in("xg_low", "arena", used[0] + KT * P, [KT, P])
        carve(2 * KT * P)
        sg = carve(2 * GU).rearrange("p (s n) -> p s n", s=2)
        hh = carve(2 * GU).rearrange("p (s n) -> p s n", s=2)
        he_high = parts_in("he_high", "arena", used[0], [FT, P])
        he_low = parts_in("he_low", "arena", used[0] + FT * P, [FT, P])
        carve(2 * FT * P)
        ye_at = used[0]
        ye = carve(1024)
        GSelT = carve(T)
        acc = carve(KT * T).rearrange("p (k n) -> p k n", k=KT)
        cmp_gt = carve(192, ye_at).rearrange("p (t e j) -> p t e j", t=3, e=8)
        cmp_eq = carve(192).rearrange("p (t e j) -> p t e j", t=3, e=8)
        high_bufs = [parts_in(f"high{n}", host, 0, [HALF]) for n, host in enumerate(("R", "SQ", "memT"))]
        ring_low = parts_in("ring_low", "ring", 0, [RING, SLOT])
        y_tok = carve(3 * 1024, 0).rearrange("p (t n) -> p t n", t=3)

        so = [0]

        def small(n):
            o = so[0]
            so[0] += n
            assert so[0] <= NST
            return st[:, o:o + n]

        dtr, dte, dtv, da = small(32), small(32), small(32), small(32)
        sc = small(56)
        ex = small(56)
        xwsc = small(16)
        dcol = small(64).rearrange("p (j c) -> p j c", j=4)
        dtx = small(32).rearrange("p (j b) -> p j b", j=4)
        ysT = small(32).rearrange("p (j b) -> p j b", j=4)
        mx, nb, rs, rr = small(8), small(8), small(8), small(8)
        sS = small(128).rearrange("p (g b h) -> p g b h", g=2, b=8)
        ms, rstd6 = small(6), small(6)
        ss, as4 = small(8), small(4)
        mx1, nb1, rs1, rr1 = small(1), small(1), small(1), small(1)
        sC = small(64).rearrange("p (t b h) -> p t b h", t=2, b=8)

        own_heads = own_rows[:].rearrange("p g (b x) -> p g b x", b=8)[:, :, :, 0:4]
        request_of = const[0:32, C_R32:C_R32 + 8]
        ident = const[:, C_ID:C_ID + P]
        upper = const[:, C_U:C_U + P]
        before = const[:, C_US:C_US + P]
        negm = const[:, C_NEG:C_NEG + P]
        cmask = const[:, C_CM:C_CM + P]
        iota = const[:, C_IOTA:C_IOTA + P]

        def col_g(l, i, k):
            o = (l * 3 + i) * 8 + k
            return vecT[:, 0, o:o + 1]

        def col_b(l, i, k):
            o = 48 + (l * 3 + i) * 8 + k
            return vecT[:, 0, o:o + 1]

        def cols_ssm(l):
            return vecT[:, 0, 96 + 4 * l:100 + 4 * l]

        def col_attn(l):
            return vecT[:, 0, 104 + l:105 + l]

        def cols_cb(l, m, n=1):
            return vecT[:, 0, 106 + 8 * l + m:106 + 8 * l + m + n]

        def col_cw(l, i, m):
            o = l * 32 + i * 8 + m
            return vecT[:, 1, o:o + 1]

        landed = [sem(f"landed{s}") for s in range(RING)]
        psum_full, emptied_by_act, emptied_by_dve = sem("psum_full"), sem("emptied_by_act"), sem("emptied_by_dve")
        const_landed, vecs_landed, small_landed, ptab_landed = (
            sem("const_landed"), sem("vecs_landed"), sem("small_landed"), sem("ptab_landed"))
        conv_state_landed, stored, state_stored = sem("conv_state_landed"), sem("stored"), sem("state_stored")
        mem_stored = sem("mem_stored")
        dve_steps, act_steps, pool_steps = sem("dve_steps"), sem("act_steps"), sem("pool_steps")
        buffers_set = sem("buffers_set")
        lam_dots, setup_exps, vectors_ready = sem("lam_dots"), sem("setup_exps"), sem("vectors_ready")

        def signal(name, per=1):
            return Signal(sem(name), per)

        dt_abs, dt_exp, dt_exp1, dt_ln, da_ready = (
            signal(n) for n in ("dt_abs", "dt_exp", "dt_exp1", "dt_ln", "da_ready"))
        tap0_done, taps_done, conv_ready = signal("tap0_done", 8), signal("taps_done", 9), signal("conv_ready", 9)
        rope_ready = signal("rope_ready", 3)
        decays_in, decays_out, xwsc_ready = signal("decays_in"), signal("decays_out"), signal("xwsc_ready")
        xdt_ready, xskip_ready = signal("xdt_ready", 2), signal("xskip_ready", 3)
        seg_ready, decay_ready = signal("seg_ready", 4), signal("decay_ready", 4)
        state_decayed, ysT_ready = signal("state_decayed", 8), signal("ysT_ready")
        max_ready, probs_ready, a_ready = signal("max_ready", 8), signal("probs_ready", 8), signal("a_ready", 2)
        dec_scores, dec_rows, dec_exp, dec_probs = (
            signal(n) for n in ("dec_scores", "dec_rows", "dec_exp", "dec_probs"))
        ms_ready, rstd_ready, mix_ready = signal("ms_ready", 3), signal("rstd_ready", 3), signal("mix_ready", 3)
        centred, squared, ln_rstd, scaled = (
            signal("centred", 9), signal("squared", 12), signal("ln_rstd", 3), signal("scaled", 24))
        sum_ready = signal("sum_ready", 2)
        xT_act, xT_dve = signal("xT_act", 21), signal("xT_dve", 3)
        cmax_ready, cP_ready = signal("cmax_ready", 4), signal("cP_ready", 2)
        cs_rows, cs_exp, cs_probs = (signal(n) for n in ("cs_rows", "cs_exp", "cs_probs"))
        lsm_ready, lexp_ready, sel_known, pos_known = (
            sem("lsm_ready"), sem("lexp_ready"), sem("sel_known"), sem("pos_known"))
        sel_ready, gu_full, sg_ready, h_ready, T_full, T_done = (
            sem("sel_ready"), sem("gu_full"), sem("sg_ready"), sem("h_ready"), sem("T_full"), sem("T_done"))
        split_high, split_low, first_half_used, T_low, xg_low_ready = (
            sem("split_high"), sem("split_low"), sem("first_half_used"), sem("T_low"), sem("xg_low_ready"))
        ffn_high, ffn_low, ffn_used = sem("ffn_high"), sem("ffn_low"), sem("ffn_used")
        x_high_ready, x_low_ready = sem("x_high_ready"), sem("x_low_ready")
        h_high_ready, h_low_ready = sem("h_high_ready"), sem("h_low_ready")
        X_full, xg_taken, part_added, dn_done, y_by_act, y_by_dve = (
            sem("X_full"), sem("xg_taken"), sem("part_added"), sem("dn_done"), sem("y_by_act"), sem("y_by_dve"))
        moe_done, pass_shift = sem("moe_done"), sem("pass_shift")

        turns = PsumTurns(psum_groups(), banks, psum_full, {"A": emptied_by_act, "V": emptied_by_dve})
        rg = Ring(ring_chunks(), landed, turns, state_stored)
        e_start = len(rg.chunks)
        epos, eper = expert_positions(e_start % RING)
        take, passed, copied, emptied_after = turns.take, turns.passed, turns.copied, turns.emptied_after

        def expert_no(e, c):
            return e + EXPERTS * c

        def transposes_before(e, c):
            return expert_no(e, c) * (NGU + 1)

        def parts_added(e, c):
            return expert_no(e, c) * KT + KT

        def x_groups_before(e, c):
            return expert_no(e, c) * (2 + KT) + 2 * (c + 1)

        block = ctx.enter_context(nc.Block())

        @block.sync
        def _(sp):
            sp.dma_start(const[:], a["consts"]).then_inc(const_landed, 16)
            for j, (src, r0) in enumerate((
                    (a["ln_g"].rearrange("l i (k n) -> (l i k) n", n=P), 0),
                    (a["ln_b"].rearrange("l i (k n) -> (l i k) n", n=P), 48),
                    (a["ssm_norm_w"].rearrange("l (k n) -> (l k) n", n=P), 96),
                    (a["attn_norm_w"], 104),
                    (a["conv_b"].rearrange("l (k n) -> (l k) n", n=P), 106))):
                sp.dma_start(vraw[r0:r0 + src.shape[0], 0, :], src).then_inc(vecs_landed, 16)
            sp.dma_start(vraw[0:64, 1, :], a["conv_w"].rearrange("l i (k n) -> (l i k) n", n=P)
                         ).then_inc(vecs_landed, 16)
            s = rg.claim(sp, ("x",))
            sp.dma_start(ring[:, s, 0:2048].rearrange("p (t n) -> p t n", t=2),
                         a["x_prompt"].rearrange("o (t p) n -> p (o t) n", p=P)).then_inc(landed[s], 16)
            sp.dma_start(ring[0:NS_TOK, s, 2048:3072], a["x_sample"].rearrange("b o n -> (b o) n")
                         ).then_inc(landed[s], 16)
            s = rg.claim(sp, ("mem",))
            sp.dma_start(ring[:, s, 0:2048].rearrange("p (t n) -> p t n", t=2),
                         a["mem_prompt"].rearrange("o (t p) n -> p (o t) n", p=P)).then_inc(landed[s], 16)
            sp.dma_start(ptab[:], a["page_table"].rearrange("b g -> (b g)").unsqueeze(0)).then_inc(ptab_landed, 16)

            def columns(key, w, c0):
                s = rg.claim(sp, key)
                sp.dma_start(ring[:, s, :].rearrange("p (k n) -> p k n", k=KT),
                             w[:, c0:c0 + 512].rearrange("(k p) n -> p k n", p=P)).then_inc(landed[s], 16)

            def pages(key, cache, b0):
                s = rg.claim(sp, key)
                for i in range(8):
                    n = b0 * PAGES + i
                    page = sp.value_load(ptab[0:1, n:n + 1], min_val=0, max_val=N_PHYS - 1)
                    sp.dma_start(ring[:, s, i * 512:(i + 1) * 512],
                                 cache[bass.ds(page, 1)].rearrange("o t h d -> (o t) (h d)")
                                 ).then_inc(landed[s], 16)

            for l in range(L):
                w_in = a["w_in"][l]
                columns((l, "q"), w_in, 0)
                if l == 0:
                    for i, n in enumerate(("dt_bias", "a_log", "d_skip")):
                        sp.dma_start(raw8[:, i], a[n].partition_broadcast(P)).then_inc(small_landed, 16)
                    with nc.allow_non_contiguous_dma(reason="sixteen words"):
                        for i, n in enumerate(("dt_bias", "a_log")):
                            sp.dma_start(col8[:, i, :], a[n].rearrange("l h -> h l")).then_inc(small_landed, 16)
                    sp.dma_start(lraw, a["lambda_params"].partition_broadcast(P)).then_inc(small_landed, 16)
                    for n in range(L):
                        sp.dma_start(wdt[:, n], a["w_in"][n, :, 3072:3080].rearrange("(k p) n -> p k n", p=P)
                                     ).then_inc(small_landed, 16)
                    sp.dma_start(wr[:], a["w_router"][0].rearrange("(k p) n -> p k n", p=P)).then_inc(small_landed, 16)
                for key, c0 in (("k", 512), ("xbc0", 2048), ("xbc1", 2560)):
                    columns((l, key), w_in, c0)
                if l == 0:
                    sp.wait_ge(ptab_landed, 16)
                for i in range(2):
                    pages((l, "K", i), a["cache_attn_k"][l], 4 * i)
                for key, c0 in (("v", 1024), ("z", 1536)):
                    columns((l, key), w_in, c0)
                s = rg.claim(sp, (l, "state"))
                sp.dma_start(ring[:, s, :].rearrange("p (j n) -> p j n", j=32),
                             a["state_ssm"][l].rearrange("b h p n -> (b h p) n").rearrange("(j p) n -> p j n", p=P)
                             ).then_inc(landed[s], 16)
                for i in range(3):
                    columns((l, "ckv", i), a["w_ckv"][l], 512 * i)
                for i in range(2):
                    pages((l, "V", i), a["cache_attn_v"][l], 4 * i)
                columns((l, "ckv", 3), a["w_ckv"][l], 512 * 3)
                for i in range(2):
                    columns((l, "out", i), a["w_out"][l], 512 * i)
                for i in range(2):
                    columns((l, "cq", i), a["w_cq"][l], 512 * i)

                def request_pair(kind, i):
                    s = rg.claim(sp, (l, kind, i))
                    for j in range(2):
                        sp.dma_start(ring[:, s, 2048 * j:2048 * (j + 1)].rearrange("p (t n) -> p t n", t=2),
                                     a[{"mK": "cache_mem_k", "mV": "cache_mem_v"}[kind]][l, 2 * i + j].rearrange(
                                         "(t p) h d -> p t (h d)", p=P)).then_inc(landed[s], 16)

                request_pair("mK", 0)
                s = rg.claim(sp, (l, "mkv"))
                sp.wait_ge(mem_stored, 16 * 8 * (l + 1))
                for i, src in enumerate((o_mk, o_mv)):
                    sp.dma_start(ring[:, s, :].rearrange("p (t n) -> p t n", t=2)[:, :, 1024 * i:1024 * (i + 1)],
                                 src[l, 0].rearrange("(t p) h d -> p t (h d)", p=P)).then_inc(landed[s], 16)
                for i in range(1, 4):
                    request_pair("mK", i)
                for i in range(4):
                    request_pair("mV", i)
                for i in range(2):
                    columns((l, "co", i), a["w_co"][l], 512 * i)
                if l == 0:
                    gu = a["w_ffn_gu"][0].rearrange("(k p) (u n) -> p k u n", p=P, u=2)
                    for f in range(NGU):
                        s = rg.claim(sp, (l, "gu", f))
                        d = ring[:, s, :].rearrange("p (k u n) -> p k u n", k=KT, u=2)
                        for u in range(2):
                            sp.dma_start(d[:, :, u, :], gu[:, :, u, f * GU:(f + 1) * GU]).then_inc(landed[s], 16)
                    dn = a["w_ffn_down"][0].rearrange("(f p) n -> p f n", p=P)
                    for i in range(NDN):
                        half, f0 = i // 3, 8 * (i % 3)
                        nf = min(8, FT - f0)
                        s = rg.claim(sp, (l, "dn", i))
                        sp.dma_start(ring[:, s, 0:nf * 512].rearrange("p (f n) -> p f n", f=nf),
                                     dn[:, f0:f0 + nf, half * 512:(half + 1) * 512]).then_inc(landed[s], 16)
            assert rg.next == e_start

            def load(e, p):
                kind, i, s, _ = epos[p]
                if kind == "gu":
                    gu = a["w_exp_gu"][0][bass.ds(e, 1)].rearrange("o (k p) (u n) -> p (o k) u n", p=P, u=2)
                    d = ring[:, s, :].rearrange("p (k u n) -> p k u n", k=KT, u=2)
                    for u in range(2):
                        sp.dma_start(d[:, :, u, :], gu[:, :, u, i * GU:(i + 1) * GU]).then_inc(landed[s], 16)
                else:
                    dn = a["w_exp_down"][0][bass.ds(e, 1)].rearrange("o (f p) n -> p (o f) n", p=P)
                    nf = min(4, FT - 4 * i)
                    sp.dma_start(ring[:, s, 0:nf * 1024].rearrange("p (f n) -> p f n", f=nf),
                                 dn[:, 4 * i:4 * i + nf, :]).then_inc(landed[s], 16)

            def expert_chunk_used(e, c, p):
                kind, i, _, _ = epos[p]
                if kind == "gu":
                    sp.wait_ge(gu_full, expert_no(e, c) * NGU + (i + 1))
                else:
                    sp.wait_ge(dn_done, expert_no(e, c) * NDN + (i + 1))

            def rest_of_expert(e, c):
                for p in range(RING, EPOS - 1):
                    expert_chunk_used(e, c, p - RING)
                    load(e, p)

            def start_of_expert(e, c):
                for p in range(RING):
                    expert_chunk_used(e - 1, c, p + 12 if p + 12 < EPOS - 1 else p + 6)
                    load(e, p)

            def stream_experts(c):
                with sp.Fori(0, EXPERTS - 1) as e:
                    rest_of_expert(e, c)
                    start_of_expert(e + 1, c)
                rest_of_expert(EXPERTS - 1, c)

            for p in range(RING):
                rg.freed(sp, e_start + p)
                load(0, p)
            stream_experts(0)
            sp.wait_ge(pos_known, 1)
            most = sp.value_load(cnti[0:1, 0:1], min_val=0, max_val=T)
            for c in range(1, passes):
                with sp.If(most > (0 if always else lots * c)):
                    for p in range(RING):
                        expert_chunk_used(EXPERTS - 1, c - 1, p + 12 if p + 12 < EPOS - 1 else p + 6)
                        load(0, p)
                    stream_experts(c)

        @block.gpsimd
        def _(pool):
            G = nc.gpsimd
            step = Steps(pool, pool_steps)
            nstore = [0]

            def store(dst, src):
                pool.dma_start(dst, src).then_inc(stored, 16)
                nstore[0] += 1

            G.memset(one_col[:], 1.0).then_inc(buffers_set, 1)
            G.memset(mean_col[:], 1.0 / D).then_inc(buffers_set, 1)
            G.memset(st[:], 0.0).then_inc(buffers_set, 1)
            G.memset(lgb[:], 0.0).then_inc(buffers_set, 1)
            G.memset(own_rows[:], 0.0).then_inc(buffers_set, 1)
            G.memset(xpad[:, :, 0:3], 0.0).then_inc(buffers_set, 1)
            pool.wait_ge(const_landed, 16)
            for l in range(L):
                if l:
                    passed(pool, (l - 1, "var", 2))
                pool.dma_start(sc_in, a["state_conv"][l].rearrange("b i n -> (b i) n")
                               ).then_inc(conv_state_landed, 16)
                store(o_cs[l, :, 0:2, :], a["state_conv"][l][:, 1:3, :])
                for i, t in enumerate(DECODE_FIRST):
                    n = TILES[t][1]
                    copied(pool, (l, "tok", "q", t))
                    copied(pool, (l, "tok", "k", t))
                    x = qk_raw[0:n, t, :].rearrange("p (h s d) -> p h s d", h=16, s=2)
                    o = qkr[0:n, t, :].rearrange("p (h s d) -> p h s d", h=16, s=2)
                    w = rope_t[0:n, :].rearrange("p (h d) -> p h d", h=16)
                    cos = const[0:n, C_COS + 32 * t:C_COS + 32 * t + 32].unsqueeze(1).to_broadcast([n, 16, 32])
                    sin = const[0:n, C_SIN + 32 * t:C_SIN + 32 * t + 32].unsqueeze(1).to_broadcast([n, 16, 32])
                    step.inc(G.tensor_tensor(o[:, :, 0, :], x[:, :, 0, :], cos, ALU.mult))
                    step.done(G.tensor_tensor(w, x[:, :, 1, :], sin, ALU.mult))
                    step.inc(G.tensor_tensor(o[:, :, 0, :], o[:, :, 0, :], w, ALU.subtract))
                    step.done(G.tensor_tensor(o[:, :, 1, :], x[:, :, 1, :], cos, ALU.mult))
                    step.done(G.tensor_tensor(w, x[:, :, 0, :], sin, ALU.mult))
                    G.tensor_tensor(o[:, :, 1, :], o[:, :, 1, :], w, ALU.add).then_inc(rope_ready.sem, 1)
                    rope_ready.wait(pool, l, i)
                for t in range(2):
                    store(o_kp[l, 0, t * P:(t + 1) * P].rearrange("t h d -> t (h d)"), qkr[:, t, 512:1024])
                store(o_ks[l, :, 0].rearrange("b h d -> b (h d)"), qkr[0:8, 2, 512:1024])
                copied(pool, (l, "dtb"))
                s = rg.arrived(pool, (l, "state"))
                S = ring[:, s, :].rearrange("p (b j n) -> p b j n", b=8, j=4)
                for b in range(8):
                    G.tensor_tensor(S[:, b], S[:, b], dcol[:, :, 8 + b].unsqueeze(2).to_broadcast([P, 4, SN]),
                                    ALU.mult).then_inc(state_decayed.sem, 1)
                xwsc_ready.wait(pool, l)
                for c in range(2):
                    copied(pool, (l, "xt", c))
                    xv = xtok[:, c, :].rearrange("p (h d) -> p h d", h=SH)
                    step.inc(G.tensor_tensor(
                        xdt[:, c, :].rearrange("p (h d) -> p h d", h=SH), xv,
                        dtv[:, 8 * c:8 * c + 8].unsqueeze(2).to_broadcast([P, SH, SP_]), ALU.mult))
                    G.tensor_tensor(
                        xw[:, c, :].rearrange("p (h d) -> p h d", h=SH), xv,
                        xwsc[:, 8 * c:8 * c + 8].unsqueeze(2).to_broadcast([P, SH, SP_]), ALU.mult
                    ).then_inc(xdt_ready.sem, 1)
                for t, (_, n) in enumerate(TILES):
                    copied(pool, (l, "xt", t))
                    G.tensor_tensor(
                        mix[0:n, t, 512:1024].rearrange("p (h d) -> p h d", h=SH),
                        xtok[0:n, t, :].rearrange("p (h d) -> p h d", h=SH),
                        raw8[0:n, 2, l, :].unsqueeze(2).to_broadcast([n, SH, SP_]), ALU.mult
                    ).then_inc(xskip_ready.sem, 1)
                copied(pool, (l, "cp", 1))
                store(o_cp[l, 0], conv_rows[0:3])
                store(o_cs[l, :, 2, :], conv_rows[3:11])
                copied(pool, (l, "tok", "v", 2))
                for t in range(2):
                    store(o_vp[l, 0, t * P:(t + 1) * P].rearrange("t h d -> t (h d)"), vz[:, t, 0:512])
                store(o_vs[l, :, 0].rearrange("b h d -> b (h d)"), vz[0:8, 2, 0:512])
                ysT_ready.wait(pool, l)
                pool.dma_start(o_ss[l].rearrange("b h p n -> (b h p) n").rearrange("(j p) n -> p j n", p=P),
                               ring[:, s, :].rearrange("p (j n) -> p j n", j=32)).then_inc(state_stored, 16)
                copied(pool, (l, "stT"))
                store(o_sp[l, 0].rearrange("h p n -> (h p) n").rearrange("(j p) n -> p j n", p=P), ssm_rows)
                assert nstore[0] == STORES_LAYER * (l + 1)
                if l == 0:
                    passed(pool, (l, "d", 7))
                    G.memset(xpad[:, :, 0:3], 0.0).then_inc(buffers_set, 1)
                else:
                    passed(pool, (l, "co", 7))
                    pool.wait_ge(stored, 16 * STORES_LAYER * (l + 1))
                    for k in range(KT):
                        G.memset(acc[:, k, :], 0.0).then_inc(part_added, 1)
                    G.memset(gates[:], 0.0).then_inc(buffers_set, 1)
                    G.memset(posp[:], -1.0).then_inc(buffers_set, 1)
            copied(pool, ("out", 5))
            store(y_p[0].rearrange("(t p) n -> p t n", p=P), y_tok[:, 0:2, :])
            store(y_s[:, 0, :], y_tok[0:8, 2, :])
            assert nstore[0] == NSTORES
            pool.wait_ge(stored, 16 * NSTORES)
            pool.wait_ge(state_stored, 16 * L)
            pool.wait_ge(mem_stored, 16 * 8 * L)

        ffn_chunks = [(0, "gu", f) for f in range(NGU)] + [(0, "dn", i) for i in range(NDN)]
        ffn_signal, used_halves = {}, 0
        for q in range(NGU + NDN):
            for j in range(2):
                if q < NGU and j:
                    ffn_signal[q, j] = (0, "u", q, 1)
                elif q >= NGU and j and (q - NGU) % 3 == 2:
                    ffn_signal[q, j] = (0, "d", 4 * ((q - NGU) // 3) + 3)
                else:
                    used_halves += 1
                    ffn_signal[q, j] = used_halves

        def ffn_half(q, j):
            n = HALF if j == 0 or q < NGU or (q - NGU) % 3 < 2 else 2 * 512
            s = rg.pos[ffn_chunks[q]] % RING
            return high_bufs[1 - j][:, HALF - n:HALF], s, slice(j * HALF, j * HALF + n)

        def ffn_half_used(eng, q, j):
            what = ffn_signal[q, j]
            if isinstance(what, int):
                eng.wait_ge(ffn_used, what)
            else:
                passed(eng, what)

        def halves_of(p):
            return [(j, 2 * p + j) for j in ((0,) if p == NGU + NDN - 1 else (0, 1))]

        def half_used(eng, e, c, h):
            i, (p, j) = expert_no(e, c), divmod(h, 2)
            if j == 0:
                eng.wait_ge(first_half_used, i * (NGU + NDN - 1) + (p + 1))
            elif p < NGU:
                eng.wait_ge(gu_full, i * NGU + (p + 1))
            else:
                eng.wait_ge(dn_done, i * NDN + (p - NGU + 1))

        GU_BANKS, T_BANKS, Y_BANKS, X_BANKS = banks[0:2], banks[2:4], banks[4:6], banks[6:8]
        SUM_BANKS = GU_BANKS + X_BANKS

        def expert_products(pe, mm, tr):
            def gather(e, c):
                pe.wait_ge(sel_ready, expert_no(e, c) + (c + 1))
                pe.wait_ge(part_added, parts_added(e, c) if isinstance(e, int) else parts_added(e - 1, c))
                for n in range(2):
                    for k in range(4):
                        for t, (_, rows) in enumerate(TILES):
                            last = mm(X_BANKS[n][:, k * lots:(k + 1) * lots],
                                      x_tok[0:rows, t, (4 * n + k) * P:(4 * n + k + 1) * P],
                                      Sel[0:rows, t, 0:lots], t == 0, t == 2)
                    last.then_inc(X_full, 1)

            def product(out, xh, xl, w, low, first, last):
                mm(out, xh, w, first, False)
                mm(out, xl, w, False, False)
                return mm(out, xh, low, False, last)

            def expert(e, c):
                i = expert_no(e, c)
                tb = transposes_before(e, c)

                def weights(p, j, h):
                    pe.wait_ge(split_low, i * HALVES + (h + 1))
                    return high_bufs[h % HIGH_BUFS][:], ring_low[:, epos[p][2], j * HALF:(j + 1) * HALF]

                def gate_up(f):
                    if f >= 2:
                        pe.wait_ge(h_ready, i * NGU + (f - 1))
                    else:
                        pe.wait_ge(part_added, i * KT + (5 + f))
                    for j, h in halves_of(f):
                        high, low = (x.rearrange("p (k n) -> p k n", k=4) for x in weights(f, j, h))
                        for kk in range(4):
                            k = 4 * j + kk
                            last = product(GU_BANKS[f % 2][0:lots, :], xg_high[:, k, 0:lots], xg_low[:, k, 0:lots],
                                           high[:, kk, :], low[:, kk, :], k == 0, k == KT - 1)
                        last.then_inc(gu_full if j else first_half_used, 1)

                def scatter_matrix():
                    for t, (t0, rows) in enumerate(TILES):
                        last = tr(T_BANKS[1][0:lots, t0:t0 + rows], GSel[0:rows, t, 0:lots], rows)
                    last.then_inc(T_full, 1)

                def transpose_h(f):
                    pe.wait_ge(h_ready, i * NGU + (f + 1))
                    if f >= 1:
                        pe.wait_ge(T_done, tb + f)
                    if f >= 2:
                        pe.wait_ge(T_low, i * NGU + (f - 1))
                    for s in range(2):
                        last = tr(T_BANKS[f % 2][:, s * lots:(s + 1) * lots],
                                  hh[0:lots, f % 2, s * P:(s + 1) * P], lots)
                    last.then_inc(T_full, 1)

                def down(d):
                    p = NGU + d
                    f_last = min(4 * d + 3, FT - 1) // 2
                    pe.wait_ge(T_done, tb + (f_last + 2))
                    pe.wait_ge(T_low, i * NGU + (f_last + 1))
                    for j, h in halves_of(p):
                        high, low = (x.rearrange("p (f n) -> p f n", n=1024) for x in weights(p, j, h))
                        for f in range(2):
                            for n in range(2):
                                ff = 4 * d + 2 * j + f
                                cols = slice(n * 512, (n + 1) * 512)
                                last = product(Y_BANKS[n][0:lots, :], he_high[:, ff, 0:lots], he_low[:, ff, 0:lots],
                                               high[:, f, cols], low[:, f, cols], ff == 0, ff == FT - 1)
                        last.then_inc(dn_done if j or p == NGU + NDN - 1 else first_half_used, 1)

                pe.wait_ge(xg_taken, i * 2 + 2 * (c + 1))
                pe.wait_ge(xg_low_ready, i * 2 + 2 * (c + 1))
                for f in range(NGU):
                    gate_up(f)
                    if f == 0:
                        scatter_matrix()
                    else:
                        transpose_h(f - 1)
                down(0)
                transpose_h(NGU - 1)
                for d in range(1, NDN):
                    down(d)
                gather(e + 1, c)
                pe.wait_ge(y_by_act, i + 1)
                pe.wait_ge(y_by_dve, i + 1)
                pe.wait_ge(T_done, tb + 1)
                for k in range(KT):
                    if k in (2, 3):
                        pe.wait_ge(xg_taken, i * 2 + (2 * (c + 1) + k - 1))
                        pe.wait_ge(xg_low_ready, i * 2 + (2 * (c + 1) + k - 1))
                    elif k >= 4:
                        pe.wait_ge(part_added, parts_added(e, c) + (k - 3))
                    last = mm(SUM_BANKS[k % 4][:, 0:T], ye[0:lots, k * P:(k + 1) * P], GSelT[0:lots, :], True, True)
                    last.then_inc(X_full, 1)

            def one_pass(c):
                gather(0, c)
                with pe.Fori(0, EXPERTS) as e:
                    expert(e, c)

            one_pass(0)
            pe.wait_ge(pos_known, 1)
            most = pe.value_load(cnti[0:1, 0:1], min_val=0, max_val=T)
            for c in range(1, passes):
                with pe.If(most > (0 if always else lots * c)):
                    one_pass(c)

        @block.tensor
        def _(pe):
            M = nc.tensor

            def mm(out, lhsT, rhs, start, stop):
                return M.matmul(out, lhsT, rhs, start=start, stop=stop)

            def tr(out, in_, n):
                return M.transpose(out, in_, ident[0:n, 0:n])

            def full(ins):
                ins.then_inc(psum_full, 1)

            def slot(key):
                return ring[:, rg.arrived(pe, key), :]

            def blocks8(name, src, wait=None):
                for n in range(5):
                    t = n // 2
                    rows = TILES[t][1]
                    if wait is not None:
                        wait(t)
                    bk = turns.open(pe, name + (n,))
                    ks = range(8) if t == 2 else range(4 * (n % 2), 4 * (n % 2) + 4)
                    for j, k in enumerate(ks):
                        last = tr(bk[:, j * rows:(j + 1) * rows], src[0:rows, t, k * P:(k + 1) * P], rows)
                    full(last)

            def to_tokens(name, ready):
                for n in range(6):
                    t, h = n // 2, n % 2
                    t0, rows = TILES[t]
                    bk = turns.open(pe, name + (n,))
                    for j in range(4):
                        if t == 0:
                            ready(4 * h + j)
                        last = tr(bk[0:rows, j * P:(j + 1) * P], xT[:, 4 * h + j, t0:t0 + rows], P)
                    full(last)

            def block_of(w, name, m, rhs, ready=None):
                bk = turns.open(pe, name + (m,))
                for k in range(KT):
                    if ready:
                        ready(k)
                    last = mm(bk[:, 0:T], w[:, k, (m % 4) * P:(m % 4 + 1) * P], rhs[:, k, :], k == 0, k == KT - 1)
                full(last)

            def columns_of(key, name, m0, rhs):
                w = slot(key).rearrange("p (k n) -> p k n", k=KT)
                for m in range(4):
                    block_of(w, name, m0 + m, rhs)

            def norm_sums(l, i, part):
                bk = turns.open(pe, (l, "mu", i))
                if i < 2:
                    sum_ready.wait(pe, l, i)
                    last = mm(bk[:, 0:T], mean_of, stat[:], True, True)
                else:
                    for k in range(KT):
                        if part:
                            copied(pe, (l, part, k))
                        last = mm(bk[:, 0:T], mean_of, R[:, k, :], k == 0, k == KT - 1)
                full(last)
                bk = turns.open(pe, (l, "var", i))
                for k in range(KT):
                    if k % 2 == 0:
                        squared.wait(pe, l, 4 * i + k // 2)
                    last = mm(bk[:, 0:T], mean_of, SQ[:, k, :], k == 0, k == KT - 1)
                full(last)

            def x_ready(l, i):
                def ready(k):
                    if l < 0:
                        if k == 0:
                            copied(pe, ("xin", 4))
                    elif k < 7:
                        xT_act.wait(pe, l, 7 * i + k)
                    else:
                        xT_dve.wait(pe, l, i)
                return ready

            pe.wait_ge(const_landed, 16)
            pe.wait_ge(vecs_landed, 16 * 6)
            bk = turns.open(pe, ("vec",))
            tr(bk[:, 0:122], vraw[0:122, 0, :], 122)
            full(tr(bk[:, 128:192], vraw[0:64, 1, :], 64))
            blocks8(("xin",), slot(("x",))[:, 0:3072].rearrange("p (t n) -> p t n", t=3))
            mem_in = slot(("mem",))[:, 0:2048].rearrange("p (t n) -> p t n", t=2)
            for n in range(4):
                bk = turns.open(pe, ("mem", n))
                for j in range(4):
                    k = 4 * (n % 2) + j
                    last = tr(bk[:, j * P:(j + 1) * P], mem_in[:, n // 2, k * P:(k + 1) * P], P)
                full(last)
            pe.wait_ge(buffers_set, 6)

            for l in range(L):
                def token_major(c, t, ready=None):
                    w = slot((l, c)).rearrange("p (k n) -> p k n", k=KT)
                    t0, n = TILES[t]
                    bk = turns.open(pe, (l, "tok", c, t))
                    for k in range(KT):
                        if ready:
                            ready(k)
                        last = mm(bk[0:n, :], xT[:, k, t0:t0 + n], w[:, k, :], k == 0, k == KT - 1)
                    full(last)

                def memory_part(i):
                    c, t = divmod(i, 2)
                    w = slot((l, "ckv", c)).rearrange("p (k n) -> p k n", k=KT)
                    bk = turns.open(pe, (l, "mkv", i))
                    if l == 0 and i == 0:
                        copied(pe, ("mem", 3))
                    for k in range(KT):
                        last = mm(bk[:], memT[:, k, t * P:(t + 1) * P], w[:, k, :], k == 0, k == KT - 1)
                    full(last)

                for c in ("q", "k"):
                    for t in DECODE_FIRST:
                        first = c == "q" and t == DECODE_FIRST[0]
                        token_major(c, t, x_ready(l - 1, 2) if first else None)
                        if first:
                            pe.wait_ge(small_landed, 16 * 9)
                            bk = turns.open(pe, (l, "dt"))
                            for t, (t0, n) in enumerate(TILES):
                                for k in range(KT):
                                    mm(bk[0:n, 8 * t:8 * t + 8], xT[:, k, t0:t0 + n], wdt[:, l, k, :],
                                       k == 0, k == KT - 1)
                            for k in range(KT):
                                last = mm(bk[0:8, 24:32], wdt[:, l, k, :], xT[:, k, NP_TOK:T], k == 0, k == KT - 1)
                            full(last)
                bk = turns.open(pe, (l, "acs"))
                da_ready.wait(pe, l)
                for c in range(2):
                    mm(bk[:, 8 * c:8 * c + 8], upper, da[:, 8 * c:8 * c + 8], True, True)
                for c in range(2):
                    last = mm(bk[:, 16 + 8 * c:24 + 8 * c], ones, da[:, 8 * c:8 * c + 8], True, True)
                full(last)
                bk = turns.open(pe, (l, "scT"))
                pe.wait_ge(conv_state_landed, 16 * (l + 1))
                for m in range(8):
                    last = tr(bk[:, 24 * m:24 * m + 24], sc_in[:, m * P:(m + 1) * P], 24)
                full(last)
                rope_ready.wait(pe, l, 0)
                for b in range(8):
                    w = slot((l, f"xbc{b // 4}")).rearrange("p (k n) -> p k n", k=KT)
                    block_of(w, (l, "xbc"), b, xT)
                    bk = turns.open(pe, (l, "qb", b))
                    full(mm(bk[:], ident[0:8, b:b + 1].to_broadcast([8, P]), qkr[0:8, 2, 0:512], True, True))
                    if b == 0:
                        bk = turns.open(pe, (l, "dtb"))
                        decays_out.wait(pe, l)
                        for h in range(SH):
                            r0, j = 64 * (h % 2), h // 2
                            this_head = ident[0:8, h:h + 1].to_broadcast([8, 64])
                            mm(bk[r0:r0 + 64, 16 * j:16 * j + 8], this_head, dtv[0:8, 24:32], True, True)
                            last = mm(bk[r0:r0 + 64, 16 * j + 8:16 * j + 16], this_head, ex[0:8, 48:56], True, True)
                        full(last)
                token_major("v", 0)
                bk = turns.open(pe, (l, "sST"))
                dec_scores.wait(pe, l)
                for g in range(2):
                    tr(bk[0:64, g * P:(g + 1) * P], sS[:, g].rearrange("p b h -> p (b h)"), P)
                full(mm(bk[0:64, 256:257], sbt[0:8, :], one_col[0:8, :], True, True))
                token_major("v", 1)
                token_major("v", 2)
                conv_ready.wait(pe, l, 8)
                for t, (t0, n) in enumerate(TILES):
                    bk = turns.open(pe, (l, "xt", t))
                    for j in range(4):
                        last = tr(bk[0:n, j * P:(j + 1) * P], convT[:, j, t0:t0 + n], P)
                    full(last)
                    bk = turns.open(pe, (l, "Bt", t))
                    for j in range(4 if t == 2 else 2):
                        last = tr(bk[0:n, j * P:(j + 1) * P], convT[:, 4 + j, t0:t0 + n], P)
                    full(last)
                for h in range(2):
                    bk = turns.open(pe, (l, "cp", h))
                    for j in range(4):
                        last = tr(bk[0:11, j * P:(j + 1) * P], ct11[:, 4 * h + j, :], P)
                    full(last)
                copied(pe, (l, "Bt", 2))
                for i in range(4):
                    for b in (2 * i, 2 * i + 1):
                        bk = turns.open(pe, (l, "BC", b))
                        full(mm(bk[:], ident[0:8, b:b + 1].to_broadcast([8, P]), BCs, True, True))
                    if i < 3:
                        token_major("z", i)
                    if i == 0:
                        bk = turns.open(pe, (l, "pT"))
                        dec_probs.wait(pe, l)
                        for g in range(2):
                            last = tr(bk[:, g * 64:(g + 1) * 64], pSx[:, g * P:(g + 1) * P], 64)
                        full(last)
                        bk = turns.open(pe, (l, "pself"))
                        full(mm(bk[0:8, 0:8], const[0:64, C_REQ:C_REQ + 8], pself_r[:], True, True))
                memory_part(0)
                for c in range(2):
                    bk = turns.open(pe, (l, "st", c))
                    xdt_ready.wait(pe, l, c)
                    copied(pe, (l, "Bt", c))
                    for g in range(SG):
                        last = mm(bk[:, g * 256:(g + 1) * 256], Btok[:, c, g * P:(g + 1) * P],
                                  xw[:, c, g * 256:(g + 1) * 256], True, True)
                    full(last)
                for c in range(2):
                    for g in range(SG):
                        bk = turns.open(pe, (l, "ab", c, g))
                        for r in range(4):
                            h = 8 * c + 4 * g + r
                            last = mm(bk[:, r * P:(r + 1) * P], da[:, h:h + 1].to_broadcast([P, P]), upper,
                                      True, True)
                        full(last)
                    bk = turns.open(pe, (l, "cb", c))
                    for g in range(SG):
                        last = mm(bk[:, g * P:(g + 1) * P], convT[:, 4 + g, c * P:(c + 1) * P],
                                  convT[:, 6 + g, c * P:(c + 1) * P], True, True)
                    full(last)
                    memory_part(1 + c)
                    bk = turns.open(pe, (l, "y", c))
                    copied(pe, (l, "cb", c))
                    for h in range(SH):
                        last = mm(bk[:, h * SP_:(h + 1) * SP_], Mdec[:, h // 4, h % 4, :],
                                  xdt[:, c, h * SP_:(h + 1) * SP_], True, True)
                    full(last)
                bk = turns.open(pe, (l, "yo"))
                copied(pe, (l, "st", 0))
                for g in range(SG):
                    last = mm(bk[:, g * 256:(g + 1) * 256], convT[:, 6 + g, P:2 * P],
                              ST0[:, g * 256:(g + 1) * 256], True, True)
                full(last)
                bk = turns.open(pe, (l, "stT"))
                copied(pe, (l, "st", 1))
                for j in range(4):
                    last = tr(bk[:, j * P:(j + 1) * P], STf[:, j * P:(j + 1) * P], P)
                full(last)
                bk = turns.open(pe, (l, "ysT"))
                ysT_ready.wait(pe, l)
                for j in range(4):
                    last = tr(bk[0:8, j * P:(j + 1) * P], ysT[:, j, :], P)
                full(last)
                rope_ready.wait(pe, l, 2)
                for i in range(4):
                    bk = turns.open(pe, (l, "qkT", i))
                    for j in range(2):
                        for t in range(2):
                            last = tr(bk[:, j * 256 + t * P:j * 256 + (t + 1) * P],
                                      qkr[:, t, (2 * i + j) * P:(2 * i + j + 1) * P], P)
                    full(last)
                copied(pe, (l, "qkT", 3))
                for qt in range(2):
                    nk = (qt + 1) * P
                    for hp in range(2):
                        for m in range(2):
                            bk = turns.open(pe, (l, "S", qt, hp, m))
                            for j in range(2):
                                h = 2 * hp + j
                                last = mm(bk[:, j * nk:(j + 1) * nk],
                                          kqT[64 * m:64 * m + 64, h, qt * P:(qt + 1) * P],
                                          kqT[64 * m:64 * m + 64, 4 + h, 0:nk], True, True)
                            full(last)
                    memory_part(3 + qt)

                def attend(qt):
                    for kt in range(qt + 1):
                        bk = turns.open(pe, (l, "aT", qt, kt))
                        a_ready.wait(pe, l, qt)
                        for h in range(AH):
                            last = tr(bk[:, h * P:(h + 1) * P], probs[:, h, 0, kt * P:(kt + 1) * P], P)
                        full(last)
                    bk = turns.open(pe, (l, "O", qt))
                    copied(pe, (l, "aT", qt, qt))
                    for h in range(AH):
                        for kt in range(qt + 1):
                            last = mm(bk[:, h * P:(h + 1) * P], aT[:, qt + kt, h, :],
                                      vz[:, kt, h * DV:(h + 1) * DV], kt == 0, kt == qt)
                    full(last)

                attend(0)
                memory_part(5)
                bk = turns.open(pe, (l, "oS"))
                copied(pe, (l, "pT"))
                for b in range(8):
                    V4 = slot((l, "V", b // 4)).rearrange("p (b g n) -> p b g n", b=4, g=2)
                    for g in range(2):
                        last = mm(bk[0:32, :], own_rows[:, g, 32 * b:32 * b + 32], V4[:, b % 4, g, :],
                                  b + g == 0, b + g == 8)
                full(last)
                memory_part(6)
                bk = turns.open(pe, (l, "oSt"))
                copied(pe, (l, "oS"))
                full(mm(bk[0:8, :], request_of, tmp[0:32, 0:512], True, True))
                attend(1)
                memory_part(7)
                blocks8((l, "mixT"), mix, lambda t: mix_ready.wait(pe, l, NORM_ORDER.index(t)))
                copied(pe, (l, "mixT", 4))
                columns_of((l, "out", 0), (l, "m"), 0, mixT)
                columns_of((l, "out", 1), (l, "m"), 4, mixT)
                mkv = slot((l, "mkv")).rearrange("p (t n) -> p t n", t=2)
                for i in range(4):
                    bk = turns.open(pe, (l, "mkT", i))
                    for j in range(2):
                        for t in range(2):
                            last = tr(bk[:, j * 256 + t * P:j * 256 + (t + 1) * P],
                                      mkv[:, t, (2 * i + j) * P:(2 * i + j + 1) * P], P)
                    full(last)
                norm_sums(l, 0, "m")
                def q_on_all(b, i):
                    bk = turns.open(pe, (l, "qsb", b, i))
                    full(mm(bk[:], ident[0:8, b:b + 1].to_broadcast([8, P]), qs[0:8, i * 512:(i + 1) * 512],
                            True, True))

                def q_rows(i):
                    bk = turns.open(pe, (l, "qsT", i))
                    copied(pe, (l, "cq", 4 * i + 3))
                    for j in range(4):
                        last = tr(bk[0:8, j * P:(j + 1) * P], qcT[:, 4 * i + j, NP_TOK:T], P)
                    full(last)

                w = slot((l, "cq", 0)).rearrange("p (k n) -> p k n", k=KT)
                for m in range(4):
                    block_of(w, (l, "cq"), m, xT, None if m else x_ready(l, 0))
                w = slot((l, "cq", 1)).rearrange("p (k n) -> p k n", k=KT)
                for n in range(4):
                    block_of(w, (l, "cq"), 4 + n, xT)
                    if n == 0:
                        q_rows(0)
                        copied(pe, (l, "qsT", 0))
                    for b in (2 * n, 2 * n + 1):
                        q_on_all(b, 0)
                copied(pe, (l, "cq", 7))
                for n in range(4):
                    t, hp = n // 2, n % 2
                    bk = turns.open(pe, (l, "cS", t, hp))
                    for j in range(2):
                        h = 2 * hp + j
                        for d in range(2):
                            last = mm(bk[:, j * 256:(j + 1) * 256], qcT[:, 2 * h + d, t * P:(t + 1) * P],
                                      mkT[:, 2 * h + d, :], d == 0, d == 1)
                    full(last)
                    if n == 0:
                        q_rows(1)
                        copied(pe, (l, "qsT", 1))
                    for b in (2 * n, 2 * n + 1):
                        q_on_all(b, 1)
                for t in range(2):
                    for kt in range(2):
                        bk = turns.open(pe, (l, "cPT", t, kt))
                        cP_ready.wait(pe, l, t)
                        for h in range(MH):
                            last = tr(bk[:, h * P:(h + 1) * P], cP[:, t, h, kt * P:(kt + 1) * P], P)
                        full(last)
                bk = turns.open(pe, (l, "sCT"))
                for t in range(2):
                    last = tr(bk[0:32, t * P:(t + 1) * P], sC[:, t].rearrange("p b h -> p (b h)"), P)
                full(last)
                copied(pe, (l, "cPT", 1, 1))
                for i in range(4):
                    bk = turns.open(pe, (l, "cO", i))
                    for d in range(2):
                        for kt in range(2):
                            last = mm(bk[:, d * 256:(d + 1) * 256],
                                      mkv[:, kt, 1024 + i * MD + d * P:1024 + i * MD + (d + 1) * P],
                                      cPT[:, kt, i, :], kt == 0, kt == 1)
                    full(last)
                bk = turns.open(pe, (l, "sPT"))
                cs_probs.wait(pe, l)
                for t in range(2):
                    last = tr(bk[:, t * 32:(t + 1) * 32], sP[0:32, t * P:(t + 1) * P], 32)
                full(last)
                bks = [turns.open(pe, (l, "oV", i)) for i in range(2)]
                copied(pe, (l, "sPT"))
                for b in range(8):
                    V2 = slot((l, "mV", b // 2)).rearrange("p (b t n) -> p b t n", b=2, t=2)
                    for t in range(2):
                        for i in range(2):
                            last = mm(bks[i][0:32, :], own_rows[:, t, 32 * b:32 * b + 32],
                                      V2[:, b % 2, t, 512 * i:512 * (i + 1)], b + t == 0, b + t == 8)
                            if b + t == 8:
                                full(last)
                bk = turns.open(pe, (l, "soT"))
                for i in range(2):
                    copied(pe, (l, "oV", i))
                for m in range(8):
                    last = mm(bk[:, m * 8:(m + 1) * 8], ctmp[0:32, m * P:(m + 1) * P], request_of, True, True)
                full(last)
                copied(pe, (l, "cO", 3))
                copied(pe, (l, "soT"))
                columns_of((l, "co", 0), (l, "co"), 0, oT)
                columns_of((l, "co", 1), (l, "co"), 4, oT)
                norm_sums(l, 1, "co")
                if l == 0:
                    def parts(q, j):
                        pe.wait_ge(ffn_low, 2 * q + j + 1)
                        high, s, part = ffn_half(q, j)
                        return high, ring_low[:, s, part]

                    def product(out, w, w_low, xh, xl, first, last):
                        mm(out, w, xh, first, False)
                        mm(out, w, xl, False, False)
                        return mm(out, w_low, xh, False, last)

                    for f in range(NGU):
                        bks = [turns.open(pe, (l, "gu"[u], f, b)) for b in range(2) for u in range(2)]
                        for j in range(2):
                            high, low = (w.rearrange("p (k u n) -> p k u n", k=4, u=2) for w in parts(f, j))
                            for b in range(2):
                                for u in range(2):
                                    for kk in range(4):
                                        k = 4 * j + kk
                                        if f + b + u == 0:
                                            pe.wait_ge(x_low_ready, k + 1)
                                        cols = slice(b * P, (b + 1) * P)
                                        last = product(bks[2 * b + u][:, 0:T], high[:, kk, u, cols],
                                                       low[:, kk, u, cols], x_high[:, k, :], x_low[:, k, :],
                                                       k == 0, k == KT - 1)
                                    if j:
                                        full(last)
                            if j == 0:
                                last.then_inc(ffn_used, 1)
                    for half in range(2):
                        bks = [turns.open(pe, (l, "d", 4 * half + m)) for m in range(4)]
                        for i in range(3):
                            nf = min(8, FT - 8 * i)
                            pe.wait_ge(h_low_ready, 8 * i + nf)
                            for j in range(2):
                                q = NGU + 3 * half + i
                                high, low = (w.rearrange("p (f n) -> p f n", n=512) for w in parts(q, j))
                                for m in range(4):
                                    for f in range(min(4, nf - 4 * j)):
                                        ff, cols = 8 * i + 4 * j + f, slice(m * P, (m + 1) * P)
                                        last = product(bks[m][:, 0:T], high[:, f, cols], low[:, f, cols],
                                                       h_high[:, ff, :], h_low[:, ff, :], ff == 0, ff == FT - 1)
                                    if ff == FT - 1:
                                        full(last)
                                if ff < FT - 1:
                                    last.then_inc(ffn_used, 1)
                    norm_sums(l, 2, "d")
                else:
                    to_tokens((l, "xtok"), x_ready(l, 1))
                    bk = turns.open(pe, (l, "lg"))
                    for t, (t0, n) in enumerate(TILES):
                        for k in range(KT):
                            last = mm(bk[0:n, 8 * t:8 * t + 8], xT[:, k, t0:t0 + n], wr[:, k, :],
                                      k == 0, k == KT - 1)
                    full(last)
                    bk = turns.open(pe, (l, "pos"))
                    pe.wait_ge(sel_known, 1)
                    for t, (_, n) in enumerate(TILES):
                        for u in range(t):
                            mm(bk[0:n, 8 * t:8 * t + 8], one_col[:].to_broadcast([P, n]), sel[:, u, :], u == 0, False)
                        mm(bk[0:n, 8 * t:8 * t + 8], before[0:n, 0:n], sel[0:n, t, :], t == 0, True)
                    for t, (_, n) in enumerate(TILES):
                        last = mm(bk[:, 24:32], one_col[0:n, :].to_broadcast([n, P]), sel[0:n, t, :], t == 0, t == 2)
                    full(last)
                    copied(pe, (l, "xtok", 5))
                    copied(pe, (l, "pos"))
                    expert_products(pe, mm, tr)
                    pe.wait_ge(moe_done, 1)
                    norm_sums(l, 2, None)
            to_tokens(("out",), x_ready(L - 1, 2))

        def expert_activations(act):
            S = nc.scalar

            def take_gathered(groups):
                for n in range(2):
                    act.wait_ge(X_full, groups + (n + 1))
                    S.activation(xg_high[:, 4 * n:4 * n + 4, 0:lots],
                                 X_BANKS[n][:, 0:4 * lots].rearrange("p (k n) -> p k n", k=4), ACT.Copy
                                 ).then_inc(xg_taken, 1)

            def high_part(e, c, p):
                i, (_, _, s, v) = expert_no(e, c), epos[p]
                act.wait_ge(landed[s], i * eper[s] + (rg.slot_total[s] + v))
                for j, h in halves_of(p):
                    if h >= HIGH_BUFS:
                        half_used(act, e, c, h - HIGH_BUFS)
                    S.activation(high_bufs[h % HIGH_BUFS][:], ring[:, s, j * HALF:(j + 1) * HALF], ACT.Copy
                                 ).then_inc(split_high, 1)

            def expert(e, c):
                i = expert_no(e, c)
                tb = transposes_before(e, c)

                def silu(f):
                    act.wait_ge(gu_full, i * NGU + (f + 1))
                    if f >= 2:
                        act.wait_ge(h_ready, i * NGU + (f - 1))
                    S.activation(sg[0:lots, f % 2, :], GU_BANKS[f % 2][0:lots, 0:GU], ACT.Silu).then_inc(sg_ready, 1)

                def take_h(f):
                    act.wait_ge(T_full, tb + (f + 2))
                    S.activation(he_high[:, 2 * f:2 * f + 2, 0:lots],
                                 T_BANKS[f % 2][:, 0:2 * lots].rearrange("p (s n) -> p s n", s=2),
                                 ACT.Copy).then_inc(T_done, 1)

                for p in range(1, NGU + NDN):
                    high_part(e, c, p)
                    if 1 <= p <= NGU:
                        silu(p - 1)
                    if p == 1:
                        act.wait_ge(T_full, tb + 1)
                        S.activation(GSelT[0:lots, :], T_BANKS[1][0:lots, 0:T], ACT.Copy).then_inc(T_done, 1)
                    if 2 <= p <= NGU + 1:
                        take_h(p - 2)
                act.wait_ge(dn_done, i * NDN + NDN)
                S.activation(ye[0:lots, 0:512], Y_BANKS[0][0:lots, :], ACT.Copy).then_inc(y_by_act, 1)
                with act.If(e < EXPERTS - 1):
                    high_part(e + 1, c, 0)
                take_gathered(x_groups_before(e, c))

            def one_pass(c):
                high_part(0, c, 0)
                take_gathered(x_groups_before(0, c) - 2)
                with act.Fori(0, EXPERTS) as e:
                    expert(e, c)

            xT_dve.wait(act, L - 1, 1)
            one_pass(0)
            act.wait_ge(pos_known, 1)
            most = act.value_load(cnti[0:1, 0:1], min_val=0, max_val=T)
            for c in range(1, passes):
                with act.If(most > (0 if always else lots * c)):
                    one_pass(c)

        @block.scalar
        def _(act):
            S = nc.scalar
            step = Steps(act, act_steps)

            def copy_out(name, dst, src, func=ACT.Copy):
                bk = take(act, name)
                emptied_after(name, S.activation(dst, src(bk), func))

            def ffn_high_part(q, j):
                high, s, part = ffn_half(q, j)
                rg.arrived(act, ffn_chunks[q])
                if q:
                    ffn_half_used(act, q - 1, j)
                S.activation(high, ring[:, s, part], ACT.Copy).then_inc(ffn_high, 1)

            def x_high_part(k):
                S.activation(x_high[:, k, :], R[:, k, :], ACT.Identity, bias=col_b(0, 1, k)).then_inc(x_high_ready, 1)

            def norm(l, i):
                for h in range(4):
                    if h < 3:
                        centred.wait(act, l, 3 * i + h)
                    else:
                        copied(act, (l, "mu", i))
                    S.activation(SQ[:, 2 * h:2 * h + 2, :], R[:, 2 * h:2 * h + 2, :], ACT.Square
                                 ).then_inc(squared.sem, 1)
                bk = take(act, (l, "var", i))
                emptied_after((l, "var", i), S.activation(stat[:], bk[:, 0:T], ACT.Ln, bias=const[:, C_EPS:C_EPS + 1]))
                copied(act, (l, "var", i))
                S.activation(stat[:], stat[:], ACT.Exp, scale=-0.5).then_inc(ln_rstd.sem, 1)
                if (l, i) == (0, 1):
                    ffn_high_part(0, 0)
                for k in range(7):
                    scaled.wait(act, l, 8 * i + k)
                    S.activation(xT[:, k, :], R[:, k, :], ACT.Identity, bias=col_b(l, i, k)
                                 ).then_inc(xT_act.sem, 1)
                    if (l, i) == (0, 1):
                        x_high_part(k)
                if (l, i) == (0, 1):
                    scaled.wait(act, l, 8 * i + 7)
                    x_high_part(7)

            for n in range(4):
                copy_out(("mem", n), memT[:, 4 * (n % 2):4 * (n % 2) + 4, (n // 2) * P:(n // 2 + 1) * P],
                         lambda bk: bk[:].rearrange("p (k n) -> p k n", k=4))
            act.wait_ge(small_landed, 16 * 9)
            step.inc(S.activation(raw8[:, 1], raw8[:, 1], ACT.Exp))
            S.activation(col8[:, 1, :], col8[:, 1, :], ACT.Exp).then_inc(setup_exps, 1)
            act.wait_ge(lam_dots, 1)
            S.activation(lamt[:], lamt[:], ACT.Exp).then_inc(setup_exps, 1)
            act.wait_ge(vectors_ready, 1)
            act.wait_ge(buffers_set, 6)

            for l in range(L):
                dt_abs.wait(act, l)
                S.activation(dte, dte, ACT.Exp, scale=-1.0).then_inc(dt_exp.sem, 1)
                dt_exp1.wait(act, l)
                S.activation(dte, dte, ACT.Ln).then_inc(dt_ln.sem, 1)
                if l:
                    act.wait_ge(buffers_set, 7)
                for c, name in enumerate(("q", "k")):
                    for t in DECODE_FIRST:
                        n = TILES[t][1]
                        copy_out((l, "tok", name, t), qk_raw[0:n, t, 512 * c:512 * (c + 1)], lambda bk: bk[0:n, :])
                decays_in.wait(act, l)
                S.activation(ex, sc, ACT.Exp).then_inc(decays_out.sem, 1)
                for m in range(10):
                    if m < 8:
                        copied(act, (l, "xbc", m))
                        S.activation(convT[:, m, 0:NP_TOK], xpad[:, m, 0:NP_TOK], ACT.Identity,
                                     bias=cols_cb(l, m), scale=col_cw(l, 0, m)).then_inc(tap0_done.sem, 1)
                    if m >= 2:
                        taps_done.wait(act, l, m - 2)
                        S.activation(convT[:, m - 2, 0:NP_TOK], convT[:, m - 2, 0:NP_TOK], ACT.Silu
                                     ).then_inc(conv_ready.sem, 1)
                taps_done.wait(act, l, 8)
                S.activation(convT[:, :, NP_TOK:T], convT[:, :, NP_TOK:T], ACT.Silu).then_inc(conv_ready.sem, 1)
                for t, (_, n) in enumerate(TILES):
                    copy_out((l, "tok", "v", t), vz[0:n, t, 0:512], lambda bk: bk[0:n, :])
                dec_rows.wait(act, l)
                S.activation(pSx, pSx, ACT.Exp, bias=nb1[0:64], scale=DQ ** -0.5, accum_out=rs1[0:64]
                             ).then_inc(dec_exp.sem, 1)
                rope_ready.wait(act, l, 2)
                for t, (_, n) in enumerate(TILES):
                    copy_out((l, "xt", t), xtok[0:n, t, :], lambda bk: bk[0:n, :])
                    if t < 2:
                        copy_out((l, "Bt", t), Btok[:, t, :], lambda bk: bk[:, 0:256])
                    else:
                        copy_out((l, "Bt", t), BCs, lambda bk: bk[0:8, :])
                for h in range(2):
                    copy_out((l, "cp", h), conv_rows[:, 512 * h:512 * (h + 1)], lambda bk: bk[0:11, :])
                for t, (_, n) in enumerate(TILES):
                    copy_out((l, "tok", "z", t), vz[0:n, t, 512:1024], lambda bk: bk[0:n, :], ACT.Silu)

                def memory_part(i):
                    c, t = divmod(i, 2)
                    n = 8 * l + i
                    if n >= 1:
                        act.wait_ge(mem_stored, 16 * n)
                    copy_out((l, "mkv", i), mem_rows[:], lambda bk: bk[:])
                    copied(act, (l, "mkv", i))
                    out = (o_mk if c < 2 else o_mv)[l, 0, t * P:(t + 1) * P].rearrange("t h d -> t (h d)")
                    act.dma_start(out[:, 512 * (c % 2):512 * (c % 2 + 1)], mem_rows[:]
                                  ).then_inc(mem_stored, 16)

                memory_part(0)
                for n in range(4):
                    seg_ready.wait(act, l, n)
                    S.activation(Mdec[:, n % 2], Mdec[:, n % 2], ACT.Exp).then_inc(decay_ready.sem, 1)
                    if n % 2:
                        memory_part(1 + n // 2)
                copy_out((l, "stT"), ssm_rows, lambda bk: bk[:].rearrange("p (j n) -> p j n", j=4))
                xskip_ready.wait(act, l, 2)
                for i in range(4):
                    copy_out((l, "qkT", i), kqT[:, 2 * i:2 * i + 2, :],
                             lambda bk: bk[:].rearrange("p (j n) -> p j n", j=2))

                def exps(qt):
                    nk = (qt + 1) * P
                    for n in range(4):
                        hp, m = n // 2, n % 2
                        max_ready.wait(act, l, 4 * qt + n)
                        for j in range(2):
                            h = 2 * hp + j
                            ins = S.activation(probs[:, h, m, 0:nk], probs[:, h, m, 0:nk], ACT.Exp,
                                               bias=nb[:, 2 * h + m:2 * h + m + 1], scale=DQ ** -0.5,
                                               accum_out=rs[:, 2 * h + m:2 * h + m + 1])
                            if j == 0:
                                step.inc(ins)
                        ins.then_inc(probs_ready.sem, 1)

                def rms(n):
                    rows = TILES[NORM_ORDER[n]][1]
                    ms_ready.wait(act, l, n)
                    step.done(S.activation(rstd6[0:rows], ms[0:rows], ACT.Ln))
                    S.activation(rstd6[0:rows], rstd6[0:rows], ACT.Exp, scale=-0.5).then_inc(rstd_ready.sem, 1)

                def take_aT(qt, kt):
                    copy_out((l, "aT", qt, kt), aT[:, qt + kt], lambda bk: bk[:].rearrange("p (h n) -> p h n", h=AH))

                exps(0)
                memory_part(3)
                memory_part(4)
                take_aT(0, 0)
                exps(1)
                rms(0)
                memory_part(5)
                memory_part(6)
                take_aT(1, 0)
                take_aT(1, 1)
                rms(1)
                memory_part(7)
                rms(2)
                act.wait_ge(stored, 16 * STORES_LAYER * (l + 1))
                for i in range(4):
                    copy_out((l, "mkT", i), mkT[:, 2 * i:2 * i + 2, :],
                             lambda bk: bk[:].rearrange("p (j n) -> p j n", j=2))
                norm(l, 0)
                for m in range(8):
                    copy_out((l, "cq", m), qcT[:, m, :], lambda bk: bk[:, 0:T])
                for t in range(2):
                    for hp in range(2):
                        q = 2 * t + hp
                        bk = take(act, (l, "cS", t, hp))
                        cmax_ready.wait(act, l, q)
                        for j in range(2):
                            ins = S.activation(cP[:, t, 2 * hp + j, :], bk[:, 256 * j:256 * (j + 1)], ACT.Exp,
                                               bias=nb[:, 2 * q + j:2 * q + j + 1], scale=MD ** -0.5,
                                               accum_out=rs[:, 2 * q + j:2 * q + j + 1])
                            if j == 0:
                                step.inc(ins)
                        emptied_after((l, "cS", t, hp), ins)
                for t in range(2):
                    for kt in range(2):
                        copy_out((l, "cPT", t, kt), cPT[:, kt, :, t * P:(t + 1) * P],
                                 lambda bk: bk[:].rearrange("p (h n) -> p h n", h=MH))
                for i in range(4):
                    copy_out((l, "cO", i), oT[:, 2 * i:2 * i + 2, 0:NP_TOK],
                             lambda bk: bk[:].rearrange("p (j n) -> p j n", j=2))
                cs_rows.wait(act, l)
                S.activation(sP[0:32], sP[0:32], ACT.Exp, bias=nb1[0:32], scale=MD ** -0.5, accum_out=rs1[0:32]
                             ).then_inc(cs_exp.sem, 1)
                norm(l, 1)
                if l == 0:
                    xT_dve.wait(act, 0, 1)
                    act.wait_ge(x_high_ready, KT)
                    for q in range(NGU + NDN):
                        for j in range(2):
                            if q + j:
                                ffn_high_part(q, j)
                        if 1 <= q <= NGU:
                            for b in range(2):
                                if q > 1:
                                    act.wait_ge(h_low_ready, 2 * (q - 2) + b + 1)
                                copy_out((l, "g", q - 1, b), h_rows[b], lambda bk: bk[:, 0:T], ACT.Silu)
                            for b in range(2):
                                copied(act, (l, "u", q - 1, b))
                                S.activation(h_high[:, 2 * (q - 1) + b, :], h_rows[b], ACT.Copy
                                             ).then_inc(h_high_ready, 1)
                else:
                    for n in range(6):
                        rows = TILES[n // 2][1]
                        copy_out((l, "xtok", n), x_tok[0:rows, n // 2, 512 * (n % 2):512 * (n % 2 + 1)],
                                 lambda bk: bk[0:rows, :])
                    act.wait_ge(lsm_ready, 1)
                    S.activation(lsm[:], lsm[:], ACT.Exp).then_inc(lexp_ready, 1)
                    expert_activations(act)
                norm(l, 2)
            for n in range(6):
                rows = TILES[n // 2][1]
                copy_out(("out", n), y_tok[0:rows, n // 2, 512 * (n % 2):512 * (n % 2 + 1)], lambda bk: bk[0:rows, :])

        def route(l, dve, step):
            V = nc.vector

            def bc(ap, shape, axis):
                return ap.unsqueeze(axis).to_broadcast(shape)

            dve.wait_ge(buffers_set, 9)
            bk = take(dve, (l, "lg"))
            step.inc(V.tensor_copy(lgb[:, 0:2, :], bk[:, 0:16].rearrange("p (t e) -> p t e", t=2)))
            emptied_after((l, "lg"), V.tensor_copy(lgb[0:8, 2, :], bk[0:8, 16:24]))
            copied(dve, (l, "lg"))
            other, this = bc(lgb[:], [P, 3, 8, 8], 2), bc(lgb[:], [P, 3, 8, 8], 3)
            step.inc(V.tensor_tensor(cmp_gt, other, this, ALU.is_gt))
            step.inc(V.tensor_tensor(cmp_eq, other, this, ALU.is_equal))
            step.done(V.reduce_max(l3[:], lgb[:], AX.X))
            tri = const[:, C_TRI:C_TRI + 64].rearrange("p (e j) -> p e j", e=8)
            step.inc(V.tensor_tensor(cmp_eq, cmp_eq, bc(tri, [P, 3, 8, 8], 1), ALU.mult))
            V.tensor_tensor(lsm[:], lgb[:], bc(l3[:], [P, 3, 8], 2), ALU.subtract).then_inc(lsm_ready, 1)
            dve.wait_ge(dve_steps, step.n)
            step.done(V.tensor_tensor(cmp_gt, cmp_gt, cmp_eq, ALU.add))
            step.done(V.reduce_sum(sel[:], cmp_gt, AX.X))
            V.tensor_scalar(sel[:], sel[:], 1.5, None, ALU.is_lt).then_inc(sel_known, 1)
            dve.wait_ge(sel_known, 1)
            dve.wait_ge(lexp_ready, 1)
            step.done(V.tensor_tensor(lsm[:], lsm[:], sel[:], ALU.mult))
            step.done(V.reduce_sum(l3[:], lsm[:], AX.X))
            step.done(V.reciprocal(l3[:], l3[:]))
            step.inc(V.tensor_tensor(gates[:, :, 0:8], lsm[:], bc(l3[:], [P, 3, 8], 2), ALU.mult))
            bk = take(dve, (l, "pos"))
            step.inc(V.tensor_scalar(posp[:, 0:2, 0:8], bk[:, 0:16].rearrange("p (t e) -> p t e", t=2), 1.0, None,
                                     ALU.add))
            step.inc(V.tensor_scalar(posp[0:8, 2, 0:8], bk[0:8, 16:24], 1.0, None, ALU.add))
            emptied_after((l, "pos"), V.reduce_max(cnt[:], bk[0:1, 24:32], AX.X))
            copied(dve, (l, "pos"))
            V.tensor_copy(cnti[:], cnt[:]).then_inc(pos_known, 1)
            dve.wait_ge(dve_steps, step.n)
            step.done(V.tensor_tensor(posp[:, :, 0:8], posp[:, :, 0:8], sel[:], ALU.mult))
            step.done(V.tensor_scalar(posp[:, :, 0:8], posp[:, :, 0:8], -1.0, None, ALU.add))

        def expert_elementwise(dve):
            V = nc.vector

            def selection(col):
                for t, (_, rows) in enumerate(TILES):
                    where = posp[0:rows, t, col]
                    V.tensor_scalar(Sel[0:rows, t, 0:lots], iota[0:rows, 0:lots], where, None, ALU.is_equal)
                    ins = V.tensor_scalar(GSel[0:rows, t, 0:lots], iota[0:rows, 0:lots], where,
                                          gates[0:rows, t, col], ALU.is_equal, ALU.mult)
                ins.then_inc(sel_ready, 1)

            def low_of_gathered(counted, groups):
                for n in range(2):
                    dve.wait_ge(X_full, groups + (n + 1))
                    dve.wait_ge(xg_taken, counted + (n + 1))
                    V.tensor_tensor(xg_low[:, 4 * n:4 * n + 4, 0:lots],
                                    X_BANKS[n][:, 0:4 * lots].rearrange("p (k n) -> p k n", k=4),
                                    xg_high[:, 4 * n:4 * n + 4, 0:lots], ALU.subtract).then_inc(xg_low_ready, 1)

            def low_part(e, c, p):
                for j, h in halves_of(p):
                    dve.wait_ge(split_high, expert_no(e, c) * HALVES + (h + 1))
                    s, part = epos[p][2], slice(j * HALF, (j + 1) * HALF)
                    V.tensor_tensor(ring_low[:, s, part], ring[:, s, part], high_bufs[h % HIGH_BUFS][:],
                                    ALU.subtract).then_inc(split_low, 1)

            def expert(e, c):
                i = expert_no(e, c)
                tb = transposes_before(e, c)

                def multiply(f):
                    dve.wait_ge(sg_ready, i * NGU + (f + 1))
                    if f >= 2:
                        dve.wait_ge(T_full, tb + f)
                    V.tensor_tensor(hh[0:lots, f % 2, :], sg[0:lots, f % 2, :], GU_BANKS[f % 2][0:lots, GU:2 * GU],
                                    ALU.mult).then_inc(h_ready, 1)

                def low_of_h(f):
                    dve.wait_ge(T_done, tb + (f + 2))
                    V.tensor_tensor(he_low[:, 2 * f:2 * f + 2, 0:lots],
                                    T_BANKS[f % 2][:, 0:2 * lots].rearrange("p (s n) -> p s n", s=2),
                                    he_high[:, 2 * f:2 * f + 2, 0:lots], ALU.subtract).then_inc(T_low, 1)

                for p in range(1, NGU + NDN):
                    low_part(e, c, p)
                    if 1 <= p <= NGU:
                        multiply(p - 1)
                    if p == 1:
                        dve.wait_ge(T_full, tb + 1)
                        selection(bass.ds(e + 1, 1))
                    if 2 <= p <= NGU + 1:
                        low_of_h(p - 2)
                dve.wait_ge(dn_done, i * NDN + NDN)
                V.tensor_copy(ye[0:lots, 512:1024], Y_BANKS[1][0:lots, :]).then_inc(y_by_dve, 1)
                with dve.If(e < EXPERTS - 1):
                    low_part(e + 1, c, 0)
                low_of_gathered(i * 2 + 2 * (c + 1), x_groups_before(e, c))
                dve.wait_ge(part_added, parts_added(e, c))
                for k in range(KT):
                    dve.wait_ge(X_full, x_groups_before(e, c) + (2 + k + 1))
                    V.tensor_tensor(acc[:, k, :], acc[:, k, :], SUM_BANKS[k % 4][:, 0:T], ALU.add
                                    ).then_inc(part_added, 1)

            def one_pass(c):
                if c:
                    V.tensor_scalar(posp[:], posp[:], -float(lots), None, ALU.add).then_inc(pass_shift, 1)
                    dve.wait_ge(pass_shift, c)
                selection(slice(0, 1))
                low_part(0, c, 0)
                low_of_gathered(EXPERTS * 2 * c + 2 * c, x_groups_before(0, c) - 2)
                with dve.Fori(0, EXPERTS) as e:
                    expert(e, c)

            one_pass(0)
            dve.wait_ge(pos_known, 1)
            most = dve.value_load(cnti[0:1, 0:1], min_val=0, max_val=T)
            for c in range(1, passes):
                with dve.If(most > (0 if always else lots * c)):
                    one_pass(c)
                    dve.wait_ge(part_added, parts_added(EXPERTS, c))

        @block.vector
        def _(dve):
            V = nc.vector
            step = Steps(dve, dve_steps)

            def bc(ap, shape, axis):
                return ap.unsqueeze(axis).to_broadcast(shape)

            def residual(l, name, m):
                bk = take(dve, (l, name, m))
                emptied_after((l, name, m), V.scalar_tensor_tensor(
                    R[:, m, :], xT[:, m, :], ALPHA, bk[:, 0:T], ALU.mult, ALU.add))

            def residuals(l, name, i):
                for m in range(8):
                    residual(l, name, m)
                    copied(dve, (l, name, m))
                    if m:
                        ins = V.tensor_tensor(stat[:], R[:, 0, :] if m == 1 else stat[:], R[:, m, :], ALU.add)
                        if m < 7:
                            step.done(ins)
                ins.then_inc(sum_ready.sem, 1)

            def norm(l, i, part):
                bk = take(dve, (l, "mu", i))
                if part:
                    copied(dve, (l, part, 7))
                for h in range(4):
                    ins = V.tensor_tensor(R[:, 2 * h:2 * h + 2, :], R[:, 2 * h:2 * h + 2, :],
                                          bc(bk[:, 0:T], [P, 2, T], 1), ALU.subtract)
                    if h < 3:
                        ins.then_inc(centred.sem, 1)
                emptied_after((l, "mu", i), ins)
                ln_rstd.wait(dve, l, i)
                copied(dve, (l, "mu", i))
                for k in range(KT):
                    V.scalar_tensor_tensor(R[:, k, :], R[:, k, :], col_g(l, i, k), stat[:], ALU.mult, ALU.mult
                                           ).then_inc(scaled.sem, 1)
                scaled.wait(dve, l, 8 * i + 7)
                V.tensor_scalar(xT[:, 7, :], R[:, 7, :], col_b(l, i, 7), None, ALU.add).then_inc(xT_dve.sem, 1)
                if (l, i) != (0, 1):
                    xT_act.wait(dve, l, 7 * i + 6)
                xT_dve.wait(dve, l, i)

            bk = take(dve, ("vec",))
            step.inc(V.tensor_copy(vecT[:, 0, 0:122], bk[:, 0:122]))
            emptied_after(("vec",), V.tensor_copy(vecT[:, 1, 0:64], bk[:, 128:192]))
            for n in range(5):
                t, bk = n // 2, take(dve, ("xin", n))
                t0, rows = TILES[t]
                nk = 8 if t == 2 else 4
                k0 = 0 if t == 2 else 4 * (n % 2)
                emptied_after(("xin", n), V.tensor_copy(
                    xT[:, k0:k0 + nk, t0:t0 + rows], bk[:, 0:nk * rows].rearrange("p (k n) -> p k n", k=nk)))
            dve.wait_ge(small_landed, 16 * 9)
            step.inc(V.tensor_tensor(lprod[:, :, 0, :], lraw[:, :, 0, :], lraw[:, :, 1, :], ALU.mult))
            step.done(V.tensor_tensor(lprod[:, :, 1, :], lraw[:, :, 2, :], lraw[:, :, 3, :], ALU.mult))
            V.reduce_sum(lamt[:], lprod, AX.X).then_inc(lam_dots, 1)
            step.inc(V.memset(dtb[:], 0.0))
            step.done(V.memset(An[:], 0.0))
            dve.wait_ge(setup_exps, 2)
            for l in range(L):
                for q in range(3):
                    step.inc(V.tensor_copy(dtb[:, l, 8 * q:8 * q + 8], raw8[:, 0, l, :]))
                    step.inc(V.tensor_scalar(An[:, l, 8 * q:8 * q + 8], raw8[:, 1, l, :], -1.0, None, ALU.mult))
                step.inc(V.tensor_copy(dtb[0:8, l, 24:32], col8[:, 0, l:l + 1].to_broadcast([8, 8])))
                step.inc(V.tensor_scalar(An[0:8, l, 24:32], col8[:, 1, l:l + 1].to_broadcast([8, 8]), -1.0, None,
                                         ALU.mult))
                step.done(V.tensor_tensor(nlam[:, l:l + 1], lamt[:, l, 1:2], lamt[:, l, 0:1], ALU.subtract))
                step.inc(V.tensor_scalar(nlam[:, l:l + 1], nlam[:, l:l + 1], -LAM_INIT[l], None, ALU.add))
                ins = V.tensor_scalar(col_attn(l), col_attn(l), 1.0 - LAM_INIT[l], None, ALU.mult)
                if l == 0:
                    step.inc(ins)
            ins.then_inc(vectors_ready, 1)
            dve.wait_ge(vectors_ready, 1)
            dve.wait_ge(buffers_set, 6)

            for l in range(L):
                bk = take(dve, (l, "dt"))
                step.inc(V.tensor_tensor(dtr[:, 0:16], bk[:, 0:16], dtb[:, l, 0:16], ALU.add))
                emptied_after((l, "dt"), V.tensor_tensor(dtr[0:8, 16:32], bk[0:8, 16:32], dtb[0:8, l, 16:32],
                                                         ALU.add))
                copied(dve, (l, "dt"))
                V.scalar_tensor_tensor(dte, dtr, -1.0, dtr, ALU.mult, ALU.max).then_inc(dt_abs.sem, 1)

                dt_exp.wait(dve, l)
                V.tensor_scalar(dte, dte, 1.0, None, ALU.add).then_inc(dt_exp1.sem, 1)
                dt_ln.wait(dve, l)
                step.done(V.scalar_tensor_tensor(dtv, dtr, 0.0, dte, ALU.max, ALU.add))
                V.tensor_tensor(da, dtv, An[:, l, :], ALU.mult).then_inc(da_ready.sem, 1)
                bk = take(dve, (l, "acs"))
                step.inc(V.tensor_copy(sc[:, 0:16], bk[:, 0:16]))
                step.done(V.tensor_copy(sc[:, 32:48], bk[:, 16:32]))
                emptied_after((l, "acs"), V.tensor_tensor(sc[:, 16:32], bk[:, 16:32], sc[:, 0:16], ALU.subtract))
                da_ready.wait(dve, l)
                V.tensor_copy(sc[0:8, 48:56], da[0:8, 24:32]).then_inc(decays_in.sem, 1)
                bk = take(dve, (l, "scT"))
                emptied_after((l, "scT"), V.tensor_copy(
                    win[:, :, 0:3, :], bk[:, 0:192].rearrange("p (m b i) -> p m i b", m=8, b=8)))
                decays_out.wait(dve, l)
                V.tensor_tensor(xwsc, dtv[:, 0:16], ex[:, 16:32], ALU.mult).then_inc(xwsc_ready.sem, 1)

                def conv_input(m):
                    bk = take(dve, (l, "xbc", m))
                    step.inc(V.tensor_copy(xpad[:, m, 3:259], bk[:, 0:NP_TOK]))
                    step.inc(V.tensor_copy(win[:, m, 3, :], bk[:, NP_TOK:T]))
                    emptied_after((l, "xbc", m), V.tensor_copy(ct11[:, m, :], bk[:, NP_TOK - 3:T]))

                def later_taps(m):
                    tap0_done.wait(dve, l, m)
                    for i in range(1, CW):
                        ins = V.scalar_tensor_tensor(convT[:, m, 0:NP_TOK], xpad[:, m, i:i + NP_TOK],
                                                     col_cw(l, i, m), convT[:, m, 0:NP_TOK], ALU.mult, ALU.add)
                        if i < CW - 1:
                            step.done(ins)
                    ins.then_inc(taps_done.sem, 1)

                def cached_scores(b):
                    bk = take(dve, (l, "qb", b))
                    s = rg.arrived(dve, (l, "K", b // 4))
                    Kb = ring[:, s, :].rearrange("p (b g n) -> p b g n", b=4, g=2)[:, b % 4]
                    tb = tmp.rearrange("p (g n) -> p g n", g=2)
                    emptied_after((l, "qb", b), V.tensor_tensor(tb, Kb, bc(bk[:], [P, 2, 512], 1), ALU.mult))
                    copied(dve, (l, "qb", b))
                    step.inc(V.reduce_sum(sS[:, :, b, :], tmp.rearrange("p (g h d) -> p g h d", g=2, h=8), AX.X))

                for m in range(8):
                    conv_input(m)
                    dve.wait_ge(dve_steps, step.n)
                    cached_scores(m)
                    if m == 0:
                        bk = take(dve, (l, "dtb"))
                        emptied_after((l, "dtb"), V.tensor_copy(dcol.rearrange("p j c -> p (j c)"), bk[:, 0:64]))
                    else:
                        later_taps(m - 1)
                later_taps(7)
                dve.wait_ge(dve_steps, step.n)
                taps = vecT[:, 1, 32 * l:32 * l + 32].rearrange("p (i m) -> p m i", i=CW)
                w4 = wtmp.rearrange("p (m i b) -> p m i b", m=8, i=CW)
                copied(dve, (l, "scT"))
                step.done(V.tensor_tensor(w4, win, bc(taps, [P, 8, CW, 8], 3), ALU.mult))
                step.done(V.reduce_sum(convT[:, :, NP_TOK:T], w4.rearrange("p m i b -> p m b i"), AX.X))
                V.tensor_tensor(convT[:, :, NP_TOK:T], convT[:, :, NP_TOK:T],
                                bc(cols_cb(l, 0, 8), [P, 8, 8], 2), ALU.add).then_inc(taps_done.sem, 1)
                step.done(V.tensor_tensor(tmp[0:8, 0:512], qkr[0:8, 2, 0:512], qkr[0:8, 2, 512:1024], ALU.mult))
                step.done(V.reduce_sum(ss[0:8], tmp[0:8, 0:512].rearrange("p (h d) -> p h d", h=8), AX.X))
                V.tensor_tensor(sbt[0:8, :].rearrange("p (b h) -> p b h", b=8),
                                const[0:8, C_REQT:C_REQT + 64].rearrange("p (b h) -> p b h", b=8),
                                bc(ss[0:8], [8, 8, 8], 1), ALU.mult).then_inc(dec_scores.sem, 1)
                bk = take(dve, (l, "sST"))
                emptied_after((l, "sST"), V.tensor_copy(pSx, bk[0:64, 0:257]))
                copied(dve, (l, "sST"))
                step.done(V.reduce_max(mx1[0:64], pSx, AX.X))
                V.tensor_scalar(nb1[0:64], mx1[0:64], -DQ ** -0.5, None, ALU.mult).then_inc(dec_rows.sem, 1)

                def decode_probabilities():
                    dec_exp.wait(dve, l)
                    step.done(V.reciprocal(rr1[0:64], rs1[0:64]))
                    step.done(V.tensor_scalar(pSx, pSx, rr1[0:64], None, ALU.mult))
                    V.tensor_scalar(pself_r[:], const[0:64, C_HEAD:C_HEAD + 8], pSx[:, 256:257], None, ALU.mult
                                    ).then_inc(dec_probs.sem, 1)
                    bk = take(dve, (l, "pT"))
                    pv = bk[:, 0:128].rearrange("p (g b h m) -> p g b h m", g=2, b=8, h=AH)
                    step.done(V.tensor_scalar(own_heads, pv[:, :, :, :, 1], nlam[:, l:l + 1], None, ALU.mult))
                    emptied_after((l, "pT"), V.tensor_tensor(own_heads, own_heads, pv[:, :, :, :, 0], ALU.add))
                    bk = take(dve, (l, "pself"))
                    pf = bk[0:8, 0:8].rearrange("p (c m) -> p c m", m=2)
                    step.done(V.tensor_scalar(as4[0:8], pf[:, :, 1], nlam[0:8, l:l + 1], None, ALU.mult))
                    emptied_after((l, "pself"), V.tensor_tensor(as4[0:8], as4[0:8], pf[:, :, 0], ALU.add))

                conv_ready.wait(dve, l, 8)
                step.done(V.tensor_tensor(dtx, dcol[:, :, 0:8], convT[:, 0:4, NP_TOK:T], ALU.mult))
                s = rg.arrived(dve, (l, "state"))
                for b in range(8):
                    if b == 2:
                        decode_probabilities()
                    state_decayed.wait(dve, l, b)
                    bk = take(dve, (l, "BC", b))
                    Sb = ring[:, s, 512 * b:512 * (b + 1)].rearrange("p (g r n) -> p g r n", g=2, r=2)
                    tb = tmp[:, 0:512].rearrange("p (g r n) -> p g r n", g=2, r=2)

                    def on_heads(q):
                        return bc(bk[:, 256 * q:256 * (q + 1)].rearrange("p (g n) -> p g n", g=2), [P, 2, 2, SN], 2)

                    xb = bc(dtx[:, :, b].rearrange("p (g r) -> p g r", g=2), [P, 2, 2, SN], 3)
                    step.done(V.tensor_tensor(tb, on_heads(0), xb, ALU.mult))
                    step.done(V.tensor_tensor(Sb, Sb, tb, ALU.add))
                    emptied_after((l, "BC", b), V.tensor_tensor(tb, Sb, on_heads(1), ALU.mult))
                    copied(dve, (l, "BC", b))
                    ins = V.reduce_sum(ysT[:, :, b], tmp[:, 0:512].rearrange("p (j n) -> p j n", j=4), AX.X)
                    if b < 7:
                        step.done(ins)
                ins.then_inc(ysT_ready.sem, 1)
                bk = take(dve, (l, "st", 0))
                emptied_after((l, "st", 0), V.tensor_copy(ST0, bk[:]))
                bk = take(dve, (l, "st", 1))
                copied(dve, (l, "st", 0))
                step.done(V.tensor_tensor(STf.rearrange("p (h d) -> p h d", h=SH),
                                          ST0.rearrange("p (h d) -> p h d", h=SH),
                                          bc(ex[:, 40:48], [P, SH, SP_], 2), ALU.mult))
                emptied_after((l, "st", 1), V.tensor_tensor(STf, STf, bk[:], ALU.add))
                for c in range(2):
                    for g in range(SG):
                        bk = take(dve, (l, "ab", c, g))
                        emptied_after((l, "ab", c, g), V.tensor_tensor(
                            Mdec[:, g], bk[:].rearrange("p (r n) -> p r n", r=4),
                            bc(sc[:, 8 * c + 4 * g:8 * c + 4 * g + 4], [P, 4, P], 2), ALU.subtract))
                        copied(dve, (l, "ab", c, g))
                        V.tensor_tensor(Mdec[:, g], Mdec[:, g], bc(negm, [P, 4, P], 1), ALU.add
                                        ).then_inc(seg_ready.sem, 1)
                    bk = take(dve, (l, "cb", c))
                    for g in range(SG):
                        decay_ready.wait(dve, l, 2 * c + g)
                        ins = V.tensor_tensor(Mdec[:, g], Mdec[:, g], bc(bk[:, g * P:(g + 1) * P], [P, 4, P], 1),
                                              ALU.mult)
                        if g == 0:
                            step.inc(ins)
                    emptied_after((l, "cb", c), ins)
                    bk = take(dve, (l, "y", c))
                    xskip_ready.wait(dve, l, c)
                    emptied_after((l, "y", c), V.tensor_tensor(mix[:, c, 512:1024], mix[:, c, 512:1024], bk[:],
                                                               ALU.add))
                bk = take(dve, (l, "yo"))
                emptied_after((l, "yo"), V.tensor_tensor(
                    tmp[:, 0:512].rearrange("p (h d) -> p h d", h=SH), bk[:].rearrange("p (h d) -> p h d", h=SH),
                    bc(ex[:, 8:16], [P, SH, SP_], 2), ALU.mult))
                copied(dve, (l, "yo"))
                step.done(V.tensor_tensor(mix[:, 1, 512:1024], mix[:, 1, 512:1024], tmp[:, 0:512], ALU.add))
                copied(dve, (l, "tok", "z", 2))
                for c in range(2):
                    step.inc(V.tensor_tensor(mix[:, c, 512:1024], mix[:, c, 512:1024], vz[:, c, 512:1024],
                                             ALU.mult))
                bk = take(dve, (l, "ysT"))
                xskip_ready.wait(dve, l, 2)
                emptied_after((l, "ysT"), V.tensor_tensor(mix[0:8, 2, 512:1024], mix[0:8, 2, 512:1024],
                                                          bk[0:8, :], ALU.add))
                copied(dve, (l, "ysT"))
                step.inc(V.tensor_tensor(mix[0:8, 2, 512:1024], mix[0:8, 2, 512:1024], vz[0:8, 2, 512:1024],
                                         ALU.mult))
                for qt in range(2):
                    nk = (qt + 1) * P
                    if qt:
                        passed(dve, (l, "aT", 0, 0))
                    for n in range(4):
                        hp, m = n // 2, n % 2
                        bk = take(dve, (l, "S", qt, hp, m))
                        sv = bk[:, 0:2 * nk].rearrange("p (j k) -> p j k", j=2)
                        pv = probs[:, 2 * hp:2 * hp + 2, m, :]
                        if qt:
                            step.inc(V.tensor_copy(pv[:, :, 0:P], sv[:, :, 0:P]))
                        emptied_after((l, "S", qt, hp, m), V.tensor_tensor(
                            pv[:, :, nk - P:nk], sv[:, :, nk - P:nk], bc(cmask, [P, 2, P], 1), ALU.add))
                        copied(dve, (l, "S", qt, hp, m))
                        mv_ = mx.rearrange("p (h m) -> p h m", m=2)[:, 2 * hp:2 * hp + 2, m]
                        nv = nb.rearrange("p (h m) -> p h m", m=2)[:, 2 * hp:2 * hp + 2, m]
                        step.done(V.reduce_max(mv_, pv[:, :, 0:nk], AX.X))
                        V.tensor_scalar(nv, mv_, -DQ ** -0.5, None, ALU.mult).then_inc(max_ready.sem, 1)
                    probs_ready.wait(dve, l, 4 * qt + 3)
                    step.done(V.reciprocal(rr, rs))
                    r2 = rr.rearrange("p (h m) -> p h m", m=2)[:, :, 1]
                    step.done(V.tensor_scalar(r2, r2, nlam[:, l:l + 1], None, ALU.mult))
                    for h in range(AH):
                        step.inc(V.tensor_scalar(probs[:, h, 0, 0:nk], probs[:, h, 0, 0:nk],
                                                 rr[:, 2 * h:2 * h + 1], None, ALU.mult))
                    first = step.n - AH
                    for h in range(AH):
                        dve.wait_ge(dve_steps, first + h + 1)
                        ins = V.scalar_tensor_tensor(probs[:, h, 0, 0:nk], probs[:, h, 1, 0:nk],
                                                     rr[:, 2 * h + 1:2 * h + 2], probs[:, h, 0, 0:nk],
                                                     ALU.mult, ALU.add)
                        if h < AH - 1:
                            step.inc(ins)
                    ins.then_inc(a_ready.sem, 1)
                def rms(t):
                    n = TILES[t][1]
                    step.done(V.tensor_tensor(tmp[0:n], mix[0:n, t, :], mix[0:n, t, :], ALU.mult))
                    step.inc(V.reduce_sum(ms[0:n, 0:4], tmp[0:n, 0:512].rearrange("p (h d) -> p h d", h=4), AX.X))
                    step.done(V.reduce_sum(ms[0:n, 4:6], tmp[0:n, 512:1024].rearrange("p (h d) -> p h d", h=2),
                                           AX.X))
                    step.inc(V.tensor_scalar(ms[0:n, 0:4], ms[0:n, 0:4], 1.0 / DV, EPS, ALU.mult, ALU.add))
                    V.tensor_scalar(ms[0:n, 4:6], ms[0:n, 4:6], 1.0 / 256, EPS, ALU.mult, ALU.add
                                    ).then_inc(ms_ready.sem, 1)
                    rstd_ready.wait(dve, l, NORM_ORDER.index(t))
                    for o, h in ((0, 4), (512, 2)):
                        v = mix[0:n, t, o:o + 512].rearrange("p (h d) -> p h d", h=h)
                        ins = V.tensor_tensor(v, v, bc(rstd6[0:n, (0 if h == 4 else 4):(4 if h == 4 else 6)],
                                                       [n, h, 512 // h], 2), ALU.mult)
                        if h == 4:
                            step.inc(ins)
                    ins.then_inc(mix_ready.sem, 1)

                bk = take(dve, (l, "O", 0))
                emptied_after((l, "O", 0), V.tensor_copy(mix[:, 0, 0:512], bk[:]))
                copied(dve, (l, "O", 0))
                rms(0)
                bk = take(dve, (l, "oS"))
                emptied_after((l, "oS"), V.tensor_tensor(
                    tmp[0:32, 0:512].rearrange("p (h d) -> p h d", h=AH),
                    bk[0:32, :].rearrange("p (h d) -> p h d", h=AH),
                    bc(const[0:32, C_H32:C_H32 + AH], [32, AH, DV], 2), ALU.mult))
                own = mix[0:8, 2, 0:512]
                copied(dve, (l, "pself"))
                step.done(V.tensor_tensor(own.rearrange("p (h d) -> p h d", h=AH),
                                          vz[0:8, 2, 0:512].rearrange("p (h d) -> p h d", h=AH),
                                          bc(as4[0:8], [8, AH, DV], 2), ALU.mult))
                bk = take(dve, (l, "oSt"))
                emptied_after((l, "oSt"), V.tensor_tensor(own, own, bk[0:8, :], ALU.add))
                copied(dve, (l, "oSt"))
                rms(2)
                bk = take(dve, (l, "O", 1))
                emptied_after((l, "O", 1), V.tensor_copy(mix[:, 1, 0:512], bk[:]))
                copied(dve, (l, "O", 1))
                rms(1)
                dve.wait_ge(stored, 16 * STORES_LAYER * (l + 1))
                for n in range(5):
                    t, bk = n // 2, take(dve, (l, "mixT", n))
                    t0, rows = TILES[t]
                    for half in ((0, 1) if t == 2 else (n % 2,)):
                        src = bk[:, (4 * rows * half if t == 2 else 0):][:, 0:4 * rows]
                        src = src.rearrange("p (k n) -> p k n", k=4)
                        dst = mixT[:, 4 * half:4 * half + 4, t0:t0 + rows]
                        if half:
                            ins = V.tensor_tensor(dst, src, bc(cols_ssm(l), [P, 4, rows], 2), ALU.mult)
                        else:
                            ins = V.tensor_scalar(dst, src, col_attn(l), None, ALU.mult)
                        if t == 2 and half == 0:
                            step.inc(ins)
                    emptied_after((l, "mixT", n), ins)
                residuals(l, "m", 0)
                norm(l, 0, "m")
                def row_maxima(q):
                    bk = take(dve, (l, "cS", q // 2, q % 2))
                    step.done(V.reduce_max(mx[:, 2 * q:2 * q + 2], bk[:].rearrange("p (j k) -> p j k", j=2), AX.X))
                    V.tensor_scalar(nb[:, 2 * q:2 * q + 2], mx[:, 2 * q:2 * q + 2], -MD ** -0.5, None, ALU.mult
                                    ).then_inc(cmax_ready.sem, 1)

                def normalize(t):
                    copied(dve, (l, "cS", t, 1))
                    step.done(V.reciprocal(rr[:, 4 * t:4 * t + 4], rs[:, 4 * t:4 * t + 4]))
                    for h in range(MH):
                        ins = V.tensor_scalar(cP[:, t, h, :], cP[:, t, h, :], rr[:, 4 * t + h:4 * t + h + 1], None,
                                              ALU.mult)
                        if h < MH - 1:
                            step.inc(ins)
                    ins.then_inc(cP_ready.sem, 1)

                def take_q_rows(i):
                    bk = take(dve, (l, "qsT", i))
                    emptied_after((l, "qsT", i), V.tensor_copy(qs[0:8, 512 * i:512 * (i + 1)], bk[0:8, :]))

                def memory_scores(b, i):
                    s = rg.arrived(dve, (l, "mK", b // 2))
                    Kb = ring[:, s, :].rearrange("p (b t n) -> p b t n", b=2, t=2)[:, b % 2]
                    bk = take(dve, (l, "qsb", b, i))
                    dve.wait_ge(dve_steps, step.n)
                    for t in range(2):
                        for j in range(2):
                            h = 2 * i + j
                            ins = V.scalar_tensor_tensor(
                                ctmp[:, (2 * t + j) * MD:(2 * t + j + 1) * MD], Kb[:, t, h * MD:(h + 1) * MD], 1.0,
                                bk[:, j * MD:(j + 1) * MD], ALU.mult, ALU.mult, accum_out=sC[:, t, b, h:h + 1])
                            if t + j < 2:
                                step.inc(ins)
                    emptied_after((l, "qsb", b, i), ins)
                    copied(dve, (l, "qsb", b, i))

                take_q_rows(0)
                for b in range(8):
                    memory_scores(b, 0)
                for n in range(4):
                    row_maxima(n)
                    if n == 0:
                        take_q_rows(1)
                    if n == 2:
                        normalize(0)
                    for b in (2 * n, 2 * n + 1):
                        memory_scores(b, 1)
                dve.wait_ge(dve_steps, step.n)
                normalize(1)
                bk = take(dve, (l, "sCT"))
                emptied_after((l, "sCT"), V.tensor_copy(sP[0:32], bk[0:32, 0:256]))
                copied(dve, (l, "sCT"))
                step.done(V.reduce_max(mx1[0:32], sP[0:32], AX.X))
                V.tensor_scalar(nb1[0:32], mx1[0:32], -MD ** -0.5, None, ALU.mult).then_inc(cs_rows.sem, 1)
                cs_exp.wait(dve, l)
                step.done(V.reciprocal(rr1[0:32], rs1[0:32]))
                V.tensor_scalar(sP[0:32], sP[0:32], rr1[0:32], None, ALU.mult).then_inc(cs_probs.sem, 1)
                bk = take(dve, (l, "sPT"))
                emptied_after((l, "sPT"), V.tensor_copy(own_heads, bk[:, 0:64].rearrange("p (t b h) -> p t b h", t=2,
                                                                                        b=8)))
                for i in range(2):
                    bk = take(dve, (l, "oV", i))
                    emptied_after((l, "oV", i), V.tensor_tensor(
                        ctmp[0:32, 512 * i:512 * (i + 1)].rearrange("p (h d) -> p h d", h=2),
                        bk[0:32, :].rearrange("p (h d) -> p h d", h=2),
                        bc(const[0:32, C_H32 + 2 * i:C_H32 + 2 * i + 2], [32, 2, MD], 2), ALU.mult))
                bk = take(dve, (l, "soT"))
                emptied_after((l, "soT"), V.tensor_copy(oT[:, :, NP_TOK:T],
                                                        bk[:, 0:64].rearrange("p (m b) -> p m b", m=8)))
                residuals(l, "co", 1)
                norm(l, 1, "co")
                if l == 0:
                    def ffn_low_part(q, j):
                        high, s, part = ffn_half(q, j)
                        dve.wait_ge(ffn_high, 2 * q + j + 1)
                        V.tensor_tensor(ring_low[:, s, part], ring[:, s, part], high, ALU.subtract
                                        ).then_inc(ffn_low, 1)

                    ffn_low_part(0, 0)
                    for k in range(KT):
                        dve.wait_ge(x_high_ready, k + 1)
                        V.tensor_tensor(x_low[:, k, :], xT[:, k, :], x_high[:, k, :], ALU.subtract
                                        ).then_inc(x_low_ready, 1)
                    for q in range(NGU + NDN):
                        for j in range(2):
                            if q + j:
                                ffn_low_part(q, j)
                        if 1 <= q <= NGU:
                            for b in range(2):
                                bk = take(dve, (l, "u", q - 1, b))
                                copied(dve, (l, "g", q - 1, b))
                                emptied_after((l, "u", q - 1, b), V.tensor_tensor(h_rows[b], h_rows[b], bk[:, 0:T],
                                                                                  ALU.mult))
                            for b in range(2):
                                f = 2 * (q - 1) + b
                                dve.wait_ge(h_high_ready, f + 1)
                                copied(dve, (l, "u", q - 1, b))
                                V.tensor_tensor(h_low[:, f, :], h_rows[b], h_high[:, f, :], ALU.subtract
                                                ).then_inc(h_low_ready, 1)
                    for m in range(8):
                        if m == 1024 // T:
                            passed(dve, (l, "d", 7))
                        residual(l, "d", m)
                    norm(l, 2, "d")
                else:
                    route(l, dve, step)
                    expert_elementwise(dve)
                    dve.wait_ge(part_added, parts_added(EXPERTS, 0))
                    V.scalar_tensor_tensor(R[:], xT[:], ALPHA, acc, ALU.mult, ALU.add).then_inc(moe_done, 1)
                    dve.wait_ge(moe_done, 1)
                    norm(l, 2, None)



_INS = ['x_prompt', 'x_sample', 'cache_attn_k', 'cache_attn_v', 'cache_mem_k', 'cache_mem_v', 'state_conv',
        'state_ssm', 'page_table', 'mem_prompt', 'ln_g', 'ln_b', 'w_in', 'conv_w', 'conv_b', 'dt_bias', 'a_log',
        'd_skip', 'ssm_norm_w', 'lambda_params', 'attn_norm_w', 'w_out', 'w_cq', 'w_ckv', 'w_co', 'w_ffn_gu',
        'w_ffn_down', 'w_router', 'w_exp_gu', 'w_exp_down']
_OUTS = [(1, 256, 1024), (8, 1, 1024), (2, 1, 256, 8, 64), (2, 1, 256, 4, 128), (2, 1, 256, 4, 256),
         (2, 1, 256, 4, 256), (2, 1, 3, 1024), (2, 1, 8, 64, 128), (2, 8, 1, 8, 64), (2, 8, 1, 4, 128),
         (2, 8, 3, 1024), (2, 8, 8, 64, 128)]


def kernel(**inputs):
    import concourse.bacc as _bacc
    from concourse.bass_utils import run_bass_kernel_spmd as _run

    nc = _bacc.Bacc("TRN2", target_bir_lowering=False, num_devices=1)
    arrays, args = {}, {}
    for name in _INS + ["consts"]:
        x = constants() if name == "consts" else np.ascontiguousarray(inputs[name])
        arrays[f"in_{name}"] = x
        args[name] = nc.dram_tensor(f"in_{name}", x.shape, mybir.dt.from_np(x.dtype), kind="ExternalInput").ap()
    outs = [nc.dram_tensor(f"out_{i}", shape, F32, kind="ExternalOutput").ap() for i, shape in enumerate(_OUTS)]
    build(nc, args, outs)
    r = _run(nc, [arrays], core_ids=[0])
    return tuple(r.results[0][f"out_{i}"] for i in range(len(_OUTS)))
```
